# Optimizing a Trainium2 kernel written in Bass

```python
import jax, jax.numpy as jnp
from jax import lax
import numpy as np

D_MODEL = 1024
BATCH = 1
SEQ = 512
DEPTH = 2
DEC_BATCH = 8
DEC_SEQ = 16
PAST_LEN = 256

CHUNK = 64
CONV_W = 4
EPS = 1e-6
SSD_HEADS = 16
SSD_HEAD_DIM = 64
SSD_INNER = SSD_HEADS * SSD_HEAD_DIM
SSD_GROUPS = 2
SSD_STATE = 64
SSD_CONV_DIM = SSD_INNER + 2 * SSD_GROUPS * SSD_STATE
LRU_WIDTH = 1024
LRU_BLOCKS = 16
LRU_BLOCK_DIM = LRU_WIDTH // LRU_BLOCKS
LRU_C = 8.0
PEER_HEADS = 8
PEER_KEYS = 128
PEER_EXPERTS = PEER_KEYS * PEER_KEYS
PEER_KEY_DIM = 256
PEER_TOPK = 16
PEER_BLOCK = 128
Z_END = SSD_INNER
XBC_END = Z_END + SSD_CONV_DIM
DT_END = XBC_END + SSD_HEADS
LX_END = DT_END + LRU_WIDTH
LY_END = LX_END + LRU_WIDTH
GS_END = LY_END + D_MODEL
IN_COLS = GS_END + D_MODEL

kernel_name = 'hybrid_ssd_rglru_peer_stream_step'

def rmsnorm(x, w):
    xf = x.astype(jnp.float32)
    y = xf * lax.rsqrt(jnp.mean(xf * xf, axis=-1, keepdims=True) + EPS)
    return (y * w.astype(jnp.float32)).astype(x.dtype)

def causal_conv(x, buf, w, b):
    L = x.shape[1]
    xp = jnp.concatenate([buf.astype(x.dtype), x], axis=1)
    y = b + w[0] * xp[:, 0:L]
    for k in range(1, CONV_W):
        y = y + w[k] * xp[:, k:k + L]
    return y, xp[:, -(CONV_W - 1):]

def ssd_scan(x, dt, a, bm, cm, h0):
    f32 = jnp.float32
    bsz, L = x.shape[0], x.shape[1]
    nc = -(-L // CHUNK)
    pad = nc * CHUNK - L
    hg = SSD_HEADS // SSD_GROUPS
    def padl(t):
        return jnp.pad(t.astype(f32), [(0, 0), (0, pad)] + [(0, 0)] * (t.ndim - 2))
    xc = padl(x).reshape(bsz, nc, CHUNK, SSD_GROUPS, hg, SSD_HEAD_DIM)
    dtc = padl(dt).reshape(bsz, nc, CHUNK, SSD_GROUPS, hg)
    bc = padl(bm).reshape(bsz, nc, CHUNK, SSD_GROUPS, SSD_STATE)
    cc = padl(cm).reshape(bsz, nc, CHUNK, SSD_GROUPS, SSD_STATE)
    acum = jnp.cumsum(dtc * a.astype(f32).reshape(SSD_GROUPS, hg), axis=2)
    causal = jnp.tril(jnp.ones((CHUNK, CHUNK), dtype=bool))[None, None, :, :, None, None]
    seg = acum[:, :, :, None] - acum[:, :, None, :]
    decay = jnp.exp(jnp.where(causal, seg, -jnp.inf))
    cb = jnp.einsum('bcqgn,bcsgn->bcqsg', cc, bc)
    wts = cb[..., None] * decay * dtc[:, :, None]
    y_diag = jnp.einsum('bcqsgh,bcsghp->bcqghp', wts, xc)
    decay_end = jnp.exp(acum[:, :, -1:] - acum)
    chunk_states = jnp.einsum('bcsgn,bcsghp->bcghpn', bc, (decay_end * dtc)[..., None] * xc)
    chunk_decay = jnp.exp(acum[:, :, -1])
    h0g = h0.astype(f32).reshape(bsz, SSD_GROUPS, hg, SSD_HEAD_DIM, SSD_STATE)
    def step(h, inp):
        dec, st = inp
        return dec[..., None, None] * h + st, h
    h_fin, h_in = lax.scan(step, h0g, (jnp.moveaxis(chunk_decay, 1, 0), jnp.moveaxis(chunk_states, 1, 0)))
    h_in = jnp.moveaxis(h_in, 0, 1)
    y_off = jnp.einsum('bcqgn,bcghpn->bcqghp', cc, h_in) * jnp.exp(acum)[..., None]
    y = (y_diag + y_off).reshape(bsz, nc * CHUNK, SSD_HEADS, SSD_HEAD_DIM)[:, :L]
    return y, h_fin.reshape(bsz, SSD_HEADS, SSD_HEAD_DIM, SSD_STATE)

def rglru(xb, h0, wa, ba, wx, bx, lam):
    f32 = jnp.float32
    bsz, L = xb.shape[0], xb.shape[1]
    xf = xb.astype(f32)
    xblk = xf.reshape(bsz, L, LRU_BLOCKS, LRU_BLOCK_DIM)
    r = jax.nn.sigmoid(jnp.einsum('blnd,nde->blne', xblk, wa.astype(f32)).reshape(bsz, L, LRU_WIDTH) + ba.astype(f32))
    i = jax.nn.sigmoid(jnp.einsum('blnd,nde->blne', xblk, wx.astype(f32)).reshape(bsz, L, LRU_WIDTH) + bx.astype(f32))
    log_a = -LRU_C * r * jax.nn.softplus(-lam.astype(f32))
    a = jnp.exp(log_a)
    u = jnp.sqrt(-jnp.expm1(2.0 * log_a)) * (i * xf)
    def step(h, inp):
        a_t, u_t = inp
        h = a_t * h + u_t
        return h, h
    h_last, hs = lax.scan(step, h0.astype(f32), (jnp.swapaxes(a, 0, 1), jnp.swapaxes(u, 0, 1)))
    return jnp.swapaxes(hs, 0, 1), h_last

def token_mixer(h, ssd_h0, ssd_buf, lru_h0, lru_buf, w_in, ssd_conv_w, ssd_conv_b, ssd_dt_bias, ssd_a_log,
                ssd_d, ssd_norm_w, lru_conv_w, lru_conv_b, lru_wa, lru_ba, lru_wx, lru_bx, lru_lambda,
                w_br_ssd, w_br_lru, w_out):
    bsz, L = h.shape[0], h.shape[1]
    proj = h @ w_in
    z, xbc, dt, lx, ly, g_ssd, g_lru = jnp.split(proj, [Z_END, XBC_END, DT_END, LX_END, LY_END, GS_END], axis=-1)
    xbc, ssd_buf_new = causal_conv(xbc, ssd_buf, ssd_conv_w, ssd_conv_b)
    xbc = jax.nn.silu(xbc)
    xs, bm, cm = jnp.split(xbc, [SSD_INNER, SSD_INNER + SSD_GROUPS * SSD_STATE], axis=-1)
    xs = xs.reshape(bsz, L, SSD_HEADS, SSD_HEAD_DIM)
    bm = bm.reshape(bsz, L, SSD_GROUPS, SSD_STATE)
    cm = cm.reshape(bsz, L, SSD_GROUPS, SSD_STATE)
    dtf = jax.nn.softplus(dt.astype(jnp.float32) + ssd_dt_bias.astype(jnp.float32))
    a = -jnp.exp(ssd_a_log.astype(jnp.float32))
    y, ssd_h_new = ssd_scan(xs, dtf, a, bm, cm, ssd_h0)
    y = y + ssd_d.astype(jnp.float32)[:, None] * xs.astype(jnp.float32)
    y = y.reshape(bsz, L, SSD_INNER).astype(h.dtype) * jax.nn.silu(z)
    y_ssd = rmsnorm(y, ssd_norm_w)
    lx, lru_buf_new = causal_conv(lx, lru_buf, lru_conv_w, lru_conv_b)
    hs, lru_h_new = rglru(lx, lru_h0, lru_wa, lru_ba, lru_wx, lru_bx, lru_lambda)
    y_lru = hs.astype(h.dtype) * jax.nn.gelu(ly)
    merged = jax.nn.sigmoid(g_ssd) * (y_ssd @ w_br_ssd) + jax.nn.sigmoid(g_lru) * (y_lru @ w_br_lru)
    return merged @ w_out, ssd_h_new, ssd_buf_new, lru_h_new, lru_buf_new

def peer(h, wq, k1, k2, u, v):
    f32 = jnp.float32
    bsz, L, D = h.shape
    T = bsz * L
    hf = h.reshape(T, D)
    q = (hf @ wq).astype(f32).reshape(T, PEER_HEADS, PEER_KEY_DIM)
    half = PEER_KEY_DIM // 2
    s1 = jnp.einsum('thd,kd->thk', q[..., :half], k1.astype(f32))
    s2 = jnp.einsum('thd,kd->thk', q[..., half:], k2.astype(f32))
    v1, i1 = lax.top_k(s1, PEER_TOPK)
    v2, i2 = lax.top_k(s2, PEER_TOPK)
    cand = (v1[..., :, None] + v2[..., None, :]).reshape(T, PEER_HEADS, PEER_TOPK * PEER_TOPK)
    sv, si = lax.top_k(cand, PEER_TOPK)
    e = (jnp.take_along_axis(i1, si // PEER_TOPK, axis=-1) * PEER_KEYS
         + jnp.take_along_axis(i2, si % PEER_TOPK, axis=-1))
    g = jax.nn.softmax(sv, axis=-1)
    e = e.reshape(T, PEER_HEADS * PEER_TOPK)
    g = g.reshape(T, PEER_HEADS * PEER_TOPK).astype(h.dtype)
    nb = -(-T // PEER_BLOCK)
    pad = nb * PEER_BLOCK - T
    hb = jnp.pad(hf, ((0, pad), (0, 0))).reshape(nb, PEER_BLOCK, D)
    eb = jnp.pad(e, ((0, pad), (0, 0))).reshape(nb, PEER_BLOCK, PEER_HEADS * PEER_TOPK)
    gb = jnp.pad(g, ((0, pad), (0, 0))).reshape(nb, PEER_BLOCK, PEER_HEADS * PEER_TOPK)
    def blk(args):
        hx, ex, gx = args
        act = jax.nn.gelu(jnp.einsum('td,tkd->tk', hx, u[ex])) * gx
        return jnp.einsum('tk,tkd->td', act, v[ex])
    out = lax.map(blk, (hb, eb, gb)).reshape(nb * PEER_BLOCK, D)[:T]
    return out.reshape(bsz, L, D)

def layer(x, c, ssd_h0, ssd_buf, lru_h0, lru_buf, ln1_w, ln2_w, w_mod, b_mod, w_in, ssd_conv_w, ssd_conv_b,
          ssd_dt_bias, ssd_a_log, ssd_d, ssd_norm_w, lru_conv_w, lru_conv_b, lru_wa, lru_ba, lru_wx, lru_bx,
          lru_lambda, w_br_ssd, w_br_lru, w_out, peer_wq, peer_k1, peer_k2, peer_u, peer_v):
    mod = (jax.nn.silu(c) @ w_mod + b_mod)[:, None, :]
    sh1, sc1, g1, sh2, sc2, g2 = jnp.split(mod, 6, axis=-1)
    h = rmsnorm(x, ln1_w) * (1.0 + sc1) + sh1
    tm, ssd_h, ssd_b, lru_h, lru_b = token_mixer(
        h, ssd_h0, ssd_buf, lru_h0, lru_buf, w_in, ssd_conv_w, ssd_conv_b, ssd_dt_bias, ssd_a_log, ssd_d,
        ssd_norm_w, lru_conv_w, lru_conv_b, lru_wa, lru_ba, lru_wx, lru_bx, lru_lambda, w_br_ssd, w_br_lru, w_out)
    x = x + g1 * tm
    h = rmsnorm(x, ln2_w) * (1.0 + sc2) + sh2
    x = x + g2 * peer(h, peer_wq, peer_k1, peer_k2, peer_u, peer_v)
    return x, ssd_h, ssd_b, lru_h, lru_b

def trunk(x, c, ssd_h, ssd_buf, lru_h, lru_buf, layer_w, final_norm_w):
    n_ssd, n_sbuf, n_lru, n_lbuf = [], [], [], []
    for l in range(DEPTH):
        wl = [w[l] for w in layer_w]
        x, sh, sb, lh, lb = layer(x, c, ssd_h[l], ssd_buf[l], lru_h[l], lru_buf[l], *wl)
        n_ssd.append(sh)
        n_sbuf.append(sb)
        n_lru.append(lh)
        n_lbuf.append(lb)
    y = rmsnorm(x, final_norm_w)
    return y, jnp.stack(n_ssd), jnp.stack(n_sbuf), jnp.stack(n_lru), jnp.stack(n_lbuf)

def setup_inputs(seed: int = 0) -> dict:
    key = jax.random.key(seed)
    ks = jax.random.split(key, 40)
    f32 = jnp.float32
    D = D_MODEL
    nrm = lambda k, shape, s: jax.random.normal(k, shape, f32) * s
    dt0 = jnp.exp(jax.random.uniform(ks[15], (DEPTH, SSD_HEADS), f32, np.log(1e-3), np.log(1e-1)))
    a0 = jax.random.uniform(ks[22], (DEPTH, LRU_WIDTH), f32, 0.9, 0.999)
    s0 = a0 ** (1.0 / LRU_C)
    return {
        'x_prompt': nrm(ks[0], (BATCH, SEQ, D), 1.0),
        'x_sample': nrm(ks[1], (DEC_BATCH, DEC_SEQ, D), 1.0),
        'c_prompt': nrm(ks[2], (BATCH, D), 1.0),
        'c_sample': nrm(ks[3], (DEC_BATCH, D), 1.0),
        'state_ssd': nrm(ks[4], (DEPTH, DEC_BATCH, SSD_HEADS, SSD_HEAD_DIM, SSD_STATE), 0.3),
        'state_ssd_conv': nrm(ks[5], (DEPTH, DEC_BATCH, CONV_W - 1, SSD_CONV_DIM), 1.0),
        'state_lru': nrm(ks[6], (DEPTH, DEC_BATCH, LRU_WIDTH), 0.5),
        'state_lru_conv': nrm(ks[7], (DEPTH, DEC_BATCH, CONV_W - 1, LRU_WIDTH), 1.0),
        'ln1_w': 1.0 + nrm(ks[8], (DEPTH, D), 0.02),
        'ln2_w': 1.0 + nrm(ks[9], (DEPTH, D), 0.02),
        'w_mod': nrm(ks[10], (DEPTH, D, 6 * D), 0.5 * D ** -0.5),
        'b_mod': nrm(ks[11], (DEPTH, 6 * D), 0.02),
        'w_in': nrm(ks[12], (DEPTH, D, IN_COLS), D ** -0.5),
        'ssd_conv_w': nrm(ks[13], (DEPTH, CONV_W, SSD_CONV_DIM), 0.5),
        'ssd_conv_b': nrm(ks[14], (DEPTH, SSD_CONV_DIM), 0.02),
        'ssd_dt_bias': dt0 + jnp.log(-jnp.expm1(-dt0)),
        'ssd_a_log': jnp.log(jax.random.uniform(ks[16], (DEPTH, SSD_HEADS), f32, 1.0, 16.0)),
        'ssd_d': 1.0 + nrm(ks[17], (DEPTH, SSD_HEADS), 0.02),
        'ssd_norm_w': 1.0 + nrm(ks[18], (DEPTH, SSD_INNER), 0.02),
        'lru_conv_w': nrm(ks[19], (DEPTH, CONV_W, LRU_WIDTH), 0.5),
        'lru_conv_b': nrm(ks[20], (DEPTH, LRU_WIDTH), 0.02),
        'lru_wa': nrm(ks[21], (DEPTH, LRU_BLOCKS, LRU_BLOCK_DIM, LRU_BLOCK_DIM), LRU_BLOCK_DIM ** -0.5),
        'lru_ba': nrm(ks[23], (DEPTH, LRU_WIDTH), 0.02),
        'lru_wx': nrm(ks[24], (DEPTH, LRU_BLOCKS, LRU_BLOCK_DIM, LRU_BLOCK_DIM), LRU_BLOCK_DIM ** -0.5),
        'lru_bx': nrm(ks[25], (DEPTH, LRU_WIDTH), 0.02),
        'lru_lambda': jnp.log(s0) - jnp.log1p(-s0),
        'w_br_ssd': nrm(ks[26], (DEPTH, SSD_INNER, D), SSD_INNER ** -0.5),
        'w_br_lru': nrm(ks[27], (DEPTH, LRU_WIDTH, D), LRU_WIDTH ** -0.5),
        'w_out': nrm(ks[28], (DEPTH, D, D), D ** -0.5),
        'peer_wq': nrm(ks[29], (DEPTH, D, PEER_HEADS * PEER_KEY_DIM), D ** -0.5),
        'peer_k1': nrm(ks[30], (DEPTH, PEER_KEYS, PEER_KEY_DIM // 2), (PEER_KEY_DIM // 2) ** -0.5),
        'peer_k2': nrm(ks[31], (DEPTH, PEER_KEYS, PEER_KEY_DIM // 2), (PEER_KEY_DIM // 2) ** -0.5),
        'peer_u': nrm(ks[32], (DEPTH, PEER_EXPERTS, D), D ** -0.5),
        'peer_v': nrm(ks[33], (DEPTH, PEER_EXPERTS, D), 0.2),
        'final_norm_w': 1.0 + nrm(ks[34], (D,), 0.02),
    }

def reference(x_prompt, x_sample, c_prompt, c_sample, state_ssd, state_ssd_conv, state_lru, state_lru_conv,
              ln1_w, ln2_w, w_mod, b_mod, w_in, ssd_conv_w, ssd_conv_b, ssd_dt_bias, ssd_a_log, ssd_d,
              ssd_norm_w, lru_conv_w, lru_conv_b, lru_wa, lru_ba, lru_wx, lru_bx, lru_lambda, w_br_ssd,
              w_br_lru, w_out, peer_wq, peer_k1, peer_k2, peer_u, peer_v, final_norm_w):
    layer_w = (ln1_w, ln2_w, w_mod, b_mod, w_in, ssd_conv_w, ssd_conv_b, ssd_dt_bias, ssd_a_log, ssd_d,
               ssd_norm_w, lru_conv_w, lru_conv_b, lru_wa, lru_ba, lru_wx, lru_bx, lru_lambda, w_br_ssd,
               w_br_lru, w_out, peer_wq, peer_k1, peer_k2, peer_u, peer_v)
    bp = x_prompt.shape[0]
    z_ssd = jnp.zeros((DEPTH, bp, SSD_HEADS, SSD_HEAD_DIM, SSD_STATE), jnp.float32)
    z_sconv = jnp.zeros((DEPTH, bp, CONV_W - 1, SSD_CONV_DIM), x_prompt.dtype)
    z_lru = jnp.zeros((DEPTH, bp, LRU_WIDTH), jnp.float32)
    z_lconv = jnp.zeros((DEPTH, bp, CONV_W - 1, LRU_WIDTH), x_prompt.dtype)
    y_prompt, p_ssd, p_sconv, p_lru, p_lconv = trunk(
        x_prompt, c_prompt, z_ssd, z_sconv, z_lru, z_lconv, layer_w, final_norm_w)
    y_sample, s_ssd, s_sconv, s_lru, s_lconv = trunk(
        x_sample, c_sample, state_ssd, state_ssd_conv, state_lru, state_lru_conv, layer_w, final_norm_w)
    return (y_prompt, y_sample, p_ssd, p_sconv, p_lru, p_lconv, s_ssd, s_sconv, s_lru, s_lconv)


_drawn_inputs = setup_inputs


def setup_inputs(seed=0):
    import zlib

    import numpy as np

    out = dict(_drawn_inputs(seed))
    spreads = {}
    factors = {'ln2_w': 8.0,
     'ssd_d': 8.0,
     'ssd_norm_w': 8.0,
     'lru_ba': 8.0,
     'lru_bx': 7.159,
     'final_norm_w': 2.842}
    for name, (base, spread) in spreads.items():
        noise = np.random.default_rng([zlib.crc32(name.encode()), seed]).standard_normal(out[name].shape)
        drawn = base * np.exp(spread * noise) if base else spread * noise
        out[name] = __import__('jax').numpy.asarray(drawn.astype(out[name].dtype))
    for name, factor in factors.items():
        out[name] = (out[name] * factor).astype(out[name].dtype)
    return out
```

```python
import concourse.bass as bass
from concourse import mybir
from contextlib import ExitStack

F32 = mybir.dt.float32
U32 = mybir.dt.uint32
ALU = mybir.AluOpType
ACT = mybir.ActivationFunctionType
AX = mybir.AxisListType
ds = bass.ds

DEPTH, D, P = 2, 1024, 128
KT = D // P
SEQ, STREAMS, SLEN = 512, 8, 16
TT = SEQ + STREAMS * SLEN
NT = TT // P
NB = TT // SLEN
HEADS, HD, NS = 16, 64, 64
CONVC = D + 4 * NS
W = 4
HIST = W - 1
EPS = 1e-6
PH, KEYS, TOPK = 8, 128, 16
PICKS = PH * TOPK
Z0, X0, DT0, LX0, LY0, GS0, GL0 = 0, D, D + CONVC, D + CONVC + HEADS, 2 * D + CONVC + HEADS, 3 * D + CONVC + HEADS, \
    4 * D + CONVC + HEADS
NEG = -3.0e38

SLOTS = 8
RING, HALF = 16, 8

LN1, LN2, NW, BA, BX, LAM, LCB, LCW, SCB = 0, 8, 16, 24, 32, 40, 48, 56, 88
ROWS_A = 98
SCW, BMOD, FIN, DD = ROWS_A, ROWS_A + 40, ROWS_A + 88, ROWS_A + 96
ROWS_B = 104
H0 = ROWS_A + ROWS_B
CV = H0 + 64
NCOLS = CV + 72


def build(nc, a):
    ctx = ExitStack()
    with ctx:
        def sb(name, shape, dt=F32):
            return ctx.enter_context(nc.sbuf_tensor(name, shape, dt))

        gathered = [ctx.enter_context(nc.semaphore(f"gathered_{n}")) for n in range(RING)]
        nums = []

        def sem(name):
            s = ctx.enter_context(nc.semaphore(name))
            nums.append(s.num)
            return s

        names = {}

        def phase_sem(name):
            if name not in names:
                names[name] = sem(name)
            return names[name]

        xT = sb("xT", [P, KT, TT])
        hT = sb("hT", [P, KT, TT])
        modE = sb("modE", [P, 6 * KT, NB])
        cols = sb("cols", [P, NCOLS])
        ident = sb("ident", [P, P])
        ones = sb("ones", [P, P])
        zeros = sb("zeros", [P, P])
        upto = [sb(f"upto{s}", [P, P]) for s in range(2)]
        after = [sb(f"after{s}", [P, P]) for s in range(2)]
        stream_of = sb("stream_of", [P, STREAMS])
        iota16 = sb("iota16", [P, TOPK])
        layer_row = sb("layer_row", [P, DEPTH])
        alog = sb("alog", [P, HEADS])
        dtb = sb("dtb", [P, HEADS])
        negA = sb("negA", [P, HEADS])
        dt = sb("dt", [P, NT, HEADS])
        dta = sb("dta", [P, NT, HEADS])
        spw = sb("spw", [P, 4, NT * HEADS])
        lamS = sb("lamS", [P, KT])
        stT = sb("stT", [P, 8 * HD])
        lruN = sb("lruN", [P, KT, 9])
        rowbuf = sb("rowbuf", [P, 2, P])
        small = sb("small", [P, 48])
        arenaR = sb("arenaR", [P, RING * D])
        arenaQ = sb("arenaQ", [P, 18 * TT])
        arenaW = sb("arenaW", [P, SLOTS * D])
        arenaX = sb("arenaX", [P, 2048])
        psum = ctx.enter_context(nc.psum_tensor("psum", [P, 8, 512], F32))

        def view(arena, at, *shape):
            n = 1
            for s in shape:
                n *= s
            v = arena[:, at:at + n]
            if len(shape) == 2:
                return v.rearrange("p (a b) -> p a b", a=shape[0])
            if len(shape) == 3:
                return v.rearrange("p (a b c) -> p a b c", a=shape[0], b=shape[1])
            return v

        wt = view(arenaW, 0, SLOTS, KT, P)
        ysT = view(arenaR, 0, KT, TT)
        ylT = view(arenaR, KT * TT, KT, TT)
        mT = view(arenaR, 2 * KT * TT, KT, TT)
        xbcT = view(arenaQ, 0, 10, TT)
        lxT = view(arenaQ, 10 * TT, KT, TT)

        def bank(b, n=1):
            return psum[:, b:b + n, :].rearrange("p b c -> p (b c)")

        def weight(name, l, col):
            w = a[name].rearrange("l (k p) c -> p (l k) c", p=P)
            return w[:, ds(l * KT, KT), ds(col, P)]

        def project(slot, src, out):
            for o, n in ((0, SEQ), (SEQ, TT - SEQ)):
                for k in range(KT):
                    last = nc.tensor.matmul(out[:, o:o + n], wt[:, slot, k, :], src[:, k, o:o + n],
                                            start=k == 0, stop=k == KT - 1)
            return last

        class Steps:

            def __init__(self, eng, name, base=0):
                self.eng, self.sem, self.base, self.n = eng, phase_sem(name), base, 0

            def __call__(self, ins):
                ins.then_inc(self.sem, 1)
                self.n += 1

            def wait(self, eng=None):
                (eng or self.eng).wait_ge(self.sem, self.base + self.n)

            def hold(self):
                hold(self.eng, self.sem, self.base + self.n)

        def hold(eng, s, value):
            eng.wait_ge(s, value)
            eng.sem_inc(phase_sem("held"), 1)

        def end_phase():
            nc.all_engine_barrier(sems_to_clear=range(min(nums), max(nums) + 1))

        def b16(ap, n=SLEN):
            return ap.unsqueeze(len(ap.shape)).to_broadcast([*ap.shape, n])

        def softplus(dve, st, ready, x, n, out, work):
            ax, z, z2, q = (work[:, i, 0:n] for i in range(4))
            st(dve.scalar_tensor_tensor(ax, x, -1.0, x, ALU.mult, ALU.min))
            st.wait()
            dve.sem_inc(ready[0], 1)
            dve.wait_ge(ready[1], 1)
            st(dve.tensor_scalar(z, ax, 2.0, None, ALU.add))
            st.wait()
            st(dve.reciprocal(z2, z))
            st.wait()
            st(dve.tensor_tensor(z, ax, z2, ALU.mult))
            st.wait()
            st(dve.tensor_tensor(z2, z, z, ALU.mult))
            st(dve.memset(q, 1.0 / 17))
            st.wait()
            first = True
            for c in (15, 13, 11, 9, 7, 5, 3):
                if first:
                    st(dve.tensor_tensor(q, q, z2, ALU.mult))
                    first = False
                    st.wait()
                st(dve.scalar_tensor_tensor(q, q, 1.0 / c, z2, ALU.add, ALU.mult))
                st.wait()
            st(dve.scalar_tensor_tensor(q, q, 1.0, z, ALU.add, ALU.mult))
            st(dve.tensor_scalar(z2, x, 0.0, None, ALU.max))
            st.wait()
            st(dve.scalar_tensor_tensor(out, q, 2.0, z2, ALU.mult, ALU.add))
            st.wait()

        xin = view(arenaR, 0, NT, D)
        x_loaded, s_const, xt_done, x_copied = (sem(n) for n in ("x_loaded", "s_const", "xt_done", "x_copied"))
        with nc.Block() as block:
            @block.sync
            def _(sp):
                sp.dma_start(xin[:, 0:4, :], a["x_prompt"].rearrange("o (t p) d -> p (o t) d", p=P)).then_inc(x_loaded, 16)
                sp.dma_start(xin[:, 4, :], a["x_sample"].rearrange("b t d -> (b t) d")).then_inc(x_loaded, 16)

            @block.gpsimd
            def _(pool):
                n = 0

                def put(ins):
                    nonlocal n
                    ins.then_inc(s_const, 1)
                    n += 1

                put(pool.memset(ident[:], 1.0))
                put(pool.memset(ones[:], 1.0))
                put(pool.memset(zeros[:], 0.0))
                put(pool.memset(stream_of[:], 1.0))
                put(pool.iota(iota16[:], [[1, TOPK]], base=0, channel_multiplier=0, allow_small_or_imprecise_dtypes=True))
                put(pool.iota(layer_row[:], [[KEYS * KEYS, DEPTH]], base=0, channel_multiplier=0, allow_small_or_imprecise_dtypes=True))
                pool.wait_ge(s_const, n)
                put(pool.affine_select(out=ident[:], in_=ident[:], compare_op=ALU.is_equal, fill=0.0, base=0,
                                       pattern=[[-1, P]], channel_multiplier=1))
                for s in range(2):
                    put(pool.affine_select(out=upto[s][:], in_=ones[:], compare_op=ALU.is_ge, fill=0.0, base=0,
                                           pattern=[[1, P]], channel_multiplier=-1))
                    put(pool.affine_select(out=after[s][:], in_=ones[:], compare_op=ALU.is_ge, fill=0.0, base=-1,
                                           pattern=[[-1, P]], channel_multiplier=1))
                put(pool.affine_select(out=stream_of[:], in_=stream_of[:], compare_op=ALU.is_ge, fill=0.0, base=0,
                                       pattern=[[-SLEN, STREAMS]], channel_multiplier=1))
                pool.wait_ge(s_const, n)
                put(pool.affine_select(out=stream_of[:], in_=stream_of[:], compare_op=ALU.is_ge, fill=0.0,
                                       base=SLEN - 1, pattern=[[SLEN, STREAMS]], channel_multiplier=-1))
                put(pool.affine_select(out=upto[1][:], in_=upto[1][:], compare_op=ALU.is_ge, fill=0.0, base=0,
                                       pattern=[[-SLEN, STREAMS], [0, SLEN]], channel_multiplier=1))
                put(pool.affine_select(out=after[1][:], in_=after[1][:], compare_op=ALU.is_ge, fill=0.0,
                                       base=SLEN - 1, pattern=[[SLEN, STREAMS], [0, SLEN]], channel_multiplier=-1))
                pool.wait_ge(s_const, n)

            @block.tensor
            def _(pe):
                pe.wait_ge(x_loaded, 32)
                pe.wait_ge(s_const, 15)
                for t in range(NT):
                    if t >= 4:
                        pe.wait_ge(x_copied, t - 3)
                    o = bank(2 * (t % 4), 2)
                    for k in range(KT):
                        last = pe.transpose(o[:, k * P:(k + 1) * P], xin[:, t, k * P:(k + 1) * P], ident[:])
                    last.then_inc(xt_done, 1)

            @block.vector
            def _(dve):
                for t in range(NT):
                    dve.wait_ge(xt_done, t + 1)
                    dve.tensor_copy(xT[:, :, t * P:(t + 1) * P],
                                    bank(2 * (t % 4), 2).rearrange("p (k c) -> p k c", k=KT)).then_inc(x_copied, 1)
                dve.wait_ge(x_copied, NT)
        end_phase()

        def norm_phase(out, scale, shift):
            sq = view(arenaW, 0, KT, TT)
            rs = arenaX[:, 0:TT]
            with nc.Block() as block:
                squared, summed, rooted, ready = (phase_sem(n) for n in ("squared", "summed", "rooted", "root_in"))

                @block.scalar
                def _(act):
                    for k in range(KT):
                        act.activation(sq[:, k, :], xT[:, k, :], ACT.Square).then_inc(squared, 1)
                    act.wait_ge(ready, 1)
                    act.activation(rs, rs, ACT.Sqrt).then_inc(rooted, 1)

                @block.tensor
                def _(pe):
                    o = bank(0, 2)
                    for k in range(KT):
                        pe.wait_ge(squared, k + 1)
                        for at, n in ((0, SEQ), (SEQ, TT - SEQ)):
                            last = pe.matmul(o[:, at:at + n], ones[:], sq[:, k, at:at + n], start=k == 0,
                                             stop=k == KT - 1)
                    last.then_inc(summed, 1)

                @block.vector
                def _(dve):
                    st = Steps(dve, "dve_step")
                    dve.wait_ge(summed, 1)
                    dve.tensor_scalar(rs, bank(0, 2)[:, 0:TT], 1.0 / D, EPS, ALU.mult, ALU.add).then_inc(ready, 1)
                    dve.wait_ge(rooted, 1)
                    st(dve.reciprocal(rs, rs))
                    st.wait()
                    for k in range(KT):
                        st(dve.tensor_tensor(out[:, k, :], xT[:, k, :], rs, ALU.mult))
                    st.wait()
                    if len(scale.shape) == 2:
                        for k in range(KT):
                            st(dve.tensor_scalar(out[:, k, :], out[:, k, :], scale[:, k:k + 1], None, ALU.mult))
                        st.wait()
                    else:
                        v = out.rearrange("p k (b t) -> p (k b) t", t=SLEN)
                        st(dve.tensor_tensor(v, v, b16(scale.rearrange("p k b -> p (k b)")), ALU.mult))
                        st.wait()
                        st(dve.tensor_tensor(v, v, b16(shift.rearrange("p k b -> p (k b)")), ALU.add))
                        st.wait()
            end_phase()

        with nc.Fori(0, DEPTH) as l:
            with nc.Block() as block:
                d2 = small[96:104, 0:2]
                rowsD = arenaX[:, 0:P]
                rowsC = arenaX[:, P:2 * P]
                loaded, d_spread, silued, turned, colsd = (phase_sem(n) for n in (
                    "vectors_loaded", "d_spread", "c_silued", "vectors_turned", "vectors_ready"))
                wready = [phase_sem(f"weight_ready_{s}") for s in range(SLOTS)]
                wused, mod_free, mod_done = phase_sem("weight_used"), phase_sem("mod_free"), phase_sem("mod_done")
                ex_in, ex_out = phase_sem("exp_in"), phase_sem("exp_out")

                def rows(name, n, spec="l (k c) -> (l k) c"):
                    return a[name].rearrange(spec, c=P)[ds(l * n, n), :]

                @block.sync
                def _(sp):
                    for r, at, src in (
                        (0, LN1, rows("ln1_w", 8)), (0, LN2, rows("ln2_w", 8)), (0, NW, rows("ssd_norm_w", 8)),
                        (0, BA, rows("lru_ba", 8)), (0, BX, rows("lru_bx", 8)), (0, LAM, rows("lru_lambda", 8)),
                        (0, LCB, rows("lru_conv_b", 8)), (0, LCW, rows("lru_conv_w", 32, "l w (k c) -> (l w k) c")),
                        (0, SCB, rows("ssd_conv_b", 10)), (1, 0, rows("ssd_conv_w", 40, "l w (k c) -> (l w k) c")),
                        (1, 40, rows("b_mod", 48)),
                        (1, 88, a["final_norm_w"].rearrange("(k c) -> k c", c=P)),
                    ):
                        sp.dma_start(rowbuf[at:at + src.shape[0], r, :], src).then_inc(loaded, 16)
                    sp.dma_start(rowsC[0:64, :], rows("state_lru", 64, "l b (k c) -> (l b k) c")).then_inc(loaded, 16)
                    sp.dma_start(rowsD[0:8, :], a["c_prompt"].rearrange("s (k c) -> (s k) c", c=P)).then_inc(loaded, 16)
                    sp.dma_start(rowsD[8:72, :], a["c_sample"].rearrange("s (k c) -> (s k) c", c=P)).then_inc(loaded, 16)
                    sp.dma_start(d2, a["ssd_d"].rearrange("l (j h) -> (l j) h", h=2)[ds(l * 8, 8), :]).then_inc(loaded, 16)
                    sp.dma_start(alog[:], a["ssd_a_log"][ds(l, 1), :].to_broadcast([P, HEADS])).then_inc(loaded, 16)
                    sp.dma_start(dtb[:], a["ssd_dt_bias"][ds(l, 1), :].to_broadcast([P, HEADS])).then_inc(loaded, 16)
                    sp.sem_inc(wused, SLOTS)
                    with sp.Fori(0, 6) as j:
                        for s in range(SLOTS):
                            sp.wait_ge(wused, j * SLOTS + s + 1)
                            sp.dma_start(wt[:, s, :, :], weight("w_mod", l, j * (SLOTS * P) + s * P)).then_inc(wready[s], 16)

                @block.scalar
                def _(act):
                    act.wait_ge(loaded, 18 * 16)
                    act.activation(rowsD[0:72, :], rowsD[0:72, :], ACT.Silu).then_inc(silued, 1)
                    act.activation(negA[:], alog[:], ACT.Exp).then_inc(silued, 1)
                    act.wait_ge(ex_in, 1)
                    act.activation(spw[:, 0, 0:KT], spw[:, 0, 0:KT], ACT.Exp).then_inc(ex_out, 1)

                @block.tensor
                def _(pe):
                    pe.wait_ge(loaded, 18 * 16)
                    pe.wait_ge(silued, 1)
                    pe.wait_ge(d_spread, 1)
                    pe.transpose(bank(7)[:, 0:ROWS_A], rowbuf[0:ROWS_A, 0, :], ident[0:ROWS_A, 0:ROWS_A])
                    pe.transpose(bank(7)[:, ROWS_A:H0], rowbuf[0:ROWS_B, 1, :], ident[0:ROWS_B, 0:ROWS_B])
                    pe.transpose(bank(7)[:, H0:CV], rowsC[0:64, :], ident[0:64, 0:64])
                    pe.transpose(bank(7)[:, CV:NCOLS], rowsD[0:72, :], ident[0:72, 0:72]).then_inc(turned, 1)
                    pe.wait_ge(colsd, 1)
                    cT = cols[:, CV:NCOLS].rearrange("p (s k) -> p k s", k=KT)
                    pe.sem_inc(mod_free, 2)
                    with pe.Fori(0, 6) as j:
                        for hf in range(2):
                            pe.wait_ge(mod_free, j * 2 + hf + 1)
                            for s in range(hf * 4, hf * 4 + 4):
                                pe.wait_ge(wready[s], j * 16 + 16)
                                o = bank(hf)[:, (s % 4) * 9:(s % 4) * 9 + 9]
                                for k in range(KT):
                                    last = pe.matmul(o, wt[:, s, k, :], cT[:, k, :], start=k == 0, stop=k == KT - 1)
                                last.then_inc(wused, 1)

                @block.vector
                def _(dve):
                    st = Steps(dve, "dve_step")
                    dve.wait_ge(loaded, 18 * 16)
                    dve.tensor_copy(rowbuf[96:104, 1, :].rearrange("p (h c) -> p h c", h=2), b16(d2, HD)).then_inc(d_spread, 1)
                    dve.wait_ge(turned, 1)
                    dve.tensor_copy(cols[:], bank(7)[:, 0:NCOLS]).then_inc(colsd, 1)
                    dve.wait_ge(silued, 2)
                    st(dve.tensor_scalar(negA[:], negA[:], -1.0, None, ALU.mult))
                    dve.wait_ge(colsd, 1)
                    lam = spw[:, 0, 16:16 + KT]
                    st(dve.tensor_scalar(lam, cols[:, LAM:LAM + KT], -1.0, None, ALU.mult))
                    st.wait()
                    softplus(dve, st, (ex_in, ex_out), lam, KT, lamS[:], spw)
                    st(dve.tensor_scalar(lamS[:], lamS[:], -4.0, None, ALU.mult))
                    with dve.Fori(0, 6) as j:
                        for hf in range(2):
                            dve.wait_ge(wused, SLOTS + j * SLOTS + hf * 4 + 4)
                            src = bank(hf)[:, 0:36].rearrange("p (s c) -> p s c", c=9)
                            at = j * SLOTS + hf * 4
                            bias = cols[:, ds(BMOD + at, 4)].unsqueeze(2)
                            dve.tensor_tensor(modE[:, ds(at, 4), 0:32], src[:, :, 0:1].to_broadcast([P, 4, 32]),
                                              bias.to_broadcast([P, 4, 32]), ALU.add)\
                               .then_inc(mod_done, 1)
                            dve.tensor_tensor(modE[:, ds(at, 4), 32:40], src[:, :, 1:9],
                                              bias.to_broadcast([P, 4, 8]), ALU.add).then_inc(mod_free, 1)
                    dve.wait_ge(mod_done, 12)
                    dve.wait_ge(mod_free, 14)
                    for at, ln in ((KT, LN1), (4 * KT, LN2)):
                        v = modE[:, at:at + KT, :]
                        st(dve.scalar_tensor_tensor(v, v, 1.0, cols[:, ln:ln + KT].unsqueeze(2).to_broadcast([P, KT, NB]),
                                                    ALU.add, ALU.mult))
                    st.wait()
            end_phase()

            norm_phase(hT[:], modE[:, KT:2 * KT, :], modE[:, 0:KT, :])

            def conv_phase(col0, tiles, dst, wcol, bcol, state, C, new_p, new_s, silu, with_dt):
                PADC = HIST + SEQ + STREAMS * (HIST + SLEN)
                xpad = view(arenaR, 0, 2, PADC + 1)
                acc = view(arenaR, 2 * (PADC + 1), 2, PADC + 1)
                pre = view(arenaR, 4 * (PADC + 1), 2, TT)
                hist = view(arenaR, 4 * (PADC + 1) + 2 * TT, 2, P)
                last27 = view(arenaR, 4 * (PADC + 1) + 2 * TT + 2 * P, 2, 27)
                newrow = view(arenaR, 8192, C)
                wdt = view(arenaR, 12288, KT, HEADS)
                sample = lambda v: v[:, HIST + SEQ:PADC].rearrange("p (b t) -> p b t", b=STREAMS)
                loops = tiles // 2
                NY = PADC - HIST
                with nc.Block() as block:
                    wready = [phase_sem(f"weight_ready_{s}") for s in range(2)]
                    hready = [phase_sem(f"history_ready_{s}") for s in range(2)]
                    proj_done, hist_done, padded, tails, tails_done, stored = (phase_sem(n) for n in (
                        "projected", "history_turned", "padded", "tails", "tails_turned", "tails_stored"))
                    conved, silued, wdt_ready, dt_done, zeroed = (phase_sem(n) for n in (
                        "convolved", "silued", "wdt_ready", "dt_projected", "zeroed"))
                    ex_in, ex_out, out_sem = phase_sem("exp_in"), phase_sem("exp_out"), phase_sem("out_written")

                    @block.sync
                    def _(sp):
                        if with_dt:
                            sp.dma_start(wdt, a["w_in"].rearrange("l (k p) c -> p (l k) c", p=P)[:, ds(l * KT, KT), DT0:DT0 + HEADS])\
                              .then_inc(wdt_ready, 16)
                        sp.sem_inc(proj_done, 2)
                        sp.sem_inc(hist_done, 2)
                        with sp.Fori(0, loops) as j:
                            for u in range(2):
                                sp.wait_ge(proj_done, 2 * j + u + 1)
                                sp.dma_start(wt[:, u, :, :], weight("w_in", l, col0 + j * (2 * P) + u * P)).then_inc(wready[u], 16)
                                sp.wait_ge(hist_done, 2 * j + u + 1)
                                sp.dma_start(hist[0:24, u, :], state.rearrange("l b w c -> (l b w) c")
                                             [ds(l * 24, 24), ds(j * (2 * P) + u * P, P)]).then_inc(hready[u], 16)
                        sp.wait_ge(stored, 2 + tiles)
                        sp.dma_start(new_p.rearrange("l b w c -> (l b w) c")[ds(l * 3, 3), :], newrow[0:3, :]).then_inc(out_sem, 16)
                        sp.dma_start(new_s.rearrange("l b w c -> (l b w) c")[ds(l * 24, 24), :], newrow[3:27, :]).then_inc(out_sem, 16)
                        sp.wait_ge(out_sem, 32)

                    @block.tensor
                    def _(pe):
                        if with_dt:
                            pe.wait_ge(wdt_ready, 16)
                            for t in range(NT):
                                for k in range(KT):
                                    last = pe.matmul(bank(7)[:, t * HEADS:(t + 1) * HEADS], hT[:, k, t * P:(t + 1) * P],
                                                     wdt[:, k, :], start=k == 0, stop=k == KT - 1)
                            last.then_inc(dt_done, 1)
                        pe.sem_inc(padded, 2)
                        pe.sem_inc(stored, 2)
                        with pe.Fori(0, loops) as j:
                            for u in range(2):
                                pe.wait_ge(wready[u], j * 16 + 16)
                                pe.wait_ge(padded, 2 * j + u + 1)
                                project(u, hT, bank(2 * u, 2)).then_inc(proj_done, 1)
                                hold(pe, hready[u], j * 16 + 16)
                                pe.transpose(bank(2 * u, 2)[:, TT:TT + 24], hist[0:24, u, :], ident[0:24, 0:24])\
                                  .then_inc(hist_done, 1)
                            for u in range(2):
                                pe.wait_ge(tails, 2 * j + u + 1)
                                pe.wait_ge(stored, 2 * j + u + 1)
                                pe.transpose(bank(5 + u)[0:27, 0:P], last27[:, u, :], ident[:]).then_inc(tails_done, 1)

                    @block.scalar
                    def _(act):
                        if with_dt:
                            act.wait_ge(ex_in, 1)
                            act.activation(spw[:, 0, :], spw[:, 0, :], ACT.Exp).then_inc(ex_out, 1)
                        act.sem_inc(conved, 2)
                        act.wait_ge(zeroed, 1)
                        filled = phase_sem("filled")
                        with act.Fori(0, loops) as j:
                            for u in range(2):
                                act.wait_ge(hist_done, 2 + 2 * j + u + 1)
                                act.wait_ge(conved, 2 * j + u + 1)
                                o = bank(2 * u, 2)
                                act.activation(xpad[:, u, HIST:HIST + SEQ], o[:, 0:SEQ], ACT.Copy).then_inc(filled, 1)
                                act.activation(sample(xpad[:, u, :])[:, :, 0:HIST],
                                               o[:, TT:TT + 24].rearrange("p (b t) -> p b t", b=STREAMS),
                                               ACT.Copy).then_inc(filled, 1)
                                act.activation(sample(xpad[:, u, :])[:, :, HIST:], o[:, SEQ:TT].rearrange("p (b t) -> p b t", b=STREAMS),
                                               ACT.Copy).then_inc(padded, 1)
                            for u in range(2):
                                act.wait_ge(tails_done, 2 * j + u + 1)
                                act.activation(newrow[0:27, ds(j * (2 * P) + u * P, P)], bank(5 + u)[0:27, 0:P], ACT.Copy)\
                                   .then_inc(stored, 1)
                                if silu:
                                    act.wait_ge(conved, 2 + 2 * j + u + 1)
                                    act.activation(dst[:, ds(2 * j + u, 1), :], pre[:, u:u + 1, :], ACT.Silu).then_inc(silued, 1)
                        if silu:
                            act.wait_ge(silued, 2 + tiles)

                    @block.vector
                    def _(dve):
                        st = Steps(dve, "dve_step")
                        for u in range(2):
                            st(dve.memset(xpad[:, u, 0:HIST], 0.0))
                        st.wait()
                        dve.sem_inc(zeroed, 1)
                        if with_dt:
                            dve.wait_ge(dt_done, 1)
                            v = dt[:].rearrange("p t h -> p (t h)")
                            st(dve.tensor_tensor(dt[:], bank(7)[:, 0:NT * HEADS].rearrange("p (t h) -> p t h", t=NT),
                                                 dtb[:].unsqueeze(1).to_broadcast([P, NT, HEADS]), ALU.add))
                            st.wait()
                            softplus(dve, st, (ex_in, ex_out), v, NT * HEADS, v, spw)
                            st(dve.tensor_tensor(dta[:], dt[:], negA[:].unsqueeze(1).to_broadcast([P, NT, HEADS]), ALU.mult))
                        filled = phase_sem("filled")
                        if silu:
                            dve.sem_inc(silued, 2)
                        PER = 10
                        with dve.Fori(0, loops) as j:
                            st = Steps(dve, "conv_step", j * PER)
                            for u in range(2):
                                dve.wait_ge(filled, 4 * j + 2 * u + 2)
                                dve.wait_ge(padded, 2 + 2 * j + u + 1)
                                x, y = xpad[:, u, :], acc[:, u, 0:NY]
                                st(dve.tensor_copy(last27[:, u, 0:3], x[:, SEQ:SEQ + HIST]))
                                dve.tensor_copy(last27[:, u, 3:27].rearrange("p (b t) -> p b t", b=STREAMS),
                                                sample(x)[:, :, SLEN:]).then_inc(tails, 1)
                                dve.wait_ge(tails, 2 * j + u + 1)
                                w = lambda k: cols[:, ds(wcol + k * tiles + 2 * j + u, 1)]
                                st(dve.tensor_scalar(y, x[:, 0:NY], w(0), cols[:, ds(bcol + 2 * j + u, 1)], ALU.mult, ALU.add))
                                st.wait()
                                for k in (1, 2):
                                    st(dve.scalar_tensor_tensor(y, x[:, k:k + NY], w(k), y, ALU.mult, ALU.add))
                                    st.wait()
                                if silu:
                                    dve.wait_ge(silued, 2 * j + u + 1)
                                    to = pre[:, u, :]
                                else:
                                    to = dst[:, ds(2 * j + u, 1), :].rearrange("p o t -> p (o t)")
                                st(dve.scalar_tensor_tensor(to[:, 0:SEQ], x[:, HIST:HIST + SEQ], w(3), y[:, 0:SEQ], ALU.mult, ALU.add))
                                ysam = acc[:, u, HIST + SEQ:HIST + SEQ + STREAMS * (HIST + SLEN)].rearrange("p (b t) -> p b t", b=STREAMS)
                                dve.scalar_tensor_tensor(to[:, SEQ:TT].rearrange("p (b t) -> p b t", b=STREAMS),
                                                         sample(x)[:, :, HIST:], w(3), ysam[:, :, 0:SLEN],
                                                         ALU.mult, ALU.add).then_inc(conved, 1)
                            assert st.n == PER, st.n
                        dve.wait_ge(conved, 2 + tiles)
                        dve.wait_ge(phase_sem("conv_step"), loops * PER)
                end_phase()

            conv_phase(X0, 10, xbcT, SCW, SCB, a["state_ssd_conv"], CONVC, a["new_ssd_conv_prompt"],
                       a["new_ssd_conv_sample"], True, True)
            conv_phase(LX0, 8, lxT, LCW, LCB, a["state_lru_conv"], D, a["new_lru_conv_prompt"],
                       a["new_lru_conv_sample"], False, False)

            at = KT * TT
            parts = {}
            for name, n in (("xc", 10 * P), ("mdta", 2048), ("E", 2048), ("Ea", 2048), ("Cw", 2048),
                            ("xw", 1024), ("cbm", 256), ("Btok", P)):
                parts[name] = (at, n)
                at += n
            assert at <= RING * D
            V = lambda n, *s: view(arenaR, parts[n][0], *s)
            xc, mdta, E, Ea = V("xc", 10, P), V("mdta", HEADS, P), V("E", HEADS, P), V("Ea", HEADS, P)
            Cw, xw, cbm, Btok = V("Cw", HEADS, P), V("xw", HEADS, HD), V("cbm", 2, P), V("Btok", P)
            xdt = view(arenaX, 0, HEADS, HD)
            Cz = view(arenaX, 1024, 2, P)
            stN = view(arenaW, 0, STREAMS * 4, P)
            stTb = view(arenaW, 4096, STREAMS, 4 * P)
            Bm = view(arenaX, 0, 2, STREAMS * NS)
            dtax = view(arenaX, 1024, HEADS, HD)
            ex = small[:, 0:48]
            with nc.Block() as block:
                S = {n: phase_sem("ssd_" + n) for n in (
                    "staged", "turned", "sums", "cb", "mdta", "seg", "E", "acb", "Ea", "ex", "xdt", "xw", "cbm", "W",
                    "Cw", "y", "stadd", "ydone", "state", "Btok", "st_in", "st_turned", "st_copied", "dtax", "dec",
                    "decE", "Bm", "cz", "zeroed", "sadd", "sadded", "outw", "free")}
                misc = bank(6)
                PX = bank(4, 2)
                Y = bank(4, 2)

                def state_view(name):
                    return a[name].rearrange("l b (j hh) p n -> (hh p) (l b j) n", hh=2)

                @block.sync
                def _(sp):
                    v = stN.rearrange("p (b j) (g n) -> p b j g n", j=4, g=2)
                    src = state_view("state_ssd")
                    for b in range(STREAMS):
                        for g in range(2):
                            sp.dma_start(v[:, b, :, g, :], src[:, ds(l * 64 + b * 8 + g * 4, 4), :]).then_inc(S["st_in"], 16)
                    sp.wait_ge(S["sadded"], 8)
                    dst = state_view("new_ssd_sample")
                    for b in range(STREAMS):
                        for g in range(2):
                            sp.dma_start(dst[:, ds(l * 64 + b * 8 + g * 4, 4), :], v[:, b, :, g, :]).then_inc(S["outw"], 16)
                    sp.wait_ge(S["stadd"], 5)
                    pv = E[:, 0:4, :].rearrange("p j (g n) -> p j g n", g=2)
                    dp = a["new_ssd_prompt"].rearrange("l b (j hh) p n -> (hh p) (l b j) n", hh=2)
                    for g in range(2):
                        sp.dma_start(dp[:, ds(l * 8 + g * 4, 4), :], pv[:, :, g, :]).then_inc(S["outw"], 16)
                    sp.wait_ge(S["outw"], 18 * 16)

                @block.gpsimd
                def _(pool):
                    def stage(t):
                        pool.tensor_copy(xc, xbcT[:, :, ds(t * P, P)]).then_inc(S["staged"], 1)
                        hold(pool, S["staged"], t + 1)
                        for g in range(2):
                            pool.tensor_copy(Cz[g * 64:g * 64 + 64, g, :], xc[g * 64:g * 64 + 64, 9, :]).then_inc(S["cz"], 1)

                    pool.memset(Cz, 0.0).then_inc(S["zeroed"], 1)
                    pool.memset(Cw, 0.0).then_inc(S["zeroed"], 1)
                    pool.wait_ge(S["zeroed"], 2)
                    with pool.Fori(0, 4) as t:
                        pool.wait_ge(S["ydone"], t)
                        stage(t)
                    pool.wait_ge(S["ydone"], 4)
                    stage(4)

                @block.tensor
                def _(pe):
                    def chunk(t, s):
                        pe.wait_ge(S["staged"], t + 1)
                        for k in range(KT):
                            pe.transpose(PX[:, k * P:(k + 1) * P], xc[:, k, :], ident[:])
                        pe.transpose(misc[:, 384:512], xc[:, 8, :], ident[:])
                        d = dta[:, ds(t, 1), :].rearrange("p o h -> p (o h)")
                        pe.wait_ge(S["cz"], 2 * t + 2)
                        last = pe.matmul(misc[:, 64:320], xc[:, 8, :], Cz.rearrange("p g q -> p (g q)"), start=True, stop=True)
                        last.then_inc(S["cb"], 1)
                        pe.wait_ge(S["state"], t + 1)
                        pe.matmul(bank(7)[:, 0:16], upto[s][:], d, start=True, stop=True)
                        pe.matmul(bank(7)[:, 16:32], after[s][:], d, start=True, stop=True)
                        pe.matmul(bank(7)[:, 32:48], ones[:], d, start=True, stop=True).then_inc(S["sums"], 1)
                        pe.wait_ge(S["mdta"], t + 1)
                        for i in range(4):
                            last = pe.matmul(bank(i), after[s][:], mdta[:, 4 * i:4 * i + 4, :].rearrange("p h q -> p (h q)"),
                                             start=True, stop=True)
                        last.then_inc(S["seg"], 1)
                        pe.wait_ge(S["E"], t + 1)
                        for i in range(4):
                            last = pe.matmul(bank(i), ones[:], mdta[:, 4 * i:4 * i + 4, :].rearrange("p h q -> p (h q)"),
                                             start=True, stop=True)
                        last.then_inc(S["acb"], 1)
                        pe.wait_ge(S["xw"], t + 1)
                        pe.wait_ge(S["W"], t + 1)
                        pe.wait_ge(S["Cw"], t + 1)
                        if s:
                            pe.wait_ge(S["st_copied"], 8)
                        for h in range(HEADS):
                            g, i = divmod(h, 8)
                            po = 64 * (h % 2)
                            o = Y[po:po + 64, (h // 2) * P:(h // 2 + 1) * P]
                            pe.matmul(o, xdt[:, h, :], E[:, h, :], start=True, stop=False, skip_group_check=bool(s))
                            if not s:
                                last = pe.matmul(o, stT[:, i * HD:(i + 1) * HD], Cw[:, h, :], start=False, stop=True)
                            else:
                                for b in range(STREAMS):
                                    last = pe.matmul(o[:, b * SLEN:(b + 1) * SLEN], stTb[:, b, i * HD:(i + 1) * HD],
                                                     Cw[:, h, b * SLEN:(b + 1) * SLEN],
                                                     start=False, stop=b == STREAMS - 1, skip_group_check=True)
                        last.then_inc(S["y"], 1)
                        if not s:
                            for g in range(2):
                                last = pe.matmul(bank(7)[g * 64:g * 64 + 64, :], Btok[:, g * NS:(g + 1) * NS],
                                                 xw[:, g * 8:g * 8 + 8, :].rearrange("p h c -> p (h c)"), start=True, stop=True)
                            last.then_inc(S["stadd"], 1)

                    with pe.Fori(0, 4) as t:
                        chunk(t, 0)
                    pe.wait_ge(S["st_in"], 16 * 16)
                    for b in range(STREAMS):
                        if b >= 2:
                            pe.wait_ge(S["st_copied"], b - 1)
                        else:
                            pe.wait_ge(S["Ea"], 4)
                        for j in range(4):
                            last = pe.transpose(bank(b % 2)[:, j * P:(j + 1) * P], stN[:, b * 4 + j, :], ident[:])
                        last.then_inc(S["st_turned"], 1)
                    pe.wait_ge(S["st_copied"], 8)
                    chunk(4, 1)
                    pe.wait_ge(S["dtax"], 1)
                    for i in range(8):
                        last = pe.matmul(bank(7)[:, i * 8:(i + 1) * 8], dtax[:, 2 * i:2 * i + 2, :].rearrange("p h c -> p (h c)"),
                                         stream_of[:], start=True, stop=True)
                    last.then_inc(S["dec"], 1)
                    pe.wait_ge(S["Bm"], 2)
                    pe.wait_ge(S["Ea"], 5)
                    for i in range(8):
                        if i >= 4:
                            pe.wait_ge(S["sadded"], i - 3)
                        pe.matmul(bank(i % 4), xw[:, 2 * i:2 * i + 2, :].rearrange("p h c -> p (h c)"), Bm[:, i // 4, :],
                                  start=True, stop=True).then_inc(S["sadd"], 1)
                    pe.wait_ge(S["ydone"], 5)
                    for j in range(4):
                        last = pe.transpose(misc[:, j * P:(j + 1) * P], stT[:, j * P:(j + 1) * P], ident[:])
                    last.then_inc(S["turned"], 1)

                @block.scalar
                def _(act):
                    def chunk(t):
                        act.wait_ge(S["sums"], t + 1)
                        act.wait_ge(S["state"], t + 1)
                        act.activation(ex, bank(7)[:, 0:48], ACT.Exp).then_inc(S["ex"], 1)
                        act.wait_ge(S["seg"], t + 1)
                        act.activation(E.rearrange("p h q -> p (h q)"), bank(0, 4), ACT.Exp).then_inc(S["E"], 1)
                        act.wait_ge(S["acb"], t + 1)
                        act.activation(Ea.rearrange("p h q -> p (h q)"), bank(0, 4), ACT.Exp).then_inc(S["Ea"], 1)

                    with act.Fori(0, 4) as t:
                        chunk(t)
                    for b in range(STREAMS):
                        act.wait_ge(S["st_turned"], b + 1)
                        act.activation(stTb[:, b, :], bank(b % 2), ACT.Copy).then_inc(S["st_copied"], 1)
                    chunk(4)
                    act.wait_ge(S["dec"], 1)
                    act.activation(spw[:, 0, 0:64], bank(7)[:, 0:64], ACT.Exp).then_inc(S["decE"], 1)
                    act.wait_ge(S["turned"], 1)
                    act.activation(E[:, 0:4, :].rearrange("p h q -> p (h q)"), misc, ACT.Copy).then_inc(S["stadd"], 1)

                @block.vector
                def _(dve):
                    st = Steps(dve, "ssd_step")

                    def chunk(t, s, st):
                        n0 = st.n
                        d = dta[:, ds(t, 1), :].rearrange("p o h -> p (o h)")
                        dtt = dt[:, ds(t, 1), :].rearrange("p o h -> p (o h)")
                        dve.tensor_tensor(mdta, upto[s][:].unsqueeze(1).to_broadcast([P, HEADS, P]), b16(d, P), ALU.mult)\
                           .then_inc(S["mdta"], 1)
                        dve.wait_ge(S["cb"], t + 1)
                        dve.tensor_copy(Btok, misc[:, 384:512]).then_inc(S["Btok"], 1)
                        st(dve.tensor_tensor(xdt, PX.rearrange("p (h c) -> p h c", h=HEADS), b16(dtt, HD), ALU.mult))
                        st.wait()
                        dve.wait_ge(S["ex"], t + 1)
                        dve.wait_ge(S["Btok"], t + 1)
                        dve.tensor_tensor(xw, xdt, b16(ex[:, 16:32], HD), ALU.mult).then_inc(S["xw"], 1)
                        st(dve.tensor_tensor(cbm, misc[:, 64:320].rearrange("p (g q) -> p g q", g=2),
                                             upto[s][:].unsqueeze(1).to_broadcast([P, 2, P]), ALU.mult))
                        st.wait()
                        dve.wait_ge(S["E"], t + 1)
                        v = E.rearrange("p (g h) q -> p g h q", g=2)
                        dve.tensor_tensor(v, v, cbm.unsqueeze(2).to_broadcast([P, 2, 8, P]), ALU.mult).then_inc(S["W"], 1)
                        dve.wait_ge(S["Ea"], t + 1)
                        for g in range(2):
                            r = slice(g * 64, g * 64 + 64)
                            ins = dve.tensor_tensor(Cw[r, g * 8:g * 8 + 8, :], Ea[r, g * 8:g * 8 + 8, :],
                                                    xc[r, 9, :].unsqueeze(1).to_broadcast([64, 8, P]), ALU.mult)
                            if g == 0:
                                st(ins)
                        st.wait()
                        ins.then_inc(S["Cw"], 1)
                        m = mdta.rearrange("p h q -> p (h q)")[:, 0:1024].rearrange("p (k q) -> p k q", k=KT)
                        st(dve.tensor_tensor(m, xc[:, 0:KT, :], b16(cols[:, DD:DD + KT], P), ALU.mult))
                        st.wait()
                        dve.wait_ge(S["y"], t + 1)
                        dve.tensor_tensor(ysT[:, :, ds(t * P, P)], Y.rearrange("p (k q) -> p k q", k=KT), m, ALU.add)\
                           .then_inc(S["ydone"], 1)
                        dve.wait_ge(S["ydone"], t + 1)
                        if not s:
                            for g in range(2):
                                r = slice(g * 64, g * 64 + 64)
                                v = stT[r, :].rearrange("p (h c) -> p h c", h=8)
                                st(dve.tensor_tensor(v, v, b16(ex[r, 32 + g * 8:40 + g * 8], HD), ALU.mult))
                            st.wait()
                            dve.wait_ge(S["stadd"], t + 1)
                            dve.tensor_tensor(stT[:], stT[:], bank(7), ALU.add).then_inc(S["state"], 1)
                            dve.wait_ge(S["state"], t + 2)
                        return st.n - n0

                    dve.memset(stT[:], 0.0).then_inc(S["state"], 1)
                    dve.wait_ge(S["state"], 1)
                    PER = 6
                    with dve.Fori(0, 4) as t:
                        used = chunk(t, 0, Steps(dve, "ssd_step", t * PER))
                        assert used == PER, used
                    st = Steps(dve, "ssd_step", 4 * PER)
                    chunk(4, 1, st)
                    dve.tensor_copy(dtax, b16(dta[:, 4, :], HD)).then_inc(S["dtax"], 1)
                    for g in range(2):
                        dve.tensor_tensor(Bm[:, g, :].rearrange("p (b n) -> p b n", b=STREAMS),
                                          Btok[:, g * NS:(g + 1) * NS].unsqueeze(1).to_broadcast([P, STREAMS, NS]),
                                          b16(stream_of[:], NS), ALU.mult).then_inc(S["Bm"], 1)
                    dve.wait_ge(S["decE"], 1)
                    v = stN.rearrange("p (b j) (g n) -> p b j g n", j=4, g=2)
                    for i in range(8):
                        g, j = divmod(i, 4)
                        st(dve.tensor_tensor(v[:, :, j, g, :], v[:, :, j, g, :], b16(spw[:, 0, i * 8:i * 8 + 8], NS), ALU.mult))
                    st.wait()
                    for i in range(8):
                        g, j = divmod(i, 4)
                        dve.wait_ge(S["sadd"], i + 1)
                        dve.tensor_tensor(v[:, :, j, g, :], v[:, :, j, g, :], bank(i % 4).rearrange("p (b n) -> p b n", b=STREAMS),
                                          ALU.add).then_inc(S["sadded"], 1)
                    dve.wait_ge(S["sadded"], 8)
            end_phase()

            with nc.Block() as block:
                wready = [phase_sem(f"weight_ready_{s}") for s in range(2)]
                done, gated, silued, squared, summed, rooted, ready = (phase_sem(n) for n in (
                    "projected", "gated", "silued", "squared", "summed", "rooted", "root_in"))
                sz = view(arenaX, 0, 2, TT)
                sq = view(arenaR, 2 * KT * TT, 2, TT)
                rs = arenaX[:, 2 * TT:3 * TT]

                @block.sync
                def _(sp):
                    sp.sem_inc(done, 2)
                    with sp.Fori(0, 4) as j:
                        for u in range(2):
                            sp.wait_ge(done, 2 * j + u + 1)
                            sp.dma_start(wt[:, u, :, :], weight("w_in", l, Z0 + j * (2 * P) + u * P)).then_inc(wready[u], 16)

                @block.tensor
                def _(pe):
                    def add_square(u, first, final):
                        for o, n in ((0, SEQ), (SEQ, TT - SEQ)):
                            last = pe.matmul(bank(4, 2)[:, o:o + n], ones[:], sq[:, u, o:o + n], start=first, stop=final)
                        return last

                    for o, n in ((0, SEQ), (SEQ, TT - SEQ)):
                        pe.matmul(bank(4, 2)[:, o:o + n], zeros[:], hT[:, 0, o:o + n], start=True, stop=False)
                    pe.sem_inc(silued, 2)
                    with pe.Fori(0, 4) as j:
                        for u in range(2):
                            pe.wait_ge(wready[u], j * 16 + 16)
                            pe.wait_ge(silued, 2 * j + u + 1)
                            project(u, hT, bank(2 * u, 2)).then_inc(done, 1)
                        for u in range(2):
                            pe.wait_ge(squared, 2 * j + u + 1)
                            add_square(u, False, False).then_inc(summed, 1)
                    for o, n in ((0, SEQ), (SEQ, TT - SEQ)):
                        last = pe.matmul(bank(4, 2)[:, o:o + n], zeros[:], hT[:, 0, o:o + n], start=False, stop=True)
                    last.then_inc(summed, 1)

                @block.scalar
                def _(act):
                    act.sem_inc(gated, 2)
                    act.sem_inc(summed, 2)
                    with act.Fori(0, 4) as j:
                        for u in range(2):
                            act.wait_ge(done, 2 + 2 * j + u + 1)
                            act.wait_ge(gated, 2 * j + u + 1)
                            act.activation(sz[:, u, :], bank(2 * u, 2)[:, 0:TT], ACT.Silu).then_inc(silued, 1)
                        for u in range(2):
                            act.wait_ge(gated, 2 + 2 * j + u + 1)
                            act.wait_ge(summed, 2 * j + u + 1)
                            act.activation(sq[:, u:u + 1, :], ysT[:, ds(2 * j + u, 1), :], ACT.Square).then_inc(squared, 1)
                    act.wait_ge(ready, 1)
                    act.activation(rs, rs, ACT.Sqrt).then_inc(rooted, 1)

                @block.vector
                def _(dve):
                    with dve.Fori(0, 4) as j:
                        for u in range(2):
                            dve.wait_ge(silued, 2 + 2 * j + u + 1)
                            y = ysT[:, ds(2 * j + u, 1), :]
                            dve.tensor_tensor(y, y, sz[:, u:u + 1, :], ALU.mult).then_inc(gated, 1)
                    dve.wait_ge(summed, 2 + 9)
                    dve.wait_ge(gated, 2 + 8)
                    dve.tensor_scalar(rs, bank(4, 2)[:, 0:TT], 1.0 / D, EPS, ALU.mult, ALU.add).then_inc(ready, 1)
                    dve.wait_ge(rooted, 1)
                    st = Steps(dve, "dve_step")
                    st(dve.reciprocal(rs, rs))
                    st.wait()
                    for k in range(KT):
                        st(dve.scalar_tensor_tensor(ysT[:, k, :], ysT[:, k, :], cols[:, NW + k:NW + k + 1], rs, ALU.mult, ALU.mult))
                    st.wait()
            end_phase()

            with nc.Block() as block:
                wready, gready = phase_sem("weight_ready_0"), phase_sem("gate_weights_ready")
                done, gates_done, evac, zeroed = (phase_sem(n) for n in ("projected", "gates_done", "ly_taken", "zeroed"))
                sg, th, gs, sgs, rt, q, fin = (phase_sem(n) for n in (
                    "sigmoids", "tanh", "gelu_in", "gelu_sig", "rooted", "root_in", "lru_done"))
                wbd = view(arenaW, 6 * D, 2, P)
                T = [arenaR[:, 2 * KT * TT + i * TT:2 * KT * TT + (i + 1) * TT] for i in range(6)]
                R, I, LY, G, Q4, AA = T
                UU, REC, HS = (arenaX[:, i * TT:(i + 1) * TT] for i in range(3))
                outrow = view(arenaW, 4096, D)

                @block.sync
                def _(sp):
                    sp.wait_ge(zeroed, 1)
                    sp.sem_inc(done, 1)
                    sp.sem_inc(gates_done, 1)
                    with sp.Fori(0, KT) as j:
                        sp.wait_ge(gates_done, j + 1)
                        for i, nm in enumerate(("lru_wa", "lru_wx")):
                            for h in range(2):
                                src = a[nm].rearrange("l n d e -> (l n d) e")[ds(l * D + j * P + h * 64, 64), :]
                                sp.dma_start(wbd[h * 64:h * 64 + 64, i, h * 64:h * 64 + 64], src).then_inc(gready, 16)
                        sp.wait_ge(done, j + 1)
                        sp.dma_start(wt[:, 0, :, :], weight("w_in", l, LY0 + j * P)).then_inc(wready, 16)
                    sp.wait_ge(phase_sem("lru_rows"), 1)
                    sp.dma_start(a["new_lru_prompt"].rearrange("l b c -> (l b) c")[ds(l, 1), :], outrow[0:1, :]).then_inc(phase_sem("out_written"), 16)
                    sp.dma_start(a["new_lru_sample"].rearrange("l b c -> (l b) c")[ds(l * 8, 8), :], outrow[1:9, :]).then_inc(phase_sem("out_written"), 16)
                    sp.wait_ge(phase_sem("out_written"), 32)

                @block.tensor
                def _(pe):
                    pe.sem_inc(sg, 2)
                    pe.sem_inc(evac, 1)
                    with pe.Fori(0, KT) as j:
                        pe.wait_ge(gready, j * 64 + 64)
                        pe.wait_ge(sg, 2 * j + 2)
                        for i in range(2):
                            for o, n in ((0, SEQ), (SEQ, TT - SEQ)):
                                last = pe.matmul(bank(2 * i, 2)[:, o:o + n], wbd[:, i, :],
                                                 lxT[:, ds(j, 1), o:o + n].rearrange("p o t -> p (o t)"), start=True, stop=True)
                        last.then_inc(gates_done, 1)
                        pe.wait_ge(wready, j * 16 + 16)
                        pe.wait_ge(evac, j + 1)
                        project(0, hT, bank(4, 2)).then_inc(done, 1)
                    pe.wait_ge(fin, KT)
                    for k in range(KT):
                        last = pe.transpose(bank(6, 2)[0:9, k * P:(k + 1) * P], lruN[:, k, :], ident[:])
                    last.then_inc(phase_sem("lru_turned"), 1)

                @block.scalar
                def _(act):
                    with act.Fori(0, KT) as j:
                        act.wait_ge(gates_done, 1 + j + 1)
                        act.wait_ge(fin, j)
                        act.activation(R, bank(0, 2)[:, 0:TT], ACT.Sigmoid, bias=cols[:, ds(BA + j, 1)]).then_inc(sg, 1)
                        act.activation(I, bank(2, 2)[:, 0:TT], ACT.Sigmoid, bias=cols[:, ds(BX + j, 1)]).then_inc(sg, 1)
                        act.wait_ge(sg, 2 + 2 * j + 1)
                        act.activation(R, R, ACT.Tanh, scale=lamS[:, ds(j, 1)]).then_inc(th, 1)
                        act.wait_ge(done, 1 + j + 1)
                        act.activation(LY, bank(4, 2)[:, 0:TT], ACT.Copy).then_inc(evac, 1)
                        act.wait_ge(gs, j + 1)
                        act.activation(G, G, ACT.Sigmoid, scale=1.5957691216057308).then_inc(sgs, 1)
                        act.wait_ge(q, j + 1)
                        act.activation(Q4, Q4, ACT.Sqrt).then_inc(rt, 1)
                    act.wait_ge(phase_sem("lru_turned"), 1)
                    act.activation(outrow[0:9, :], bank(6, 2)[0:9, :], ACT.Copy).then_inc(phase_sem("lru_rows"), 1)

                @block.vector
                def _(dve):
                    st = Steps(dve, "dve_step")
                    st(dve.memset(wbd, 0.0))
                    st.wait()
                    dve.sem_inc(zeroed, 1)
                    PER = 14
                    with dve.Fori(0, KT) as j:
                        st = Steps(dve, "lru_step", j * PER)
                        blk = lambda v: v.rearrange("p (b t) -> p b t", t=SLEN)
                        dve.wait_ge(th, j + 1)
                        st(dve.tensor_scalar(REC, R, -1.0, 1.0, ALU.mult, ALU.add))
                        st(dve.tensor_scalar(AA, R, -4.0, 1e-30, ALU.mult, ALU.max))
                        st.wait()
                        dve.tensor_copy(Q4, AA).then_inc(q, 1)
                        st(dve.reciprocal(REC, REC))
                        dve.wait_ge(evac, 1 + j + 1)
                        st(dve.tensor_tensor(G, LY, LY, ALU.mult))
                        st.wait()
                        st(dve.tensor_scalar(G, G, 0.044715, 1.0, ALU.mult, ALU.add))
                        dve.wait_ge(q, j + 1)
                        st(dve.scalar_tensor_tensor(AA, R, 1.0, REC, ALU.add, ALU.mult))
                        st.wait()
                        dve.tensor_tensor(G, G, LY, ALU.mult).then_inc(gs, 1)
                        dve.wait_ge(sg, 2 + 2 * j + 2)
                        st(dve.tensor_tensor(I, I, lxT[:, ds(j, 1), :].rearrange("p o t -> p (o t)"), ALU.mult))
                        st.wait()
                        st(dve.tensor_tensor(I, I, REC, ALU.mult))
                        st.wait()
                        dve.wait_ge(rt, j + 1)
                        st(dve.tensor_tensor(UU, I, Q4, ALU.mult))
                        h0 = cols[:, H0:CV].rearrange("p (b k) -> p b k", k=KT)[:, :, ds(j, 1)]
                        first = blk(AA)[:, 32:40, 0:1]
                        tmp = small[:, 0:8].unsqueeze(2)
                        st(dve.tensor_tensor(tmp, first, h0, ALU.mult))
                        st.wait()
                        st(dve.tensor_tensor(blk(UU)[:, 32:40, 0:1], blk(UU)[:, 32:40, 0:1], tmp, ALU.add))
                        st(dve.memset(first, 0.0))
                        st.wait()
                        st(dve.tensor_tensor_scan(HS, AA, UU, 0.0, ALU.mult, ALU.add))
                        dve.wait_ge(sgs, j + 1)
                        st.wait()
                        dve.tensor_copy(lruN[:, ds(j, 1), 1:9], blk(HS)[:, 32:40, SLEN - 1:SLEN].rearrange("p b o -> p o b"))\
                           .then_inc(phase_sem("last_taken"), 1)
                        dve.tensor_copy(lruN[:, ds(j, 1), 0:1], HS[:, SEQ - 1:SEQ].unsqueeze(1)).then_inc(phase_sem("last_taken"), 1)
                        st(dve.tensor_tensor(G, G, LY, ALU.mult))
                        st.wait()
                        dve.tensor_tensor(ylT[:, ds(j, 1), :], G.unsqueeze(1), HS.unsqueeze(1), ALU.mult)\
                           .then_inc(fin, 1)
                        assert st.n == PER, st.n
                        dve.wait_ge(fin, j + 1)
                        dve.wait_ge(phase_sem("last_taken"), 2 * j + 2)
            end_phase()

            with nc.Block() as block:
                wready = [phase_sem(f"weight_ready_{s}") for s in range(4)]
                done, sg, taken = phase_sem("projected"), phase_sem("sigmoids"), phase_sem("taken")
                G2 = view(arenaX, 0, 2, TT)
                M1 = arenaX[:, 2 * TT:3 * TT]
                srcs = ((("w_in", GS0), hT), (("w_br_ssd", 0), ysT), (("w_in", GL0), hT), (("w_br_lru", 0), ylT))

                @block.sync
                def _(sp):
                    sp.sem_inc(done, 4)
                    with sp.Fori(0, KT) as j:
                        for u, ((nm, c0), _) in enumerate(srcs):
                            sp.wait_ge(done, 4 * j + u + 1)
                            sp.dma_start(wt[:, u, :, :], weight(nm, l, c0 + j * P)).then_inc(wready[u], 16)

                @block.tensor
                def _(pe):
                    pe.sem_inc(sg, 2)
                    pe.sem_inc(taken, 2)
                    with pe.Fori(0, KT) as j:
                        for u, (_, src) in enumerate(srcs):
                            pe.wait_ge(wready[u], j * 16 + 16)
                            pe.wait_ge(taken if u % 2 else sg, 2 * j + u // 2 + 1)
                            project(u, src, bank(2 * u, 2)).then_inc(done, 1)

                @block.scalar
                def _(act):
                    with act.Fori(0, KT) as j:
                        for i in range(2):
                            act.wait_ge(done, 4 + 4 * j + 2 * i + 1)
                            act.wait_ge(taken, 2 * j + i + 1)
                            act.activation(G2[:, i, :], bank(4 * i, 2)[:, 0:TT], ACT.Sigmoid).then_inc(sg, 1)

                @block.vector
                def _(dve):
                    with dve.Fori(0, KT) as j:
                        m = mT[:, ds(j, 1), :].rearrange("p o t -> p (o t)")
                        dve.wait_ge(sg, 2 + 2 * j + 1)
                        dve.wait_ge(done, 4 + 4 * j + 2)
                        dve.tensor_tensor(M1, bank(2, 2)[:, 0:TT], G2[:, 0, :], ALU.mult).then_inc(taken, 1)
                        dve.wait_ge(sg, 2 + 2 * j + 2)
                        dve.wait_ge(done, 4 + 4 * j + 4)
                        dve.tensor_tensor(m, bank(6, 2)[:, 0:TT], G2[:, 1, :], ALU.mult).then_inc(taken, 1)
                        dve.wait_ge(taken, 2 + 2 * j + 2)
                        dve.tensor_tensor(m, m, M1, ALU.add).then_inc(phase_sem("merged"), 1)
                        dve.wait_ge(phase_sem("merged"), j + 1)
            end_phase()

            with nc.Block() as block:
                wready = [phase_sem(f"weight_ready_{s}") for s in range(2)]
                done, taken = phase_sem("projected"), phase_sem("taken")
                TMP = view(arenaX, 0, 2, TT)

                @block.sync
                def _(sp):
                    sp.sem_inc(done, 2)
                    with sp.Fori(0, 4) as j:
                        for u in range(2):
                            sp.wait_ge(done, 2 * j + u + 1)
                            sp.dma_start(wt[:, u, :, :], weight("w_out", l, j * (2 * P) + u * P)).then_inc(wready[u], 16)

                @block.tensor
                def _(pe):
                    pe.sem_inc(taken, 2)
                    with pe.Fori(0, 4) as j:
                        for u in range(2):
                            pe.wait_ge(wready[u], j * 16 + 16)
                            pe.wait_ge(taken, 2 * j + u + 1)
                            project(u, mT, bank(2 * u, 2)).then_inc(done, 1)

                @block.vector
                def _(dve):
                    blk = lambda v: v.rearrange("p (b t) -> p b t", t=SLEN)
                    with dve.Fori(0, 4) as j:
                        for u in range(2):
                            dve.wait_ge(done, 2 + 2 * j + u + 1)
                            g = modE[:, ds(2 * KT + 2 * j + u, 1), :].rearrange("p o b -> p (o b)")
                            x = xT[:, ds(2 * j + u, 1), :].rearrange("p o t -> p (o t)")
                            dve.tensor_tensor(blk(TMP[:, u, :]), blk(bank(2 * u, 2)[:, 0:TT]), b16(g), ALU.mult).then_inc(taken, 1)
                            dve.wait_ge(taken, 2 + 2 * j + u + 1)
                            dve.tensor_tensor(x, x, TMP[:, u, :], ALU.add).then_inc(phase_sem("added"), 1)
                    dve.wait_ge(phase_sem("added"), KT)
            end_phase()

            norm_phase(hT[:], modE[:, 4 * KT:5 * KT, :], modE[:, 3 * KT:4 * KT, :])

            qT = view(arenaQ, 0, 2 * PH, TT)
            with nc.Block() as block:
                wready = [phase_sem(f"weight_ready_{s}") for s in range(2)]
                done, taken = phase_sem("projected"), phase_sem("taken")

                @block.sync
                def _(sp):
                    sp.sem_inc(done, 2)
                    with sp.Fori(0, PH) as j:
                        for u in range(2):
                            sp.wait_ge(done, 2 * j + u + 1)
                            sp.dma_start(wt[:, u, :, :], weight("peer_wq", l, j * (2 * P) + u * P)).then_inc(wready[u], 16)

                @block.tensor
                def _(pe):
                    pe.sem_inc(taken, 2)
                    with pe.Fori(0, PH) as j:
                        for u in range(2):
                            pe.wait_ge(wready[u], j * 16 + 16)
                            pe.wait_ge(taken, 2 * j + u + 1)
                            project(u, hT, bank(2 * u, 2)).then_inc(done, 1)

                @block.scalar
                def _(act):
                    with act.Fori(0, PH) as j:
                        for u in range(2):
                            act.wait_ge(done, 2 + 2 * j + u + 1)
                            act.activation(qT[:, ds(2 * j + u, 1), :].rearrange("p o t -> p (o t)"), bank(2 * u, 2)[:, 0:TT], ACT.Copy)\
                               .then_inc(taken, 1)
            end_phase()

            ring = view(arenaR, 0, RING, D)
            diag = view(arenaW, 0, RING, P)
            qs = view(arenaW, 2048, 2 * PH, P)
            cand = view(arenaW, 2048, PH, TOPK * TOPK)
            hs = view(arenaW, 4096, KT, P)
            osb = arenaW[:, 4096:4096 + D]
            hrow = arenaW[:, 5120:6144]
            cut = view(arenaX, 0, 2 * PH, KEYS)
            ccut = view(arenaX, 0, PH, TOPK * TOPK)
            kT = view(arenaQ, 16 * TT + 1024, 2, P)
            ps_out, ps_sc, ps_t = bank(0, 2), bank(2, 4), bank(6, 2)
            free = [(arenaW, 6144, 8192), (arenaQ, 16 * TT, 16 * TT + 1024)]

            def tile_of(*shape):
                n = 1
                for x in shape:
                    n *= x
                for i, (ar, lo, hi) in enumerate(free):
                    if hi - lo >= n:
                        free[i] = (ar, lo + n, hi)
                        return view(ar, lo, *shape)
                raise ValueError("no room")

            val = tile_of(2 * PH, TOPK)
            key = tile_of(2 * PH, TOPK).bitcast(U32)
            keyf = tile_of(2 * PH, TOPK)
            eidx = tile_of(NT, PICKS).bitcast(U32)
            sval = tile_of(PH, TOPK)
            place = tile_of(PH, TOPK).bitcast(U32)
            parts = tile_of(2, PICKS).bitcast(U32)
            partf = tile_of(2, PICKS)
            gate = tile_of(PH, TOPK)
            hid = tile_of(PICKS)
            gel = tile_of(PICKS)
            wgt = tile_of(PICKS)
            slot_idx = small[:, 16:32].rearrange("p (h n) -> p h n", h=2).bitcast(U32)
            den = small[:, 32:40]
            row0 = small[:, 40:41]
            with nc.Block() as block:
                G = {n: phase_sem("peer_" + n) for n in (
                    "keys_in", "keys_turned", "keys", "q_staged", "h_staged", "h_turned", "h_rows", "scores", "idx",
                    "exp_in", "exp_out", "u_used", "v_used", "hid", "gelu", "wgt", "diag", "sum", "osb",
                    "o_turned", "resid", "slots", "row0")}

                @block.sync
                def _(sp):
                    for i, nm in enumerate(("peer_k1", "peer_k2")):
                        sp.dma_start(rowbuf[:, i, :], a[nm].rearrange("l k d -> (l k) d")[ds(l * KEYS, KEYS), :]).then_inc(G["keys_in"], 16)

                @block.gpsimd
                def _(pool):
                    pool.sem_inc(G["u_used"], RING)
                    pool.sem_inc(G["v_used"], RING)

                    def gather(t, which, table, mine, other, other_at):
                        with pool.Fori(0, PICKS // RING) as m:
                            for hf in range(2):
                                pool.wait_ge(mine, t * PICKS + m * RING + (hf + 1) * HALF)
                                hold(pool, other, other_at + (hf + 1) * HALF)
                                pool.tensor_copy(slot_idx[:, hf:hf + 1, :], eidx[:, ds(t, 1), ds(m * RING + hf * HALF, HALF)])\
                                    .then_inc(G["slots"], 1)
                                hold(pool, G["slots"], t * 32 + which * 16 + m * 2 + hf + 1)
                                for n in range(HALF):
                                    pool.indirect_dma_start(
                                        ring[:, hf * HALF + n, :], None, table,
                                        bass.IndirectOffsetOnAxis(ap=slot_idx[:, hf, n:n + 1], axis=0))\
                                        .then_inc(gathered[hf * HALF + n], 16)

                    with pool.Fori(0, NT) as t:
                        hold(pool, G["idx"], t + 1)
                        gather(t, 0, a["peer_u"].rearrange("l e d -> (l e) d"), G["u_used"], G["v_used"], t * PICKS)
                        gather(t, 1, a["peer_v"].rearrange("l e d -> (l e) d"), G["v_used"], G["u_used"], (t + 1) * PICKS)

                @block.tensor
                def _(pe):
                    pe.wait_ge(G["keys_in"], 32)
                    for i in range(2):
                        last = pe.transpose(ps_t[:, i * P:(i + 1) * P], rowbuf[:, i, :], ident[:])
                    last.then_inc(G["keys_turned"], 1)
                    pe.wait_ge(G["keys"], 1)

                    def score(t):
                        pe.wait_ge(G["q_staged"], t + 1)
                        for i in range(2 * PH):
                            last = pe.matmul(ps_sc[:, i * KEYS:(i + 1) * KEYS], qs[:, i, :], kT[:, i % 2, :], start=True, stop=True)
                        last.then_inc(G["scores"], 1)

                    def turn_h(t):
                        pe.wait_ge(G["h_staged"], t + 1)
                        for k in range(KT):
                            last = pe.transpose(ps_t[:, k * P:(k + 1) * P], hs[:, k, :], ident[:])
                        last.then_inc(G["h_turned"], 1)

                    def retrieve(t):
                        for c in range(2):
                            pe.matmul(ps_out[:, c * 512:(c + 1) * 512], zeros[:], hT[:, 0, 0:512], start=True, stop=False)
                        with pe.Fori(0, PICKS // RING) as m:
                            for n in range(RING):
                                pe.wait_ge(G["diag"], t * PICKS + m * RING + n + 1)
                                pe.wait_ge(gathered[n], l * (NT * 256) + t * 256 + 128 + m * 16 + 16)
                                for c in range(2):
                                    last = pe.matmul(ps_out[:, c * 512:(c + 1) * 512], diag[:, n, :],
                                                     ring[:, n, c * 512:(c + 1) * 512], start=False, stop=False)
                                last.then_inc(G["v_used"], 1)
                        for c in range(2):
                            last = pe.matmul(ps_out[:, c * 512:(c + 1) * 512], zeros[:], hT[:, 0, 0:512], start=False, stop=True)
                        last.then_inc(G["sum"], 1)
                        pe.wait_ge(G["osb"], t + 1)
                        for k in range(KT):
                            last = pe.transpose(ps_t[:, k * P:(k + 1) * P], osb[:, k * P:(k + 1) * P], ident[:])
                        last.then_inc(G["o_turned"], 1)

                    score(0)
                    turn_h(0)
                    with pe.Fori(0, NT - 1) as t:
                        score(t + 1)
                        retrieve(t)
                        pe.wait_ge(G["resid"], t + 1)
                        turn_h(t + 1)
                    retrieve(NT - 1)

                @block.scalar
                def _(act):
                    act.wait_ge(G["keys_turned"], 1)
                    act.activation(kT.rearrange("p i k -> p (i k)"), ps_t[:, 0:2 * P], ACT.Copy).then_inc(G["keys"], 1)

                    def stage_q(t):
                        act.activation(qs, qT[:, :, ds(t * P, P)], ACT.Copy).then_inc(G["q_staged"], 1)

                    def stage_h(t):
                        act.activation(hs, hT[:, :, ds(t * P, P)], ACT.Copy).then_inc(G["h_staged"], 1)
                        act.wait_ge(G["h_turned"], t + 1)
                        act.activation(hrow, ps_t, ACT.Copy).then_inc(G["h_rows"], 1)

                    def exponent(t):
                        act.wait_ge(G["exp_in"], t + 1)
                        act.activation(gate, gate, ACT.Exp).then_inc(G["exp_out"], 1)

                    def tile(t, more):
                        act.wait_ge(G["hid"], t + 1)
                        act.activation(gel, hid, ACT.Gelu_apprx_tanh).then_inc(G["gelu"], 1)
                        if more:
                            stage_q(t + 1)
                        act.wait_ge(G["wgt"], t + 1)
                        with act.Fori(0, PICKS // RING) as m:
                            for n in range(RING):
                                act.wait_ge(G["v_used"], t * PICKS + m * RING + n + 1)
                                act.activation(diag[:, n, :], ident[:], ACT.Copy, scale=wgt[:, ds(m * RING + n, 1)])\
                                   .then_inc(G["diag"], 1)
                        if more:
                            exponent(t + 1)
                        act.wait_ge(G["sum"], t + 1)
                        act.activation(osb, ps_out, ACT.Copy).then_inc(G["osb"], 1)
                        if more:
                            act.wait_ge(G["o_turned"], t + 1)
                            stage_h(t + 1)

                    stage_q(0)
                    stage_h(0)
                    exponent(0)
                    with act.Fori(0, NT - 1) as t:
                        tile(t, True)
                    tile(NT - 1, False)

                @block.vector
                def _(dve):
                    def top16(st, src, work, vals, places, n):
                        for i in range(n):
                            st(dve.max(vals[:, i, 0:8], src[:, i, :]))
                        st.hold()
                        for i in range(n):
                            st(dve.max_index(places[:, i, 0:8], vals[:, i, 0:8], src[:, i, :]))
                            st(dve.match_replace(work[:, i, :], vals[:, i, 0:8], src[:, i, :], NEG))
                        st.hold()
                        for i in range(n):
                            st(dve.max(vals[:, i, 8:16], work[:, i, :]))
                        st.hold()
                        for i in range(n):
                            st(dve.max_index(places[:, i, 8:16], vals[:, i, 8:16], work[:, i, :]))
                        st.hold()

                    def pick(t, st):
                        n0 = st.n
                        hold(dve, G["scores"], t + 1)
                        top16(st, ps_sc.rearrange("p (i k) -> p i k", k=KEYS), cut, val, key, 2 * PH)
                        st(dve.tensor_copy(keyf, key))
                        v4 = val.rearrange("p (h s) k -> p h s k", s=2)
                        k4 = keyf.rearrange("p (h s) k -> p h s k", s=2)
                        shape = [P, PH, TOPK, TOPK]
                        st(dve.tensor_tensor(cand.rearrange("p h (a b) -> p h a b", a=TOPK),
                                             v4[:, :, 0, :].unsqueeze(3).to_broadcast(shape),
                                             v4[:, :, 1, :].unsqueeze(2).to_broadcast(shape), ALU.add))
                        st.hold()
                        top16(st, cand, ccut, sval, place, PH)
                        dve.tensor_tensor(gate, sval, sval[:, :, 0:1].to_broadcast([P, PH, TOPK]), ALU.subtract)\
                           .then_inc(G["exp_in"], 1)
                        pl = place.rearrange("p h k -> p (h k)")
                        st(dve.tensor_scalar(parts[:, 0, :], pl, 4, None, ALU.logical_shift_right))
                        st(dve.tensor_scalar(parts[:, 1, :], pl, TOPK - 1, None, ALU.bitwise_and))
                        st.wait()
                        st(dve.tensor_copy(partf, parts))
                        st.wait()
                        eqs = (cand, ccut)
                        for s in range(2):
                            st(dve.tensor_tensor(eqs[s].rearrange("p h (k a) -> p (h k) a", a=TOPK),
                                                 partf[:, s, :].unsqueeze(2).to_broadcast([P, PICKS, TOPK]),
                                                 iota16[:].unsqueeze(1).to_broadcast([P, PICKS, TOPK]), ALU.is_equal))
                        st.wait()
                        for s in range(2):
                            e4 = eqs[s].rearrange("p h (k a) -> p h k a", a=TOPK)
                            st(dve.tensor_tensor(e4, e4, k4[:, :, s, :].unsqueeze(2).to_broadcast(shape), ALU.mult))
                        st.wait()
                        for s in range(2):
                            st(dve.tensor_reduce(partf[:, s, :], eqs[s].rearrange("p h (k a) -> p (h k) a", a=TOPK),
                                                 op=ALU.add, axis=AX.X))
                        st.wait()
                        st(dve.scalar_tensor_tensor(partf[:, 0, :], partf[:, 0, :], float(KEYS), partf[:, 1, :], ALU.mult, ALU.add))
                        st.wait()
                        dve.tensor_scalar(eidx[:, ds(t, 1), :], partf[:, 0:1, :], row0, None, ALU.add).then_inc(G["idx"], 1)
                        dve.wait_ge(G["exp_out"], t + 1)
                        st(dve.tensor_reduce(den, gate, op=ALU.add, axis=AX.X))
                        st.wait()
                        st(dve.reciprocal(den, den))
                        st.wait()
                        st(dve.tensor_tensor(gate, gate, b16(den, TOPK), ALU.mult))
                        st.wait()
                        assert st.n - n0 == PICK, st.n - n0

                    def tile(t, more):
                        st = Steps(dve, "peer_step", PICK + t * (PICK + KT))
                        hold(dve, G["h_rows"], t + 1)
                        with dve.Fori(0, PICKS // RING) as m:
                            for n in range(RING):
                                dve.wait_ge(gathered[n], l * (NT * 256) + t * 256 + m * 16 + 16)
                                dve.scalar_tensor_tensor(out=ring[:, n, :], in0=ring[:, n, :], scalar=1.0, in1=hrow, op0=ALU.mult,
                                                         op1=ALU.mult, accum_out=hid[:, ds(m * RING + n, 1)])\
                                   .then_inc(G["u_used"], 1)
                        dve.wait_ge(G["u_used"], t * PICKS + RING + PICKS)
                        dve.sem_inc(G["hid"], 1)
                        dve.wait_ge(G["gelu"], t + 1)
                        dve.tensor_tensor(wgt, gel, gate.rearrange("p h k -> p (h k)"), ALU.mult).then_inc(G["wgt"], 1)
                        dve.wait_ge(G["wgt"], t + 1)
                        if more:
                            pick(t + 1, st)
                        dve.wait_ge(G["o_turned"], t + 1)
                        tmp = arenaX[:, 0:D]
                        for k in range(KT):
                            blk = lambda v: v[:, k * P:(k + 1) * P].rearrange("p (b t) -> p b t", t=SLEN)
                            g = modE[:, 5 * KT + k:5 * KT + k + 1, ds(t * 8, 8)].rearrange("p o b -> p (o b)")
                            st(dve.tensor_tensor(blk(tmp), blk(ps_t), b16(g), ALU.mult))
                        st.wait()
                        x = xT[:, :, ds(t * P, P)]
                        dve.tensor_tensor(x, x, tmp.rearrange("p (k c) -> p k c", k=KT), ALU.add).then_inc(G["resid"], 1)
                        dve.wait_ge(G["resid"], t + 1)

                    PICK = 2 * PH * 5 + PH * 5 + 2 + 3 + 6 + 1 + 3
                    dve.tensor_copy(row0, layer_row[:, ds(l, 1)]).then_inc(G["row0"], 1)
                    dve.wait_ge(G["row0"], 1)
                    pick(0, Steps(dve, "peer_step"))
                    with dve.Fori(0, NT - 1) as t:
                        tile(t, True)
                    tile(NT - 1, False)
            end_phase()

        norm_phase(hT[:], cols[:, FIN:FIN + KT], None)
        yout = view(arenaR, 0, NT, D)
        with nc.Block() as block:
            turned, y_ready, out_sem = phase_sem("y_turned"), phase_sem("y_ready"), phase_sem("out_written")

            @block.tensor
            def _(pe):
                for t in range(NT):
                    if t >= 4:
                        pe.wait_ge(y_ready, t - 3)
                    for k in range(KT):
                        last = pe.transpose(bank(2 * (t % 4), 2)[:, k * P:(k + 1) * P], hT[:, k, t * P:(t + 1) * P], ident[:])
                    last.then_inc(turned, 1)

            @block.scalar
            def _(act):
                for t in range(NT):
                    act.wait_ge(turned, t + 1)
                    act.activation(yout[:, t, :], bank(2 * (t % 4), 2), ACT.Copy).then_inc(y_ready, 1)

            @block.sync
            def _(sp):
                sp.wait_ge(y_ready, 4)
                sp.dma_start(a["y_prompt"].rearrange("o (t p) d -> p (o t) d", p=P), yout[:, 0:4, :]).then_inc(out_sem, 16)
                sp.wait_ge(y_ready, 5)
                sp.dma_start(a["y_sample"].rearrange("b t d -> (b t) d"), yout[:, 4, :]).then_inc(out_sem, 16)
                sp.wait_ge(out_sem, 32)


_INS = ["x_prompt", "x_sample", "c_prompt", "c_sample", "state_ssd", "state_ssd_conv", "state_lru", "state_lru_conv",
        "ln1_w", "ln2_w", "w_mod", "b_mod", "w_in", "ssd_conv_w", "ssd_conv_b", "ssd_dt_bias", "ssd_a_log", "ssd_d",
        "ssd_norm_w", "lru_conv_w", "lru_conv_b", "lru_wa", "lru_ba", "lru_wx", "lru_bx", "lru_lambda", "w_br_ssd",
        "w_br_lru", "w_out", "peer_wq", "peer_k1", "peer_k2", "peer_u", "peer_v", "final_norm_w"]
_OUTS = [("y_prompt", (1, SEQ, D)), ("y_sample", (STREAMS, SLEN, D)),
         ("new_ssd_prompt", (DEPTH, 1, HEADS, HD, NS)), ("new_ssd_conv_prompt", (DEPTH, 1, HIST, CONVC)),
         ("new_lru_prompt", (DEPTH, 1, D)), ("new_lru_conv_prompt", (DEPTH, 1, HIST, D)),
         ("new_ssd_sample", (DEPTH, STREAMS, HEADS, HD, NS)), ("new_ssd_conv_sample", (DEPTH, STREAMS, HIST, CONVC)),
         ("new_lru_sample", (DEPTH, STREAMS, D)), ("new_lru_conv_sample", (DEPTH, STREAMS, HIST, D))]


def kernel(**inputs):
    import numpy as _np
    import concourse.bacc as _bacc
    from concourse.bass_utils import run_bass_kernel_spmd as _run

    nc = _bacc.Bacc("TRN2", target_bir_lowering=False, num_devices=1)
    arrays, args = {}, {}
    for name in _INS:
        x = _np.ascontiguousarray(inputs[name])
        arrays["in_" + name] = x
        args[name] = nc.dram_tensor("in_" + name, x.shape, F32, kind="ExternalInput").ap()
    for name, shape in _OUTS:
        args[name] = nc.dram_tensor("out_" + name, shape, F32, kind="ExternalOutput").ap()
    build(nc, args)
    r = _run(nc, [arrays], core_ids=[0])
    return tuple(r.results[0]["out_" + name] for name, _ in _OUTS)
```

```python
import concourse.bass as bass
from concourse import mybir
from contextlib import ExitStack

F32 = mybir.dt.float32
U32 = mybir.dt.uint32
ALU = mybir.AluOpType
ACT = mybir.ActivationFunctionType
AX = mybir.AxisListType
ds = bass.ds

DEPTH, D, P = 2, 1024, 128
KT = D // P
SEQ, STREAMS, SLEN = 512, 8, 16
TT = SEQ + STREAMS * SLEN
NT = TT // P
NB = TT // SLEN
HEADS, HD, NS = 16, 64, 64
CONVC = D + 4 * NS
W = 4
HIST = W - 1
EPS = 1e-6
PH, KEYS, TOPK = 8, 128, 16
PICKS = PH * TOPK
Z0, X0, DT0, LX0, LY0, GS0, GL0 = 0, D, D + CONVC, D + CONVC + HEADS, 2 * D + CONVC + HEADS, 3 * D + CONVC + HEADS, \
    4 * D + CONVC + HEADS
NEG = -3.0e38

SLOTS = 8
RING, HALF = 16, 8
BATCHES = PICKS // RING
SHARED = 3
SHARE = (BATCHES - SHARED) * RING // 4

LN1, LN2, NW, BA, BX, LAM, LCB, LCW, SCB = 0, 8, 16, 24, 32, 40, 48, 56, 88
ROWS_A = 98
SCW, BMOD, FIN, DD = ROWS_A, ROWS_A + 40, ROWS_A + 88, ROWS_A + 96
ROWS_B = 104
H0 = ROWS_A + ROWS_B
CV = H0 + 64
NCOLS = CV + 72


def build(nc, a):
    ctx = ExitStack()
    with ctx:
        def sb(name, shape, dt=F32):
            return ctx.enter_context(nc.sbuf_tensor(name, shape, dt))

        gathered = [ctx.enter_context(nc.semaphore(f"gathered_{n}")) for n in range(RING)]
        nums = []

        def sem(name):
            s = ctx.enter_context(nc.semaphore(name))
            nums.append(s.num)
            return s

        names = {}

        def phase_sem(name):
            if name not in names:
                names[name] = sem(name)
            return names[name]

        xT = sb("xT", [P, KT, TT])
        hT = sb("hT", [P, KT, TT])
        modE = sb("modE", [P, 6 * KT, NB])
        cols = sb("cols", [P, NCOLS])
        ident = sb("ident", [P, P])
        ones = sb("ones", [P, P])
        zeros = sb("zeros", [P, P])
        upto = [sb(f"upto{s}", [P, P]) for s in range(2)]
        after = [sb(f"after{s}", [P, P]) for s in range(2)]
        stream_of = sb("stream_of", [P, STREAMS])
        iota16 = sb("iota16", [P, TOPK])
        layer_row = sb("layer_row", [P, DEPTH])
        alog = sb("alog", [P, HEADS])
        dtb = sb("dtb", [P, HEADS])
        negA = sb("negA", [P, HEADS])
        dt = sb("dt", [P, NT, HEADS])
        dta = sb("dta", [P, NT, HEADS])
        spw = sb("spw", [P, 4, NT * HEADS])
        lamS = sb("lamS", [P, KT])
        stT = sb("stT", [P, 8 * HD])
        lruN = sb("lruN", [P, KT, 9])
        rowbuf = sb("rowbuf", [P, 2, P])
        small = sb("small", [P, 48])
        arenaR = sb("arenaR", [P, RING * D])
        arenaQ = sb("arenaQ", [P, 18 * TT])
        arenaW = sb("arenaW", [P, SLOTS * D])
        arenaX = sb("arenaX", [P, 2048])
        psum = ctx.enter_context(nc.psum_tensor("psum", [P, 8, 512], F32))

        def view(arena, at, *shape):
            n = 1
            for s in shape:
                n *= s
            v = arena[:, at:at + n]
            if len(shape) == 2:
                return v.rearrange("p (a b) -> p a b", a=shape[0])
            if len(shape) == 3:
                return v.rearrange("p (a b c) -> p a b c", a=shape[0], b=shape[1])
            return v

        wt = view(arenaW, 0, SLOTS, KT, P)
        ysT = view(arenaR, 0, KT, TT)
        ylT = view(arenaR, KT * TT, KT, TT)
        mT = view(arenaR, 2 * KT * TT, KT, TT)
        xbcT = view(arenaQ, 0, 10, TT)
        lxT = view(arenaQ, 10 * TT, KT, TT)

        def bank(b, n=1):
            return psum[:, b:b + n, :].rearrange("p b c -> p (b c)")

        def weight(name, l, col):
            w = a[name].rearrange("l (k p) c -> p (l k) c", p=P)
            return w[:, ds(l * KT, KT), ds(col, P)]

        def project(slot, src, out):
            for o, n in ((0, SEQ), (SEQ, TT - SEQ)):
                for k in range(KT):
                    last = nc.tensor.matmul(out[:, o:o + n], wt[:, slot, k, :], src[:, k, o:o + n],
                                            start=k == 0, stop=k == KT - 1)
            return last

        class Steps:

            def __init__(self, eng, name, base=0):
                self.eng, self.sem, self.base, self.n = eng, phase_sem(name), base, 0

            def __call__(self, ins):
                ins.then_inc(self.sem, 1)
                self.n += 1

            def wait(self, eng=None):
                (eng or self.eng).wait_ge(self.sem, self.base + self.n)

            def hold(self):
                hold(self.eng, self.sem, self.base + self.n)

        def hold(eng, s, value):
            eng.wait_ge(s, value)
            eng.sem_inc(phase_sem("held"), 1)

        def end_phase():
            nc.all_engine_barrier(sems_to_clear=range(min(nums), max(nums) + 1))

        def b16(ap, n=SLEN):
            return ap.unsqueeze(len(ap.shape)).to_broadcast([*ap.shape, n])

        def softplus(dve, st, ready, x, n, out, work):
            ax, z, z2, q = (work[:, i, 0:n] for i in range(4))
            st(dve.scalar_tensor_tensor(ax, x, -1.0, x, ALU.mult, ALU.min))
            st.wait()
            dve.sem_inc(ready[0], 1)
            dve.wait_ge(ready[1], 1)
            st(dve.tensor_scalar(z, ax, 2.0, None, ALU.add))
            st.wait()
            st(dve.reciprocal(z2, z))
            st.wait()
            st(dve.tensor_tensor(z, ax, z2, ALU.mult))
            st.wait()
            st(dve.tensor_tensor(z2, z, z, ALU.mult))
            st(dve.memset(q, 1.0 / 17))
            st.wait()
            first = True
            for c in (15, 13, 11, 9, 7, 5, 3):
                if first:
                    st(dve.tensor_tensor(q, q, z2, ALU.mult))
                    first = False
                    st.wait()
                st(dve.scalar_tensor_tensor(q, q, 1.0 / c, z2, ALU.add, ALU.mult))
                st.wait()
            st(dve.scalar_tensor_tensor(q, q, 1.0, z, ALU.add, ALU.mult))
            st(dve.tensor_scalar(z2, x, 0.0, None, ALU.max))
            st.wait()
            st(dve.scalar_tensor_tensor(out, q, 2.0, z2, ALU.mult, ALU.add))
            st.wait()

        xin = view(arenaR, 0, NT, D)
        x_loaded, s_const, xt_done, x_copied = (sem(n) for n in ("x_loaded", "s_const", "xt_done", "x_copied"))
        with nc.Block() as block:
            @block.sync
            def _(sp):
                sp.dma_start(xin[:, 0:4, :], a["x_prompt"].rearrange("o (t p) d -> p (o t) d", p=P)).then_inc(x_loaded, 16)
                sp.dma_start(xin[:, 4, :], a["x_sample"].rearrange("b t d -> (b t) d")).then_inc(x_loaded, 16)

            @block.gpsimd
            def _(pool):
                n = 0

                def put(ins):
                    nonlocal n
                    ins.then_inc(s_const, 1)
                    n += 1

                put(pool.memset(ident[:], 1.0))
                put(pool.memset(ones[:], 1.0))
                put(pool.memset(zeros[:], 0.0))
                put(pool.memset(stream_of[:], 1.0))
                put(pool.iota(iota16[:], [[1, TOPK]], base=0, channel_multiplier=0, allow_small_or_imprecise_dtypes=True))
                put(pool.iota(layer_row[:], [[KEYS * KEYS, DEPTH]], base=0, channel_multiplier=0, allow_small_or_imprecise_dtypes=True))
                pool.wait_ge(s_const, n)
                put(pool.affine_select(out=ident[:], in_=ident[:], compare_op=ALU.is_equal, fill=0.0, base=0,
                                       pattern=[[-1, P]], channel_multiplier=1))
                for s in range(2):
                    put(pool.affine_select(out=upto[s][:], in_=ones[:], compare_op=ALU.is_ge, fill=0.0, base=0,
                                           pattern=[[1, P]], channel_multiplier=-1))
                    put(pool.affine_select(out=after[s][:], in_=ones[:], compare_op=ALU.is_ge, fill=0.0, base=-1,
                                           pattern=[[-1, P]], channel_multiplier=1))
                put(pool.affine_select(out=stream_of[:], in_=stream_of[:], compare_op=ALU.is_ge, fill=0.0, base=0,
                                       pattern=[[-SLEN, STREAMS]], channel_multiplier=1))
                pool.wait_ge(s_const, n)
                put(pool.affine_select(out=stream_of[:], in_=stream_of[:], compare_op=ALU.is_ge, fill=0.0,
                                       base=SLEN - 1, pattern=[[SLEN, STREAMS]], channel_multiplier=-1))
                put(pool.affine_select(out=upto[1][:], in_=upto[1][:], compare_op=ALU.is_ge, fill=0.0, base=0,
                                       pattern=[[-SLEN, STREAMS], [0, SLEN]], channel_multiplier=1))
                put(pool.affine_select(out=after[1][:], in_=after[1][:], compare_op=ALU.is_ge, fill=0.0,
                                       base=SLEN - 1, pattern=[[SLEN, STREAMS], [0, SLEN]], channel_multiplier=-1))
                pool.wait_ge(s_const, n)

            @block.tensor
            def _(pe):
                pe.wait_ge(x_loaded, 32)
                pe.wait_ge(s_const, 15)
                for t in range(NT):
                    if t >= 4:
                        pe.wait_ge(x_copied, t - 3)
                    o = bank(2 * (t % 4), 2)
                    for k in range(KT):
                        last = pe.transpose(o[:, k * P:(k + 1) * P], xin[:, t, k * P:(k + 1) * P], ident[:])
                    last.then_inc(xt_done, 1)

            @block.vector
            def _(dve):
                for t in range(NT):
                    dve.wait_ge(xt_done, t + 1)
                    dve.tensor_copy(xT[:, :, t * P:(t + 1) * P],
                                    bank(2 * (t % 4), 2).rearrange("p (k c) -> p k c", k=KT)).then_inc(x_copied, 1)
                dve.wait_ge(x_copied, NT)
        end_phase()

        def norm_phase(out, scale, shift):
            sq = view(arenaW, 0, KT, TT)
            rs = arenaX[:, 0:TT]
            with nc.Block() as block:
                squared, summed, rooted, ready, scaled, modulated = (phase_sem(n) for n in (
                    "squared", "summed", "rooted", "root_in", "scaled", "modulated"))

                @block.scalar
                def _(act):
                    for k in range(KT):
                        act.activation(sq[:, k, :], xT[:, k, :], ACT.Square).then_inc(squared, 1)
                    act.wait_ge(ready, 1)
                    act.activation(rs, rs, ACT.Sqrt).then_inc(rooted, 1)
                    for k in range(KT):
                        act.wait_ge(scaled, k + 1)
                        if shift is None:
                            v = out[:, k, :]
                            ins = act.activation(v, v, ACT.Copy, scale=scale[:, k:k + 1])
                        else:
                            v = out[:, k, 0:SEQ]
                            ins = act.activation(v, v, ACT.Identity, scale=scale[:, k, 0:1], bias=shift[:, k, 0:1])
                        ins.then_inc(modulated, 1)

                @block.tensor
                def _(pe):
                    o = bank(0, 2)
                    for k in range(KT):
                        pe.wait_ge(squared, k + 1)
                        for at, n in ((0, SEQ), (SEQ, TT - SEQ)):
                            last = pe.matmul(o[:, at:at + n], ones[:], sq[:, k, at:at + n], start=k == 0,
                                             stop=k == KT - 1)
                    last.then_inc(summed, 1)

                @block.vector
                def _(dve):
                    st = Steps(dve, "dve_step")
                    dve.wait_ge(summed, 1)
                    dve.tensor_scalar(rs, bank(0, 2)[:, 0:TT], 1.0 / D, EPS, ALU.mult, ALU.add).then_inc(ready, 1)
                    dve.wait_ge(rooted, 1)
                    st(dve.reciprocal(rs, rs))
                    st.wait()
                    for k in range(KT):
                        dve.tensor_tensor(out[:, k, :], xT[:, k, :], rs, ALU.mult).then_inc(scaled, 1)
                    if shift is not None:
                        dve.wait_ge(scaled, KT)
                        v = out[:, :, SEQ:TT].rearrange("p k (b t) -> p k b t", t=SLEN)
                        st(dve.tensor_tensor(v, v, b16(scale[:, :, 32:40]), ALU.mult))
                        st.wait()
                        st(dve.tensor_tensor(v, v, b16(shift[:, :, 32:40]), ALU.add))
                        st.wait()
            end_phase()

        with nc.Fori(0, DEPTH) as l:
            with nc.Block() as block:
                d2 = small[96:104, 0:2]
                rowsD = arenaX[:, 0:P]
                rowsC = arenaX[:, P:2 * P]
                loaded, d_spread, silued, turned, colsd = (phase_sem(n) for n in (
                    "vectors_loaded", "d_spread", "c_silued", "vectors_turned", "vectors_ready"))
                slab = view(arenaR, 0, 2, 6 * D)
                wready = [phase_sem(f"weight_ready_{s}") for s in range(2)]
                wused, mod_sum, mod_done = phase_sem("weight_used"), phase_sem("mod_sum"), phase_sem("mod_done")
                ex_in, ex_out = phase_sem("exp_in"), phase_sem("exp_out")

                def rows(name, n, spec="l (k c) -> (l k) c"):
                    return a[name].rearrange(spec, c=P)[ds(l * n, n), :]

                @block.sync
                def _(sp):
                    for r, at, src in (
                        (0, LN1, rows("ln1_w", 8)), (0, LN2, rows("ln2_w", 8)), (0, NW, rows("ssd_norm_w", 8)),
                        (0, BA, rows("lru_ba", 8)), (0, BX, rows("lru_bx", 8)), (0, LAM, rows("lru_lambda", 8)),
                        (0, LCB, rows("lru_conv_b", 8)), (0, LCW, rows("lru_conv_w", 32, "l w (k c) -> (l w k) c")),
                        (0, SCB, rows("ssd_conv_b", 10)), (1, 0, rows("ssd_conv_w", 40, "l w (k c) -> (l w k) c")),
                        (1, 40, rows("b_mod", 48)),
                        (1, 88, a["final_norm_w"].rearrange("(k c) -> k c", c=P)),
                    ):
                        sp.dma_start(rowbuf[at:at + src.shape[0], r, :], src).then_inc(loaded, 16)
                    sp.dma_start(rowsC[0:64, :], rows("state_lru", 64, "l b (k c) -> (l b k) c")).then_inc(loaded, 16)
                    sp.dma_start(rowsD[0:8, :], a["c_prompt"].rearrange("s (k c) -> (s k) c", c=P)).then_inc(loaded, 16)
                    sp.dma_start(rowsD[8:72, :], a["c_sample"].rearrange("s (k c) -> (s k) c", c=P)).then_inc(loaded, 16)
                    sp.dma_start(d2, a["ssd_d"].rearrange("l (j h) -> (l j) h", h=2)[ds(l * 8, 8), :]).then_inc(loaded, 16)
                    sp.dma_start(alog[:], a["ssd_a_log"][ds(l, 1), :].to_broadcast([P, HEADS])).then_inc(loaded, 16)
                    sp.dma_start(dtb[:], a["ssd_dt_bias"][ds(l, 1), :].to_broadcast([P, HEADS])).then_inc(loaded, 16)
                    sp.sem_inc(wused, 2)
                    with sp.Fori(0, KT // 2) as j:
                        for u in range(2):
                            sp.wait_ge(wused, 2 * j + u + 1)
                            sp.dma_start(slab[:, u, :], a["w_mod"].rearrange("l r c -> (l r) c")
                                         [ds(l * D + j * (2 * P) + u * P, P), :]).then_inc(wready[u], 16)

                @block.scalar
                def _(act):
                    act.wait_ge(loaded, 18 * 16)
                    act.activation(rowsD[0:72, :], rowsD[0:72, :], ACT.Silu).then_inc(silued, 1)
                    act.activation(negA[:], alog[:], ACT.Exp).then_inc(silued, 1)
                    act.wait_ge(ex_in, 1)
                    act.activation(spw[:, 0, 0:KT], spw[:, 0, 0:KT], ACT.Exp).then_inc(ex_out, 1)

                @block.tensor
                def _(pe):
                    pe.wait_ge(loaded, 18 * 16)
                    pe.wait_ge(silued, 1)
                    pe.wait_ge(d_spread, 1)
                    pe.transpose(bank(7)[:, 0:ROWS_A], rowbuf[0:ROWS_A, 0, :], ident[0:ROWS_A, 0:ROWS_A])
                    pe.transpose(bank(7)[:, ROWS_A:H0], rowbuf[0:ROWS_B, 1, :], ident[0:ROWS_B, 0:ROWS_B])
                    pe.transpose(bank(7)[:, H0:CV], rowsC[0:64, :], ident[0:64, 0:64])
                    pe.transpose(bank(7)[:, CV:NCOLS], rowsD[0:72, :], ident[0:72, 0:72]).then_inc(turned, 1)
                    pe.wait_ge(colsd, 1)
                    cT = cols[:, CV:NCOLS].rearrange("p (s k) -> p k s", k=KT)
                    mod_ps = bank(0)[:, 0:6 * KT * 9]
                    pe.matmul(mod_ps, zeros[:], xT[:, 0, 0:6 * KT * 9], start=True, stop=False)
                    with pe.Fori(0, KT // 2) as j:
                        for u in range(2):
                            pe.wait_ge(wready[u], j * 16 + 16)
                            for c in range(6 * KT):
                                last = pe.matmul(mod_ps[:, c * 9:c * 9 + 9], slab[:, u, c * P:(c + 1) * P],
                                                 cT[:, ds(2 * j + u, 1), :].rearrange("p o s -> p (o s)"), start=False, stop=False)
                            last.then_inc(wused, 1)
                    pe.matmul(mod_ps, zeros[:], xT[:, 0, 0:6 * KT * 9], start=False, stop=True).then_inc(mod_sum, 1)

                @block.vector
                def _(dve):
                    st = Steps(dve, "dve_step")
                    dve.wait_ge(loaded, 18 * 16)
                    dve.tensor_copy(rowbuf[96:104, 1, :].rearrange("p (h c) -> p h c", h=2), b16(d2, HD)).then_inc(d_spread, 1)
                    dve.wait_ge(turned, 1)
                    dve.tensor_copy(cols[:], bank(7)[:, 0:NCOLS]).then_inc(colsd, 1)
                    dve.wait_ge(silued, 2)
                    st(dve.tensor_scalar(negA[:], negA[:], -1.0, None, ALU.mult))
                    dve.wait_ge(colsd, 1)
                    lam = spw[:, 0, 16:16 + KT]
                    st(dve.tensor_scalar(lam, cols[:, LAM:LAM + KT], -1.0, None, ALU.mult))
                    st.wait()
                    softplus(dve, st, (ex_in, ex_out), lam, KT, lamS[:], spw)
                    st(dve.tensor_scalar(lamS[:], lamS[:], -4.0, None, ALU.mult))
                    dve.wait_ge(mod_sum, 1)
                    src = bank(0)[:, 0:6 * KT * 9].rearrange("p (c s) -> p c s", s=9)
                    bias = cols[:, BMOD:BMOD + 6 * KT].unsqueeze(2)
                    for lo, hi, v in ((0, 32, src[:, :, 0:1].to_broadcast([P, 6 * KT, 32])), (32, 40, src[:, :, 1:9])):
                        dve.tensor_tensor(modE[:, :, lo:hi], v, bias.to_broadcast([P, 6 * KT, hi - lo]), ALU.add)\
                           .then_inc(mod_done, 1)
                    dve.wait_ge(mod_done, 2)
                    for at, ln in ((KT, LN1), (4 * KT, LN2)):
                        v = modE[:, at:at + KT, :]
                        st(dve.scalar_tensor_tensor(v, v, 1.0, cols[:, ln:ln + KT].unsqueeze(2).to_broadcast([P, KT, NB]),
                                                    ALU.add, ALU.mult))
                    st.wait()
            end_phase()

            norm_phase(hT[:], modE[:, KT:2 * KT, :], modE[:, 0:KT, :])

            def conv_phase(col0, tiles, dst, wcol, bcol, state, C, new_p, new_s, silu, with_dt):
                PADC = HIST + SEQ + STREAMS * (HIST + SLEN)
                xpad = view(arenaR, 0, 2, PADC + 1)
                acc = view(arenaR, 2 * (PADC + 1), 2, PADC + 1)
                pre = view(arenaR, 4 * (PADC + 1), 2, TT)
                hist = view(arenaR, 4 * (PADC + 1) + 2 * TT, 2, P)
                last27 = view(arenaR, 4 * (PADC + 1) + 2 * TT + 2 * P, 2, 27)
                newrow = view(arenaR, 8192, C)
                wdt = view(arenaR, 12288, KT, HEADS)
                sample = lambda v: v[:, HIST + SEQ:PADC].rearrange("p (b t) -> p b t", b=STREAMS)
                loops = tiles // 2
                NY = PADC - HIST
                with nc.Block() as block:
                    wready = [phase_sem(f"weight_ready_{s}") for s in range(2)]
                    hready = [phase_sem(f"history_ready_{s}") for s in range(2)]
                    proj_done, hist_done, padded, tails, tails_done, stored = (phase_sem(n) for n in (
                        "projected", "history_turned", "padded", "tails", "tails_turned", "tails_stored"))
                    conved, silued, wdt_ready, dt_done, zeroed = (phase_sem(n) for n in (
                        "convolved", "silued", "wdt_ready", "dt_projected", "zeroed"))
                    ex_in, ex_out, out_sem = phase_sem("exp_in"), phase_sem("exp_out"), phase_sem("out_written")

                    @block.sync
                    def _(sp):
                        if with_dt:
                            sp.dma_start(wdt, a["w_in"].rearrange("l (k p) c -> p (l k) c", p=P)[:, ds(l * KT, KT), DT0:DT0 + HEADS])\
                              .then_inc(wdt_ready, 16)
                        sp.sem_inc(proj_done, 2)
                        sp.sem_inc(hist_done, 2)
                        with sp.Fori(0, loops) as j:
                            for u in range(2):
                                sp.wait_ge(proj_done, 2 * j + u + 1)
                                sp.dma_start(wt[:, u, :, :], weight("w_in", l, col0 + j * (2 * P) + u * P)).then_inc(wready[u], 16)
                                sp.wait_ge(hist_done, 2 * j + u + 1)
                                sp.dma_start(hist[0:24, u, :], state.rearrange("l b w c -> (l b w) c")
                                             [ds(l * 24, 24), ds(j * (2 * P) + u * P, P)]).then_inc(hready[u], 16)
                        sp.wait_ge(stored, 2 + tiles)
                        sp.dma_start(new_p.rearrange("l b w c -> (l b w) c")[ds(l * 3, 3), :], newrow[0:3, :]).then_inc(out_sem, 16)
                        sp.dma_start(new_s.rearrange("l b w c -> (l b w) c")[ds(l * 24, 24), :], newrow[3:27, :]).then_inc(out_sem, 16)
                        sp.wait_ge(out_sem, 32)

                    @block.tensor
                    def _(pe):
                        if with_dt:
                            pe.wait_ge(wdt_ready, 16)
                            for t in range(NT):
                                for k in range(KT):
                                    last = pe.matmul(bank(7)[:, t * HEADS:(t + 1) * HEADS], hT[:, k, t * P:(t + 1) * P],
                                                     wdt[:, k, :], start=k == 0, stop=k == KT - 1)
                            last.then_inc(dt_done, 1)
                        pe.sem_inc(padded, 2)
                        pe.sem_inc(stored, 2)
                        with pe.Fori(0, loops) as j:
                            for u in range(2):
                                pe.wait_ge(wready[u], j * 16 + 16)
                                pe.wait_ge(padded, 2 * j + u + 1)
                                project(u, hT, bank(2 * u, 2)).then_inc(proj_done, 1)
                                hold(pe, hready[u], j * 16 + 16)
                                pe.transpose(bank(2 * u, 2)[:, TT:TT + 24], hist[0:24, u, :], ident[0:24, 0:24])\
                                  .then_inc(hist_done, 1)
                            for u in range(2):
                                pe.wait_ge(tails, 2 * j + u + 1)
                                pe.wait_ge(stored, 2 * j + u + 1)
                                pe.transpose(bank(5 + u)[0:27, 0:P], last27[:, u, :], ident[:]).then_inc(tails_done, 1)

                    @block.scalar
                    def _(act):
                        if with_dt:
                            act.wait_ge(ex_in, 1)
                            act.activation(spw[:, 0, :], spw[:, 0, :], ACT.Exp).then_inc(ex_out, 1)
                        act.sem_inc(conved, 2)
                        act.wait_ge(zeroed, 1)
                        filled = phase_sem("filled")
                        with act.Fori(0, loops) as j:
                            for u in range(2):
                                act.wait_ge(hist_done, 2 + 2 * j + u + 1)
                                act.wait_ge(conved, 2 * j + u + 1)
                                o = bank(2 * u, 2)
                                act.activation(xpad[:, u, HIST:HIST + SEQ], o[:, 0:SEQ], ACT.Copy).then_inc(filled, 1)
                                act.activation(sample(xpad[:, u, :])[:, :, 0:HIST],
                                               o[:, TT:TT + 24].rearrange("p (b t) -> p b t", b=STREAMS),
                                               ACT.Copy).then_inc(filled, 1)
                                act.activation(sample(xpad[:, u, :])[:, :, HIST:], o[:, SEQ:TT].rearrange("p (b t) -> p b t", b=STREAMS),
                                               ACT.Copy).then_inc(padded, 1)
                            for u in range(2):
                                act.wait_ge(tails_done, 2 * j + u + 1)
                                act.activation(newrow[0:27, ds(j * (2 * P) + u * P, P)], bank(5 + u)[0:27, 0:P], ACT.Copy)\
                                   .then_inc(stored, 1)
                                if silu:
                                    act.wait_ge(conved, 2 + 2 * j + u + 1)
                                    act.activation(dst[:, ds(2 * j + u, 1), :], pre[:, u:u + 1, :], ACT.Silu).then_inc(silued, 1)
                        if silu:
                            act.wait_ge(silued, 2 + tiles)

                    @block.vector
                    def _(dve):
                        st = Steps(dve, "dve_step")
                        for u in range(2):
                            st(dve.memset(xpad[:, u, 0:HIST], 0.0))
                        st.wait()
                        dve.sem_inc(zeroed, 1)
                        if with_dt:
                            dve.wait_ge(dt_done, 1)
                            v = dt[:].rearrange("p t h -> p (t h)")
                            st(dve.tensor_tensor(dt[:], bank(7)[:, 0:NT * HEADS].rearrange("p (t h) -> p t h", t=NT),
                                                 dtb[:].unsqueeze(1).to_broadcast([P, NT, HEADS]), ALU.add))
                            st.wait()
                            softplus(dve, st, (ex_in, ex_out), v, NT * HEADS, v, spw)
                            st(dve.tensor_tensor(dta[:], dt[:], negA[:].unsqueeze(1).to_broadcast([P, NT, HEADS]), ALU.mult))
                        filled = phase_sem("filled")
                        if silu:
                            dve.sem_inc(silued, 2)
                        PER = 10
                        with dve.Fori(0, loops) as j:
                            st = Steps(dve, "conv_step", j * PER)
                            for u in range(2):
                                dve.wait_ge(filled, 4 * j + 2 * u + 2)
                                dve.wait_ge(padded, 2 + 2 * j + u + 1)
                                x, y = xpad[:, u, :], acc[:, u, 0:NY]
                                st(dve.tensor_copy(last27[:, u, 0:3], x[:, SEQ:SEQ + HIST]))
                                dve.tensor_copy(last27[:, u, 3:27].rearrange("p (b t) -> p b t", b=STREAMS),
                                                sample(x)[:, :, SLEN:]).then_inc(tails, 1)
                                dve.wait_ge(tails, 2 * j + u + 1)
                                w = lambda k: cols[:, ds(wcol + k * tiles + 2 * j + u, 1)]
                                st(dve.tensor_scalar(y, x[:, 0:NY], w(0), cols[:, ds(bcol + 2 * j + u, 1)], ALU.mult, ALU.add))
                                st.wait()
                                for k in (1, 2):
                                    st(dve.scalar_tensor_tensor(y, x[:, k:k + NY], w(k), y, ALU.mult, ALU.add))
                                    st.wait()
                                if silu:
                                    dve.wait_ge(silued, 2 * j + u + 1)
                                    to = pre[:, u, :]
                                else:
                                    to = dst[:, ds(2 * j + u, 1), :].rearrange("p o t -> p (o t)")
                                st(dve.scalar_tensor_tensor(to[:, 0:SEQ], x[:, HIST:HIST + SEQ], w(3), y[:, 0:SEQ], ALU.mult, ALU.add))
                                ysam = acc[:, u, HIST + SEQ:HIST + SEQ + STREAMS * (HIST + SLEN)].rearrange("p (b t) -> p b t", b=STREAMS)
                                dve.scalar_tensor_tensor(to[:, SEQ:TT].rearrange("p (b t) -> p b t", b=STREAMS),
                                                         sample(x)[:, :, HIST:], w(3), ysam[:, :, 0:SLEN],
                                                         ALU.mult, ALU.add).then_inc(conved, 1)
                            assert st.n == PER, st.n
                        dve.wait_ge(conved, 2 + tiles)
                        dve.wait_ge(phase_sem("conv_step"), loops * PER)
                end_phase()

            conv_phase(X0, 10, xbcT, SCW, SCB, a["state_ssd_conv"], CONVC, a["new_ssd_conv_prompt"],
                       a["new_ssd_conv_sample"], True, True)
            conv_phase(LX0, 8, lxT, LCW, LCB, a["state_lru_conv"], D, a["new_lru_conv_prompt"],
                       a["new_lru_conv_sample"], False, False)

            at = KT * TT
            parts = {}
            for name, n in (("xc", 10 * P), ("mdta", 2048), ("E", 2048), ("Ea", 2048), ("Cw", 2048),
                            ("xw", 1024), ("cbm", 256), ("Btok", P)):
                parts[name] = (at, n)
                at += n
            assert at <= RING * D
            V = lambda n, *s: view(arenaR, parts[n][0], *s)
            xc, mdta, E, Ea = V("xc", 10, P), V("mdta", HEADS, P), V("E", HEADS, P), V("Ea", HEADS, P)
            Cw, xw, cbm, Btok = V("Cw", HEADS, P), V("xw", HEADS, HD), V("cbm", 2, P), V("Btok", P)
            xdt = view(arenaX, 0, HEADS, HD)
            Cz = view(arenaX, 1024, 2, P)
            stN = view(arenaW, 0, STREAMS * 4, P)
            stTb = view(arenaW, 4096, STREAMS, 4 * P)
            Bm = view(arenaX, 0, 2, STREAMS * NS)
            dtax = view(arenaX, 1024, HEADS, HD)
            ex = small[:, 0:48]
            with nc.Block() as block:
                S = {n: phase_sem("ssd_" + n) for n in (
                    "staged", "turned", "sums", "cb", "mdta", "seg", "E", "acb", "Ea", "ex", "xdt", "xw", "cbm", "W",
                    "Cw", "y", "stadd", "ydone", "state", "Btok", "st_in", "st_turned", "st_copied", "dtax", "dec",
                    "decE", "Bm", "cz", "zeroed", "sadd", "sadded", "outw", "free")}
                misc = bank(6)
                PX = bank(4, 2)
                Y = bank(4, 2)

                def state_view(name):
                    return a[name].rearrange("l b (j hh) p n -> (hh p) (l b j) n", hh=2)

                @block.sync
                def _(sp):
                    v = stN.rearrange("p (b j) (g n) -> p b j g n", j=4, g=2)
                    src = state_view("state_ssd")
                    for b in range(STREAMS):
                        for g in range(2):
                            sp.dma_start(v[:, b, :, g, :], src[:, ds(l * 64 + b * 8 + g * 4, 4), :]).then_inc(S["st_in"], 16)
                    sp.wait_ge(S["sadded"], 8)
                    dst = state_view("new_ssd_sample")
                    for b in range(STREAMS):
                        for g in range(2):
                            sp.dma_start(dst[:, ds(l * 64 + b * 8 + g * 4, 4), :], v[:, b, :, g, :]).then_inc(S["outw"], 16)
                    sp.wait_ge(S["stadd"], 5)
                    pv = E[:, 0:4, :].rearrange("p j (g n) -> p j g n", g=2)
                    dp = a["new_ssd_prompt"].rearrange("l b (j hh) p n -> (hh p) (l b j) n", hh=2)
                    for g in range(2):
                        sp.dma_start(dp[:, ds(l * 8 + g * 4, 4), :], pv[:, :, g, :]).then_inc(S["outw"], 16)
                    sp.wait_ge(S["outw"], 18 * 16)

                @block.gpsimd
                def _(pool):
                    def stage(t):
                        pool.tensor_copy(xc, xbcT[:, :, ds(t * P, P)]).then_inc(S["staged"], 1)
                        hold(pool, S["staged"], t + 1)
                        for g in range(2):
                            pool.tensor_copy(Cz[g * 64:g * 64 + 64, g, :], xc[g * 64:g * 64 + 64, 9, :]).then_inc(S["cz"], 1)

                    pool.memset(Cz, 0.0).then_inc(S["zeroed"], 1)
                    pool.memset(Cw, 0.0).then_inc(S["zeroed"], 1)
                    pool.wait_ge(S["zeroed"], 2)
                    with pool.Fori(0, 4) as t:
                        pool.wait_ge(S["ydone"], t)
                        stage(t)
                    pool.wait_ge(S["ydone"], 4)
                    stage(4)

                @block.tensor
                def _(pe):
                    def chunk(t, s):
                        pe.wait_ge(S["staged"], t + 1)
                        for k in range(KT):
                            pe.transpose(PX[:, k * P:(k + 1) * P], xc[:, k, :], ident[:])
                        pe.transpose(misc[:, 384:512], xc[:, 8, :], ident[:])
                        d = dta[:, ds(t, 1), :].rearrange("p o h -> p (o h)")
                        pe.wait_ge(S["cz"], 2 * t + 2)
                        last = pe.matmul(misc[:, 64:320], xc[:, 8, :], Cz.rearrange("p g q -> p (g q)"), start=True, stop=True)
                        last.then_inc(S["cb"], 1)
                        pe.wait_ge(S["state"], t + 1)
                        pe.matmul(bank(7)[:, 0:16], upto[s][:], d, start=True, stop=True)
                        pe.matmul(bank(7)[:, 16:32], after[s][:], d, start=True, stop=True)
                        pe.matmul(bank(7)[:, 32:48], ones[:], d, start=True, stop=True).then_inc(S["sums"], 1)
                        pe.wait_ge(S["mdta"], t + 1)
                        for i in range(4):
                            last = pe.matmul(bank(i), after[s][:], mdta[:, 4 * i:4 * i + 4, :].rearrange("p h q -> p (h q)"),
                                             start=True, stop=True)
                        last.then_inc(S["seg"], 1)
                        pe.wait_ge(S["E"], t + 1)
                        for i in range(4):
                            last = pe.matmul(bank(i), ones[:], mdta[:, 4 * i:4 * i + 4, :].rearrange("p h q -> p (h q)"),
                                             start=True, stop=True)
                        last.then_inc(S["acb"], 1)
                        pe.wait_ge(S["xw"], t + 1)
                        pe.wait_ge(S["W"], t + 1)
                        pe.wait_ge(S["Cw"], t + 1)
                        if s:
                            pe.wait_ge(S["st_copied"], 8)
                        for h in range(HEADS):
                            g, i = divmod(h, 8)
                            po = 64 * (h % 2)
                            o = Y[po:po + 64, (h // 2) * P:(h // 2 + 1) * P]
                            pe.matmul(o, xdt[:, h, :], E[:, h, :], start=True, stop=False, skip_group_check=bool(s))
                            if not s:
                                last = pe.matmul(o, stT[:, i * HD:(i + 1) * HD], Cw[:, h, :], start=False, stop=True)
                            else:
                                for b in range(STREAMS):
                                    last = pe.matmul(o[:, b * SLEN:(b + 1) * SLEN], stTb[:, b, i * HD:(i + 1) * HD],
                                                     Cw[:, h, b * SLEN:(b + 1) * SLEN],
                                                     start=False, stop=b == STREAMS - 1, skip_group_check=True)
                        last.then_inc(S["y"], 1)
                        if not s:
                            for g in range(2):
                                last = pe.matmul(bank(7)[g * 64:g * 64 + 64, :], Btok[:, g * NS:(g + 1) * NS],
                                                 xw[:, g * 8:g * 8 + 8, :].rearrange("p h c -> p (h c)"), start=True, stop=True)
                            last.then_inc(S["stadd"], 1)

                    with pe.Fori(0, 4) as t:
                        chunk(t, 0)
                    pe.wait_ge(S["st_in"], 16 * 16)
                    for b in range(STREAMS):
                        if b >= 2:
                            pe.wait_ge(S["st_copied"], b - 1)
                        else:
                            pe.wait_ge(S["Ea"], 4)
                        for j in range(4):
                            last = pe.transpose(bank(b % 2)[:, j * P:(j + 1) * P], stN[:, b * 4 + j, :], ident[:])
                        last.then_inc(S["st_turned"], 1)
                    pe.wait_ge(S["st_copied"], 8)
                    chunk(4, 1)
                    pe.wait_ge(S["dtax"], 1)
                    for i in range(8):
                        last = pe.matmul(bank(7)[:, i * 8:(i + 1) * 8], dtax[:, 2 * i:2 * i + 2, :].rearrange("p h c -> p (h c)"),
                                         stream_of[:], start=True, stop=True)
                    last.then_inc(S["dec"], 1)
                    pe.wait_ge(S["Bm"], 2)
                    pe.wait_ge(S["Ea"], 5)
                    for i in range(8):
                        if i >= 4:
                            pe.wait_ge(S["sadded"], i - 3)
                        pe.matmul(bank(i % 4), xw[:, 2 * i:2 * i + 2, :].rearrange("p h c -> p (h c)"), Bm[:, i // 4, :],
                                  start=True, stop=True).then_inc(S["sadd"], 1)
                    pe.wait_ge(S["ydone"], 5)
                    for j in range(4):
                        last = pe.transpose(misc[:, j * P:(j + 1) * P], stT[:, j * P:(j + 1) * P], ident[:])
                    last.then_inc(S["turned"], 1)

                @block.scalar
                def _(act):
                    def chunk(t):
                        act.wait_ge(S["sums"], t + 1)
                        act.wait_ge(S["state"], t + 1)
                        act.activation(ex, bank(7)[:, 0:48], ACT.Exp).then_inc(S["ex"], 1)
                        act.wait_ge(S["seg"], t + 1)
                        act.activation(E.rearrange("p h q -> p (h q)"), bank(0, 4), ACT.Exp).then_inc(S["E"], 1)
                        act.wait_ge(S["acb"], t + 1)
                        act.activation(Ea.rearrange("p h q -> p (h q)"), bank(0, 4), ACT.Exp).then_inc(S["Ea"], 1)

                    with act.Fori(0, 4) as t:
                        chunk(t)
                    for b in range(STREAMS):
                        act.wait_ge(S["st_turned"], b + 1)
                        act.activation(stTb[:, b, :], bank(b % 2), ACT.Copy).then_inc(S["st_copied"], 1)
                    chunk(4)
                    act.wait_ge(S["dec"], 1)
                    act.activation(spw[:, 0, 0:64], bank(7)[:, 0:64], ACT.Exp).then_inc(S["decE"], 1)
                    act.wait_ge(S["turned"], 1)
                    act.activation(E[:, 0:4, :].rearrange("p h q -> p (h q)"), misc, ACT.Copy).then_inc(S["stadd"], 1)

                @block.vector
                def _(dve):
                    st = Steps(dve, "ssd_step")

                    def chunk(t, s, st):
                        n0 = st.n
                        d = dta[:, ds(t, 1), :].rearrange("p o h -> p (o h)")
                        dtt = dt[:, ds(t, 1), :].rearrange("p o h -> p (o h)")
                        dve.tensor_tensor(mdta, upto[s][:].unsqueeze(1).to_broadcast([P, HEADS, P]), b16(d, P), ALU.mult)\
                           .then_inc(S["mdta"], 1)
                        dve.wait_ge(S["cb"], t + 1)
                        dve.tensor_copy(Btok, misc[:, 384:512]).then_inc(S["Btok"], 1)
                        st(dve.tensor_tensor(xdt, PX.rearrange("p (h c) -> p h c", h=HEADS), b16(dtt, HD), ALU.mult))
                        st.wait()
                        dve.wait_ge(S["ex"], t + 1)
                        dve.wait_ge(S["Btok"], t + 1)
                        dve.tensor_tensor(xw, xdt, b16(ex[:, 16:32], HD), ALU.mult).then_inc(S["xw"], 1)
                        st(dve.tensor_tensor(cbm, misc[:, 64:320].rearrange("p (g q) -> p g q", g=2),
                                             upto[s][:].unsqueeze(1).to_broadcast([P, 2, P]), ALU.mult))
                        st.wait()
                        dve.wait_ge(S["E"], t + 1)
                        v = E.rearrange("p (g h) q -> p g h q", g=2)
                        dve.tensor_tensor(v, v, cbm.unsqueeze(2).to_broadcast([P, 2, 8, P]), ALU.mult).then_inc(S["W"], 1)
                        dve.wait_ge(S["Ea"], t + 1)
                        for g in range(2):
                            r = slice(g * 64, g * 64 + 64)
                            ins = dve.tensor_tensor(Cw[r, g * 8:g * 8 + 8, :], Ea[r, g * 8:g * 8 + 8, :],
                                                    xc[r, 9, :].unsqueeze(1).to_broadcast([64, 8, P]), ALU.mult)
                            if g == 0:
                                st(ins)
                        st.wait()
                        ins.then_inc(S["Cw"], 1)
                        m = mdta.rearrange("p h q -> p (h q)")[:, 0:1024].rearrange("p (k q) -> p k q", k=KT)
                        st(dve.tensor_tensor(m, xc[:, 0:KT, :], b16(cols[:, DD:DD + KT], P), ALU.mult))
                        st.wait()
                        dve.wait_ge(S["y"], t + 1)
                        dve.tensor_tensor(ysT[:, :, ds(t * P, P)], Y.rearrange("p (k q) -> p k q", k=KT), m, ALU.add)\
                           .then_inc(S["ydone"], 1)
                        dve.wait_ge(S["ydone"], t + 1)
                        if not s:
                            for g in range(2):
                                r = slice(g * 64, g * 64 + 64)
                                v = stT[r, :].rearrange("p (h c) -> p h c", h=8)
                                st(dve.tensor_tensor(v, v, b16(ex[r, 32 + g * 8:40 + g * 8], HD), ALU.mult))
                            st.wait()
                            dve.wait_ge(S["stadd"], t + 1)
                            dve.tensor_tensor(stT[:], stT[:], bank(7), ALU.add).then_inc(S["state"], 1)
                            dve.wait_ge(S["state"], t + 2)
                        return st.n - n0

                    dve.memset(stT[:], 0.0).then_inc(S["state"], 1)
                    dve.wait_ge(S["state"], 1)
                    PER = 6
                    with dve.Fori(0, 4) as t:
                        used = chunk(t, 0, Steps(dve, "ssd_step", t * PER))
                        assert used == PER, used
                    st = Steps(dve, "ssd_step", 4 * PER)
                    chunk(4, 1, st)
                    dve.tensor_copy(dtax, b16(dta[:, 4, :], HD)).then_inc(S["dtax"], 1)
                    for g in range(2):
                        dve.tensor_tensor(Bm[:, g, :].rearrange("p (b n) -> p b n", b=STREAMS),
                                          Btok[:, g * NS:(g + 1) * NS].unsqueeze(1).to_broadcast([P, STREAMS, NS]),
                                          b16(stream_of[:], NS), ALU.mult).then_inc(S["Bm"], 1)
                    dve.wait_ge(S["decE"], 1)
                    v = stN.rearrange("p (b j) (g n) -> p b j g n", j=4, g=2)
                    for i in range(8):
                        g, j = divmod(i, 4)
                        st(dve.tensor_tensor(v[:, :, j, g, :], v[:, :, j, g, :], b16(spw[:, 0, i * 8:i * 8 + 8], NS), ALU.mult))
                    st.wait()
                    for i in range(8):
                        g, j = divmod(i, 4)
                        dve.wait_ge(S["sadd"], i + 1)
                        dve.tensor_tensor(v[:, :, j, g, :], v[:, :, j, g, :], bank(i % 4).rearrange("p (b n) -> p b n", b=STREAMS),
                                          ALU.add).then_inc(S["sadded"], 1)
                    dve.wait_ge(S["sadded"], 8)
            end_phase()

            with nc.Block() as block:
                wready = [phase_sem(f"weight_ready_{s}") for s in range(2)]
                done, gated, silued, squared, summed, rooted, ready = (phase_sem(n) for n in (
                    "projected", "gated", "silued", "squared", "summed", "rooted", "root_in"))
                sz = view(arenaX, 0, 2, TT)
                sq = view(arenaR, 2 * KT * TT, 2, TT)
                rs = arenaX[:, 2 * TT:3 * TT]

                @block.sync
                def _(sp):
                    sp.sem_inc(done, 2)
                    with sp.Fori(0, 4) as j:
                        for u in range(2):
                            sp.wait_ge(done, 2 * j + u + 1)
                            sp.dma_start(wt[:, u, :, :], weight("w_in", l, Z0 + j * (2 * P) + u * P)).then_inc(wready[u], 16)

                @block.tensor
                def _(pe):
                    def add_square(u, first, final):
                        for o, n in ((0, SEQ), (SEQ, TT - SEQ)):
                            last = pe.matmul(bank(4, 2)[:, o:o + n], ones[:], sq[:, u, o:o + n], start=first, stop=final)
                        return last

                    for o, n in ((0, SEQ), (SEQ, TT - SEQ)):
                        pe.matmul(bank(4, 2)[:, o:o + n], zeros[:], hT[:, 0, o:o + n], start=True, stop=False)
                    pe.sem_inc(silued, 2)
                    with pe.Fori(0, 4) as j:
                        for u in range(2):
                            pe.wait_ge(wready[u], j * 16 + 16)
                            pe.wait_ge(silued, 2 * j + u + 1)
                            project(u, hT, bank(2 * u, 2)).then_inc(done, 1)
                        for u in range(2):
                            pe.wait_ge(squared, 2 * j + u + 1)
                            add_square(u, False, False).then_inc(summed, 1)
                    for o, n in ((0, SEQ), (SEQ, TT - SEQ)):
                        last = pe.matmul(bank(4, 2)[:, o:o + n], zeros[:], hT[:, 0, o:o + n], start=False, stop=True)
                    last.then_inc(summed, 1)

                @block.scalar
                def _(act):
                    act.sem_inc(gated, 2)
                    act.sem_inc(summed, 2)
                    with act.Fori(0, 4) as j:
                        for u in range(2):
                            act.wait_ge(done, 2 + 2 * j + u + 1)
                            act.wait_ge(gated, 2 * j + u + 1)
                            act.activation(sz[:, u, :], bank(2 * u, 2)[:, 0:TT], ACT.Silu).then_inc(silued, 1)
                        for u in range(2):
                            act.wait_ge(gated, 2 + 2 * j + u + 1)
                            act.wait_ge(summed, 2 * j + u + 1)
                            act.activation(sq[:, u:u + 1, :], ysT[:, ds(2 * j + u, 1), :], ACT.Square).then_inc(squared, 1)
                    act.wait_ge(ready, 1)
                    act.activation(rs, rs, ACT.Sqrt).then_inc(rooted, 1)

                @block.vector
                def _(dve):
                    with dve.Fori(0, 4) as j:
                        for u in range(2):
                            dve.wait_ge(silued, 2 + 2 * j + u + 1)
                            y = ysT[:, ds(2 * j + u, 1), :]
                            dve.tensor_tensor(y, y, sz[:, u:u + 1, :], ALU.mult).then_inc(gated, 1)
                    dve.wait_ge(summed, 2 + 9)
                    dve.wait_ge(gated, 2 + 8)
                    dve.tensor_scalar(rs, bank(4, 2)[:, 0:TT], 1.0 / D, EPS, ALU.mult, ALU.add).then_inc(ready, 1)
                    dve.wait_ge(rooted, 1)
                    st = Steps(dve, "dve_step")
                    st(dve.reciprocal(rs, rs))
                    st.wait()
                    for k in range(KT):
                        st(dve.scalar_tensor_tensor(ysT[:, k, :], ysT[:, k, :], cols[:, NW + k:NW + k + 1], rs, ALU.mult, ALU.mult))
                    st.wait()
            end_phase()

            with nc.Block() as block:
                wready = [phase_sem(f"weight_ready_{s}") for s in range(2)]
                gready = [phase_sem(f"gate_weights_ready_{s}") for s in range(2)]
                done, gates_done, evac, zeroed = (phase_sem(n) for n in ("projected", "gates_done", "ly_taken", "zeroed"))
                sg, th, gs, sgs, rt, q, fin = (phase_sem(n) for n in (
                    "sigmoids", "tanh", "gelu_in", "gelu_sig", "rooted", "root_in", "lru_done"))
                wbd = view(arenaW, 6 * D, 4, P)
                rows = [arenaR[:, 2 * KT * TT + i * TT:2 * KT * TT + (i + 1) * TT] for i in range(9)]
                rows += [arenaQ[:, i * TT:(i + 1) * TT] for i in range(9)]
                buf = [dict(zip(("R", "I", "LY", "G", "Q4", "AA", "UU", "REC", "HS"), rows[u * 9:])) for u in range(2)]
                outrow = view(arenaW, 4096, D)

                @block.sync
                def _(sp):
                    sp.wait_ge(zeroed, 1)
                    sp.sem_inc(done, 2)
                    sp.sem_inc(gates_done, 2)
                    with sp.Fori(0, KT // 2) as j:
                        for u in range(2):
                            sp.wait_ge(gates_done, 2 * j + u + 1)
                            for i, nm in enumerate(("lru_wa", "lru_wx")):
                                for h in range(2):
                                    src = a[nm].rearrange("l n d e -> (l n d) e")[ds(l * D + j * (2 * P) + u * P + h * 64, 64), :]
                                    sp.dma_start(wbd[h * 64:h * 64 + 64, 2 * u + i, h * 64:h * 64 + 64], src).then_inc(gready[u], 16)
                            sp.wait_ge(done, 2 * j + u + 1)
                            sp.dma_start(wt[:, u, :, :], weight("w_in", l, LY0 + j * (2 * P) + u * P)).then_inc(wready[u], 16)
                    sp.wait_ge(phase_sem("lru_rows"), 1)
                    sp.dma_start(a["new_lru_prompt"].rearrange("l b c -> (l b) c")[ds(l, 1), :], outrow[0:1, :]).then_inc(phase_sem("out_written"), 16)
                    sp.dma_start(a["new_lru_sample"].rearrange("l b c -> (l b) c")[ds(l * 8, 8), :], outrow[1:9, :]).then_inc(phase_sem("out_written"), 16)
                    sp.wait_ge(phase_sem("out_written"), 32)

                @block.tensor
                def _(pe):
                    pe.sem_inc(sg, 2)
                    pe.sem_inc(evac, 2)
                    with pe.Fori(0, KT // 2) as j:
                        for u in range(2):
                            pe.wait_ge(gready[u], j * 64 + 64)
                            pe.wait_ge(sg, 4 * j + 2 * u + 2)
                            for i in range(2):
                                for o, n in ((0, SEQ), (SEQ, TT - SEQ)):
                                    last = pe.matmul(bank(2 * i, 2)[:, o:o + n], wbd[:, 2 * u + i, :],
                                                     lxT[:, ds(2 * j + u, 1), o:o + n].rearrange("p o t -> p (o t)"),
                                                     start=True, stop=True)
                            last.then_inc(gates_done, 1)
                            pe.wait_ge(wready[u], j * 16 + 16)
                            pe.wait_ge(evac, 2 * j + u + 1)
                            project(u, hT, bank(4 + 2 * u, 2)).then_inc(done, 1)
                    pe.wait_ge(fin, 2 + KT)
                    for k in range(KT):
                        last = pe.transpose(bank(6, 2)[0:9, k * P:(k + 1) * P], lruN[:, k, :], ident[:])
                    last.then_inc(phase_sem("lru_turned"), 1)

                @block.scalar
                def _(act):
                    act.sem_inc(fin, 2)
                    with act.Fori(0, KT // 2) as j:
                        for u in range(2):
                            B = buf[u]
                            act.wait_ge(gates_done, 2 + 2 * j + u + 1)
                            act.wait_ge(fin, 2 * j + u + 1)
                            act.activation(B["R"], bank(0, 2)[:, 0:TT], ACT.Sigmoid, bias=cols[:, ds(BA + 2 * j + u, 1)]).then_inc(sg, 1)
                            act.activation(B["I"], bank(2, 2)[:, 0:TT], ACT.Sigmoid, bias=cols[:, ds(BX + 2 * j + u, 1)]).then_inc(sg, 1)
                            act.wait_ge(sg, 2 + 4 * j + 2 * u + 1)
                            act.activation(B["R"], B["R"], ACT.Tanh, scale=lamS[:, ds(2 * j + u, 1)]).then_inc(th, 1)
                            act.wait_ge(done, 2 + 2 * j + u + 1)
                            act.activation(B["LY"], bank(4 + 2 * u, 2)[:, 0:TT], ACT.Copy).then_inc(evac, 1)
                        for u in range(2):
                            act.wait_ge(gs, 2 * j + u + 1)
                            act.activation(buf[u]["G"], buf[u]["G"], ACT.Sigmoid, scale=1.5957691216057308).then_inc(sgs, 1)
                        for u in range(2):
                            act.wait_ge(q, 2 * j + u + 1)
                            act.activation(buf[u]["Q4"], buf[u]["Q4"], ACT.Sqrt).then_inc(rt, 1)
                    act.wait_ge(phase_sem("lru_turned"), 1)
                    act.activation(outrow[0:9, :], bank(6, 2)[0:9, :], ACT.Copy).then_inc(phase_sem("lru_rows"), 1)

                @block.vector
                def _(dve):
                    st = Steps(dve, "dve_step")
                    st(dve.memset(wbd, 0.0))
                    st.wait()
                    dve.sem_inc(zeroed, 1)
                    PER = 24
                    blk = lambda v: v.rearrange("p (b t) -> p b t", t=SLEN)
                    with dve.Fori(0, KT // 2) as j:
                        st = Steps(dve, "lru_step", j * PER)
                        for u in range(2):
                            R, I, LY, G, Q4, AA, UU, REC, HS = (buf[u][n] for n in ("R", "I", "LY", "G", "Q4", "AA", "UU", "REC", "HS"))
                            dve.wait_ge(th, 2 * j + u + 1)
                            st(dve.tensor_scalar(REC, R, -1.0, 1.0, ALU.mult, ALU.add))
                            dve.tensor_scalar(Q4, R, -4.0, 1e-30, ALU.mult, ALU.max).then_inc(q, 1)
                            dve.wait_ge(evac, 2 + 2 * j + u + 1)
                            st(dve.tensor_tensor(G, LY, LY, ALU.mult))
                            st.wait()
                            st(dve.reciprocal(REC, REC))
                            st(dve.tensor_scalar(G, G, 0.044715, 1.0, ALU.mult, ALU.add))
                            st(dve.tensor_tensor(I, I, lxT[:, ds(2 * j + u, 1), :].rearrange("p o t -> p (o t)"), ALU.mult))
                            st.wait()
                            dve.tensor_tensor(G, G, LY, ALU.mult).then_inc(gs, 1)
                            st(dve.scalar_tensor_tensor(AA, R, 1.0, REC, ALU.add, ALU.mult))
                            st(dve.tensor_tensor(I, I, REC, ALU.mult))
                        for u in range(2):
                            R, I, LY, G, Q4, AA, UU, REC, HS = (buf[u][n] for n in ("R", "I", "LY", "G", "Q4", "AA", "UU", "REC", "HS"))
                            st.wait()
                            dve.wait_ge(rt, 2 * j + u + 1)
                            st(dve.tensor_tensor(UU, I, Q4, ALU.mult))
                            h0 = cols[:, H0:CV].rearrange("p (b k) -> p b k", k=KT)[:, :, ds(2 * j + u, 1)]
                            first = blk(AA)[:, 32:40, 0:1]
                            tmp = small[:, 8 * u:8 * u + 8].unsqueeze(2)
                            st(dve.tensor_tensor(tmp, first, h0, ALU.mult))
                            dve.wait_ge(sgs, 2 * j + u + 1)
                            dve.tensor_tensor(G, G, LY, ALU.mult).then_inc(phase_sem("gelu"), 1)
                            st.wait()
                            st(dve.tensor_tensor(blk(UU)[:, 32:40, 0:1], blk(UU)[:, 32:40, 0:1], tmp, ALU.add))
                            st(dve.memset(first, 0.0))
                            st.wait()
                            st(dve.tensor_tensor_scan(HS, AA, UU, 0.0, ALU.mult, ALU.add))
                            st.wait()
                            dve.wait_ge(phase_sem("gelu"), 2 * j + u + 1)
                            dve.tensor_copy(lruN[:, ds(2 * j + u, 1), 1:9], blk(HS)[:, 32:40, SLEN - 1:SLEN].rearrange("p b o -> p o b"))\
                               .then_inc(phase_sem("last_taken"), 1)
                            dve.tensor_copy(lruN[:, ds(2 * j + u, 1), 0:1], HS[:, SEQ - 1:SEQ].unsqueeze(1)).then_inc(phase_sem("last_taken"), 1)
                            dve.tensor_tensor(ylT[:, ds(2 * j + u, 1), :], G.unsqueeze(1), HS.unsqueeze(1), ALU.mult).then_inc(fin, 1)
                        assert st.n == PER, st.n
                    dve.wait_ge(fin, 2 + KT)
                    dve.wait_ge(phase_sem("last_taken"), 2 * KT)
            end_phase()

            with nc.Block() as block:
                wready = [phase_sem(f"weight_ready_{s}") for s in range(4)]
                done, sg, taken = phase_sem("projected"), phase_sem("sigmoids"), phase_sem("taken")
                G2 = view(arenaX, 0, 2, TT)
                M1 = arenaX[:, 2 * TT:3 * TT]
                srcs = ((("w_in", GS0), hT), (("w_br_ssd", 0), ysT), (("w_in", GL0), hT), (("w_br_lru", 0), ylT))

                @block.sync
                def _(sp):
                    sp.sem_inc(done, 4)
                    with sp.Fori(0, KT) as j:
                        for u, ((nm, c0), _) in enumerate(srcs):
                            sp.wait_ge(done, 4 * j + u + 1)
                            sp.dma_start(wt[:, u, :, :], weight(nm, l, c0 + j * P)).then_inc(wready[u], 16)

                @block.tensor
                def _(pe):
                    pe.sem_inc(sg, 2)
                    pe.sem_inc(taken, 2)
                    with pe.Fori(0, KT) as j:
                        for u, (_, src) in enumerate(srcs):
                            pe.wait_ge(wready[u], j * 16 + 16)
                            pe.wait_ge(taken if u % 2 else sg, 2 * j + u // 2 + 1)
                            project(u, src, bank(2 * u, 2)).then_inc(done, 1)

                @block.scalar
                def _(act):
                    with act.Fori(0, KT) as j:
                        for i in range(2):
                            act.wait_ge(done, 4 + 4 * j + 2 * i + 1)
                            act.wait_ge(taken, 2 * j + i + 1)
                            act.activation(G2[:, i, :], bank(4 * i, 2)[:, 0:TT], ACT.Sigmoid).then_inc(sg, 1)

                @block.vector
                def _(dve):
                    with dve.Fori(0, KT) as j:
                        m = mT[:, ds(j, 1), :].rearrange("p o t -> p (o t)")
                        dve.wait_ge(sg, 2 + 2 * j + 1)
                        dve.wait_ge(done, 4 + 4 * j + 2)
                        dve.tensor_tensor(M1, bank(2, 2)[:, 0:TT], G2[:, 0, :], ALU.mult).then_inc(taken, 1)
                        dve.wait_ge(sg, 2 + 2 * j + 2)
                        dve.wait_ge(done, 4 + 4 * j + 4)
                        dve.tensor_tensor(m, bank(6, 2)[:, 0:TT], G2[:, 1, :], ALU.mult).then_inc(taken, 1)
                        dve.wait_ge(taken, 2 + 2 * j + 2)
                        dve.tensor_tensor(m, m, M1, ALU.add).then_inc(phase_sem("merged"), 1)
                        dve.wait_ge(phase_sem("merged"), j + 1)
            end_phase()

            with nc.Block() as block:
                wready = [phase_sem(f"weight_ready_{s}") for s in range(2)]
                done, taken = phase_sem("projected"), phase_sem("taken")
                TMP = view(arenaX, 0, 2, TT)

                @block.sync
                def _(sp):
                    sp.sem_inc(done, 2)
                    with sp.Fori(0, 4) as j:
                        for u in range(2):
                            sp.wait_ge(done, 2 * j + u + 1)
                            sp.dma_start(wt[:, u, :, :], weight("w_out", l, j * (2 * P) + u * P)).then_inc(wready[u], 16)

                @block.tensor
                def _(pe):
                    pe.sem_inc(taken, 2)
                    with pe.Fori(0, 4) as j:
                        for u in range(2):
                            pe.wait_ge(wready[u], j * 16 + 16)
                            pe.wait_ge(taken, 2 * j + u + 1)
                            project(u, mT, bank(2 * u, 2)).then_inc(done, 1)

                @block.vector
                def _(dve):
                    blk = lambda v: v.rearrange("p (b t) -> p b t", t=SLEN)
                    with dve.Fori(0, 4) as j:
                        for u in range(2):
                            dve.wait_ge(done, 2 + 2 * j + u + 1)
                            g = modE[:, ds(2 * KT + 2 * j + u, 1), :].rearrange("p o b -> p (o b)")
                            x = xT[:, ds(2 * j + u, 1), :].rearrange("p o t -> p (o t)")
                            dve.tensor_tensor(blk(TMP[:, u, :]), blk(bank(2 * u, 2)[:, 0:TT]), b16(g), ALU.mult).then_inc(taken, 1)
                            dve.wait_ge(taken, 2 + 2 * j + u + 1)
                            dve.tensor_tensor(x, x, TMP[:, u, :], ALU.add).then_inc(phase_sem("added"), 1)
                    dve.wait_ge(phase_sem("added"), KT)
            end_phase()

            norm_phase(hT[:], modE[:, 4 * KT:5 * KT, :], modE[:, 3 * KT:4 * KT, :])

            qT = view(arenaQ, 0, 2 * PH, TT)
            ring = view(arenaR, 0, RING, D)
            diag = view(arenaW, 0, RING, P)
            qs = view(arenaW, 2048, 2 * PH, P)
            cand = view(arenaW, 2048, PH, TOPK * TOPK)
            cand1 = view(arenaW, 3072, 1, TOPK * TOPK)
            hs = view(arenaW, 4096, KT, P)
            osb = arenaW[:, 4096:4096 + D]
            hrow = arenaW[:, 5120:6144]
            cut = view(arenaX, 0, 2 * PH, KEYS)
            ccut = view(arenaX, 0, PH, TOPK * TOPK)
            kT = view(arenaQ, 16 * TT + 1024, 2, P)
            ps_out, ps_sc, ps_t = bank(0, 2), bank(2, 4), bank(6, 2)
            free = [(arenaW, 6144, 8192), (arenaQ, 16 * TT, 16 * TT + 1024)]
            acc = hrow

            def tile_of(*shape):
                n = 1
                for x in shape:
                    n *= x
                for i, (ar, lo, hi) in enumerate(free):
                    if hi - lo >= n:
                        free[i] = (ar, lo + n, hi)
                        return view(ar, lo, *shape)
                raise ValueError("no room")

            val = tile_of(2 * PH, TOPK)
            key = tile_of(2 * PH, TOPK).bitcast(U32)
            keyf = tile_of(2 * PH, TOPK)
            eidx = tile_of(NT, PICKS).bitcast(U32)
            sval = tile_of(PH, TOPK)
            place = tile_of(PH, TOPK).bitcast(U32)
            parts = tile_of(2, PICKS).bitcast(U32)
            partf = tile_of(2, PICKS)
            gate = tile_of(PH, TOPK)
            hid = tile_of(PICKS)
            gel = tile_of(PICKS)
            wgt = tile_of(PICKS)
            slot_idx = small[:, 16:32].rearrange("p (h n) -> p h n", h=2).bitcast(U32)
            den = small[:, 32:40]
            sv1 = spw[:, 0:1, 0:TOPK]
            pl1 = spw[:, 1:2, 0:TOPK].bitcast(U32)
            row0 = small[:, 40:41]
            with nc.Block() as block:
                G = {n: phase_sem("peer_" + n) for n in (
                    "keys_in", "keys_turned", "keys", "q_staged", "h_staged", "h_turned", "h_rows", "scores", "idx",
                    "exp_in", "exp_out", "u_used", "v_used", "v_added", "hid", "gelu", "wgt", "diag", "sum", "osb",
                    "o_turned", "resid", "slots", "row0", "projected", "q_taken", "head_idx", "acc")}
                wready = [phase_sem(f"weight_ready_{s}") for s in range(2)]

                @block.sync
                def _(sp):
                    for i, nm in enumerate(("peer_k1", "peer_k2")):
                        sp.dma_start(rowbuf[:, i, :], a[nm].rearrange("l k d -> (l k) d")[ds(l * KEYS, KEYS), :]).then_inc(G["keys_in"], 16)
                    sp.sem_inc(G["projected"], 2)
                    with sp.Fori(0, PH) as j:
                        for u in range(2):
                            sp.wait_ge(G["projected"], 2 * j + u + 1)
                            sp.dma_start(wt[:, u, :, :], weight("peer_wq", l, j * (2 * P) + u * P)).then_inc(wready[u], 16)

                @block.gpsimd
                def _(pool):
                    for n in ("u_used", "v_used", "v_added"):
                        pool.sem_inc(G[n], 2)
                    u_table = a["peer_u"].rearrange("l e d -> (l e) d")
                    v_table = a["peer_v"].rearrange("l e d -> (l e) d")

                    def gather(t, i, hf, table, at):
                        pool.tensor_copy(slot_idx[:, hf:hf + 1, :], eidx[:, ds(t, 1), ds(at, HALF)]).then_inc(G["slots"], 1)
                        hold(pool, G["slots"], t * 32 + i + 1)
                        for n in range(HALF):
                            pool.indirect_dma_start(ring[:, hf * HALF + n, :], None, table,
                                                    bass.IndirectOffsetOnAxis(ap=slot_idx[:, hf, n:n + 1], axis=0))\
                                .then_inc(gathered[hf * HALF + n], 16)

                    def gather_u(t, first):
                        with pool.Fori(0, BATCHES) as m:
                            if first:
                                hold(pool, G["head_idx"], m + 1)
                            for hf in range(2):
                                hold(pool, G["u_used"], t * 16 + m * 2 + hf + 1)
                                if not first:
                                    hold(pool, G["v_used"], t * 16 + hf + 1)
                                    hold(pool, G["v_added"], t * (SHARE // 2) + hf + 1)
                                gather(t, m * 2 + hf, hf, u_table, m * RING + hf * HALF)

                    def gather_v(t):
                        for lo, hi in ((0, SHARED), (SHARED, BATCHES)):
                            with pool.Fori(lo, hi) as m:
                                for hf in range(2):
                                    hold(pool, G["u_used"], t * 16 + 16 + hf + 1)
                                    hold(pool, G["v_used"], t * 16 + m * 2 + hf + 1)
                                    if lo:
                                        hold(pool, G["v_added"], t * (SHARE // 2) + (m - SHARED) * 2 + hf + 1)
                                    gather(t, m * 2 + (16 + hf), hf, v_table, m * RING + hf * HALF)

                    gather_u(0, True)
                    gather_v(0)
                    with pool.Fori(1, NT) as t:
                        hold(pool, G["idx"], t)
                        gather_u(t, False)
                        gather_v(t)

                @block.tensor
                def _(pe):
                    pe.wait_ge(G["keys_in"], 32)
                    for i in range(2):
                        last = pe.transpose(ps_t[:, i * P:(i + 1) * P], rowbuf[:, i, :], ident[:])
                    last.then_inc(G["keys_turned"], 1)
                    pe.wait_ge(G["keys"], 1)
                    pe.sem_inc(G["q_taken"], 2)

                    def queries():
                        with pe.Fori(0, PH) as j:
                            for u in range(2):
                                pe.wait_ge(wready[u], j * 16 + 16)
                                pe.wait_ge(G["q_taken"], 2 * j + u + 1)
                                project(u, hT, bank(2 * u, 2)).then_inc(G["projected"], 1)
                            pe.wait_ge(G["q_staged"], 2 * j + 2)
                            pe.wait_ge(G["head_idx"], j)
                            for u in range(2):
                                last = pe.matmul(bank(4 + u)[:, 0:KEYS], qs[:, u, :], kT[:, u, :], start=True, stop=True)
                            last.then_inc(G["scores"], 1)

                    def score(t):
                        pe.wait_ge(G["q_staged"], 2 * PH + t)
                        for i in range(2 * PH):
                            last = pe.matmul(ps_sc[:, i * KEYS:(i + 1) * KEYS], qs[:, i, :], kT[:, i % 2, :], start=True, stop=True)
                        last.then_inc(G["scores"], 1)

                    def turn_h(t):
                        pe.wait_ge(G["h_staged"], t + 1)
                        for k in range(KT):
                            last = pe.transpose(ps_t[:, k * P:(k + 1) * P], hs[:, k, :], ident[:])
                        last.then_inc(G["h_turned"], 1)

                    def retrieve(t):
                        for c in range(2):
                            pe.matmul(ps_out[:, c * 512:(c + 1) * 512], zeros[:], hT[:, 0, 0:512], start=True, stop=False)
                        for lo, hi in ((0, SHARED), (SHARED, BATCHES)):
                            with pe.Fori(lo, hi) as m:
                                for hf in range(2):
                                    pe.wait_ge(G["diag"], t * 16 + m * 2 + hf + 1)
                                    for n in range(hf * HALF, (hf + 1) * HALF):
                                        if lo and n % 4 == 3:
                                            continue
                                        pe.wait_ge(gathered[n], l * (NT * 256) + t * 256 + 128 + m * 16 + 16)
                                        for c in range(2):
                                            last = pe.matmul(ps_out[:, c * 512:(c + 1) * 512], diag[:, n, :],
                                                             ring[:, n, c * 512:(c + 1) * 512], start=False, stop=False)
                                    last.then_inc(G["v_used"], 1)
                        pe.wait_ge(G["acc"], t + 1)
                        for c in range(2):
                            last = pe.matmul(ps_out[:, c * 512:(c + 1) * 512], ident[:], acc[:, c * 512:(c + 1) * 512],
                                             start=False, stop=True)
                        last.then_inc(G["sum"], 1)
                        pe.wait_ge(G["osb"], t + 1)
                        for k in range(KT):
                            last = pe.transpose(ps_t[:, k * P:(k + 1) * P], osb[:, k * P:(k + 1) * P], ident[:])
                        last.then_inc(G["o_turned"], 1)

                    turn_h(0)
                    queries()
                    with pe.Fori(0, NT - 1) as t:
                        score(t + 1)
                        retrieve(t)
                        pe.wait_ge(G["resid"], t + 1)
                        turn_h(t + 1)
                    retrieve(NT - 1)

                @block.scalar
                def _(act):
                    act.wait_ge(G["keys_turned"], 1)
                    act.activation(kT.rearrange("p i k -> p (i k)"), ps_t[:, 0:2 * P], ACT.Copy).then_inc(G["keys"], 1)

                    def stage_q(t):
                        act.activation(qs, qT[:, :, ds(t * P, P)], ACT.Copy).then_inc(G["q_staged"], 1)

                    def stage_h(t):
                        act.activation(hs, hT[:, :, ds(t * P, P)], ACT.Copy).then_inc(G["h_staged"], 1)
                        act.wait_ge(G["h_turned"], t + 1)
                        act.wait_ge(G["sum"], t)
                        act.activation(hrow, ps_t, ACT.Copy).then_inc(G["h_rows"], 1)

                    def exponent(t):
                        act.wait_ge(G["exp_in"], t + 1)
                        act.activation(gate, gate, ACT.Exp).then_inc(G["exp_out"], 1)

                    def tile(t, more):
                        act.wait_ge(G["hid"], t + 1)
                        act.activation(gel, hid, ACT.Gelu_apprx_tanh).then_inc(G["gelu"], 1)
                        if more:
                            stage_q(t + 1)
                        act.wait_ge(G["wgt"], t + 1)
                        for lo, hi in ((0, SHARED), (SHARED, BATCHES)):
                            with act.Fori(lo, hi) as m:
                                for hf in range(2):
                                    act.wait_ge(G["v_used"], t * 16 + m * 2 + hf + 1)
                                    for n in range(hf * HALF, (hf + 1) * HALF):
                                        if lo and n % 4 == 3:
                                            continue
                                        last = act.activation(diag[:, n, :], ident[:], ACT.Copy, scale=wgt[:, ds(m * RING + n, 1)])
                                        if n < (hf + 1) * HALF - (2 if lo else 1):
                                            last.then_inc(phase_sem("diag_part"), 1)
                                    last.then_inc(G["diag"], 1)
                        if more:
                            exponent(t + 1)
                        act.wait_ge(G["sum"], t + 1)
                        act.activation(osb, ps_out, ACT.Copy).then_inc(G["osb"], 1)
                        if more:
                            act.wait_ge(G["o_turned"], t + 1)
                            stage_h(t + 1)

                    stage_h(0)
                    with act.Fori(0, PH) as j:
                        for u in range(2):
                            act.wait_ge(G["projected"], 2 + 2 * j + u + 1)
                            act.activation(qT[:, ds(2 * j + u, 1), :], bank(2 * u, 2)[:, 0:TT].unsqueeze(1), ACT.Copy)\
                               .then_inc(G["q_taken"], 1)
                            if u == 0:
                                act.wait_ge(G["scores"], j)
                            hold(act, G["q_taken"], 2 + 2 * j + u + 1)
                            act.activation(qs[:, u:u + 1, :], qT[:, ds(2 * j + u, 1), 0:P], ACT.Copy).then_inc(G["q_staged"], 1)
                    exponent(0)
                    with act.Fori(0, NT - 1) as t:
                        tile(t, True)
                    tile(NT - 1, False)

                @block.vector
                def _(dve):
                    def top16(st, src, work, vals, places, n):
                        for i in range(n):
                            st(dve.max(vals[:, i, 0:8], src[:, i, :]))
                        st.hold()
                        for i in range(n):
                            st(dve.max_index(places[:, i, 0:8], vals[:, i, 0:8], src[:, i, :]))
                            st(dve.match_replace(work[:, i, :], vals[:, i, 0:8], src[:, i, :], NEG))
                        st.hold()
                        for i in range(n):
                            st(dve.max(vals[:, i, 8:16], work[:, i, :]))
                        st.hold()
                        for i in range(n):
                            st(dve.max_index(places[:, i, 8:16], vals[:, i, 8:16], work[:, i, :]))
                        st.hold()

                    def choose(st, sc, cnd, nh, v, k, kf, sv, pl, e_out, signal):
                        shape = [P, nh, TOPK, TOPK]
                        picks = nh * TOPK
                        top16(st, sc, cut, v, k, 2 * nh)
                        st(dve.tensor_copy(kf, k))
                        v4 = v.rearrange("p (h s) k -> p h s k", s=2)
                        k4 = kf.rearrange("p (h s) k -> p h s k", s=2)
                        st(dve.tensor_tensor(cnd.rearrange("p h (a b) -> p h a b", a=TOPK),
                                             v4[:, :, 0, :].unsqueeze(3).to_broadcast(shape),
                                             v4[:, :, 1, :].unsqueeze(2).to_broadcast(shape), ALU.add))
                        st.hold()
                        top16(st, cnd, ccut, sv, pl, nh)
                        flat = pl.rearrange("p h k -> p (h k)")
                        pt, pf = parts[:, :, 0:picks], partf[:, :, 0:picks]
                        st(dve.tensor_scalar(pt[:, 0, :], flat, 4, None, ALU.logical_shift_right))
                        st(dve.tensor_scalar(pt[:, 1, :], flat, TOPK - 1, None, ALU.bitwise_and))
                        st.wait()
                        st(dve.tensor_copy(pf, pt))
                        st.wait()
                        eqs = (cnd, ccut[:, 0:nh, :])
                        for s in range(2):
                            st(dve.tensor_tensor(eqs[s].rearrange("p h (k a) -> p (h k) a", a=TOPK),
                                                 pf[:, s, :].unsqueeze(2).to_broadcast([P, picks, TOPK]),
                                                 iota16[:].unsqueeze(1).to_broadcast([P, picks, TOPK]), ALU.is_equal))
                        st.wait()
                        for s in range(2):
                            e4 = eqs[s].rearrange("p h (k a) -> p h k a", a=TOPK)
                            st(dve.tensor_tensor(e4, e4, k4[:, :, s, :].unsqueeze(2).to_broadcast(shape), ALU.mult))
                        st.wait()
                        for s in range(2):
                            st(dve.tensor_reduce(pf[:, s, :], eqs[s].rearrange("p h (k a) -> p (h k) a", a=TOPK),
                                                 op=ALU.add, axis=AX.X))
                        st.wait()
                        st(dve.scalar_tensor_tensor(pf[:, 0, :], pf[:, 0, :], float(KEYS), pf[:, 1, :], ALU.mult, ALU.add))
                        st.wait()
                        dve.tensor_scalar(e_out, pf[:, 0:1, :], row0, None, ALU.add).then_inc(signal, 1)

                    def gates(t, st):
                        dve.tensor_tensor(gate, sval, sval[:, :, 0:1].to_broadcast([P, PH, TOPK]), ALU.subtract)\
                           .then_inc(G["exp_in"], 1)
                        dve.wait_ge(G["exp_out"], t + 1)
                        st(dve.tensor_reduce(den, gate, op=ALU.add, axis=AX.X))
                        st.wait()
                        st(dve.reciprocal(den, den))
                        st.wait()
                        st(dve.tensor_tensor(gate, gate, b16(den, TOPK), ALU.mult))
                        st.wait()

                    def dot_ring(t, m):
                        for n in range(RING):
                            dve.wait_ge(gathered[n], l * (NT * 256) + t * 256 + m * 16 + 16)
                            ins = dve.scalar_tensor_tensor(out=ring[:, n, :], in0=ring[:, n, :], scalar=1.0, in1=hrow,
                                                           op0=ALU.mult, op1=ALU.mult,
                                                           accum_out=hid[:, ds(m * RING + n, 1)])
                            ins.then_inc(G["u_used"] if n % HALF == HALF - 1 else phase_sem("dot_part"), 1)

                    def tile(t, more, dotted=False):
                        base = FIRST + t * TILE
                        st = Steps(dve, "peer_step", base)
                        if not dotted:
                            hold(dve, G["h_rows"], t + 1)
                            with dve.Fori(0, BATCHES) as m:
                                dot_ring(t, m)
                        dve.wait_ge(G["u_used"], t * 16 + 16 + 2)
                        dve.sem_inc(G["hid"], 1)
                        dve.wait_ge(G["gelu"], t + 1)
                        dve.tensor_tensor(wgt, gel, gate.rearrange("p h k -> p (h k)"), ALU.mult).then_inc(G["wgt"], 1)
                        st(dve.memset(acc, 0.0))
                        dve.wait_ge(G["wgt"], t + 1)
                        if more:
                            hold(dve, G["scores"], PH + t + 1)
                            choose(st, ps_sc.rearrange("p (i k) -> p i k", k=KEYS), cand, PH, val, key, keyf, sval, place,
                                   eidx[:, ds(t + 1, 1), :], G["idx"])
                        st.hold()
                        with dve.Fori(SHARED, BATCHES) as m:
                            for i, n in enumerate(range(3, RING, 4)):
                                dve.wait_ge(gathered[n], l * (NT * 256) + t * 256 + 128 + m * 16 + 16)
                                if i:
                                    dve.wait_ge(phase_sem("share"), t * SHARE + (m - SHARED) * 4 + i)
                                else:
                                    dve.wait_ge(phase_sem("share"), t * SHARE + (m - SHARED) * 4)
                                dve.scalar_tensor_tensor(acc, ring[:, n, :], wgt[:, ds(m * RING + n, 1)], acc, ALU.mult, ALU.add)\
                                   .then_inc(phase_sem("share"), 1)
                                if i % 2:
                                    dve.wait_ge(phase_sem("share"), t * SHARE + (m - SHARED) * 4 + i + 1)
                                    dve.sem_inc(G["v_added"], 1)
                        dve.wait_ge(phase_sem("share"), t * SHARE + SHARE)
                        dve.sem_inc(G["acc"], 1)
                        if more:
                            gates(t + 1, st)
                        dve.wait_ge(G["o_turned"], t + 1)
                        tmp = arenaX[:, 0:D]
                        for k in range(KT):
                            blk = lambda v: v[:, k * P:(k + 1) * P].rearrange("p (b t) -> p b t", t=SLEN)
                            g = modE[:, 5 * KT + k:5 * KT + k + 1, ds(t * 8, 8)].rearrange("p o b -> p (o b)")
                            st(dve.tensor_tensor(blk(tmp), blk(ps_t), b16(g), ALU.mult))
                        if more:
                            assert st.n == TILE, st.n
                        st.wait()
                        x = xT[:, :, ds(t * P, P)]
                        dve.tensor_tensor(x, x, tmp.rearrange("p (k c) -> p k c", k=KT), ALU.add).then_inc(G["resid"], 1)
                        dve.wait_ge(G["resid"], t + 1)

                    TOP = 5
                    LOOKUP = 2 + 3 + 6 + 1
                    PICK = 3 * PH * TOP + LOOKUP + 3
                    HEAD = 3 * TOP + LOOKUP
                    FIRST = PH * HEAD + 3
                    TILE = 1 + PICK + KT
                    dve.tensor_copy(row0, layer_row[:, ds(l, 1)]).then_inc(G["row0"], 1)
                    dve.wait_ge(G["row0"], 1)
                    def head(j):
                        st = Steps(dve, "peer_step", j * HEAD)
                        hold(dve, G["scores"], j + 1)
                        choose(st, psum[:, 4:6, 0:KEYS], cand1, 1, val[:, 0:2, :], key[:, 0:2, :], keyf[:, 0:2, :], sv1,
                               pl1, eidx[:, 0:1, ds(j * TOPK, TOPK)], G["head_idx"])
                        dve.tensor_copy(sval[:, ds(j, 1), :], sv1).then_inc(phase_sem("sums_kept"), 1)
                        dve.wait_ge(phase_sem("sums_kept"), j + 1)
                        assert st.n == HEAD, st.n

                    head(0)
                    hold(dve, G["h_rows"], 1)
                    with dve.Fori(1, PH) as j:
                        head(j)
                        dot_ring(0, j - 1)
                    dot_ring(0, PH - 1)
                    gates(0, Steps(dve, "peer_step", PH * HEAD))
                    tile(0, True, True)
                    with dve.Fori(1, NT - 1) as t:
                        tile(t, True)
                    tile(NT - 1, False)
            end_phase()

        norm_phase(hT[:], cols[:, FIN:FIN + KT], None)
        yout = view(arenaR, 0, NT, D)
        with nc.Block() as block:
            turned, y_ready, out_sem = phase_sem("y_turned"), phase_sem("y_ready"), phase_sem("out_written")

            @block.tensor
            def _(pe):
                for t in range(NT):
                    if t >= 4:
                        pe.wait_ge(y_ready, t - 3)
                    for k in range(KT):
                        last = pe.transpose(bank(2 * (t % 4), 2)[:, k * P:(k + 1) * P], hT[:, k, t * P:(t + 1) * P], ident[:])
                    last.then_inc(turned, 1)

            @block.scalar
            def _(act):
                for t in range(NT):
                    act.wait_ge(turned, t + 1)
                    act.activation(yout[:, t, :], bank(2 * (t % 4), 2), ACT.Copy).then_inc(y_ready, 1)

            @block.sync
            def _(sp):
                sp.wait_ge(y_ready, 4)
                sp.dma_start(a["y_prompt"].rearrange("o (t p) d -> p (o t) d", p=P), yout[:, 0:4, :]).then_inc(out_sem, 16)
                sp.wait_ge(y_ready, 5)
                sp.dma_start(a["y_sample"].rearrange("b t d -> (b t) d"), yout[:, 4, :]).then_inc(out_sem, 16)
                sp.wait_ge(out_sem, 32)


_INS = ["x_prompt", "x_sample", "c_prompt", "c_sample", "state_ssd", "state_ssd_conv", "state_lru", "state_lru_conv",
        "ln1_w", "ln2_w", "w_mod", "b_mod", "w_in", "ssd_conv_w", "ssd_conv_b", "ssd_dt_bias", "ssd_a_log", "ssd_d",
        "ssd_norm_w", "lru_conv_w", "lru_conv_b", "lru_wa", "lru_ba", "lru_wx", "lru_bx", "lru_lambda", "w_br_ssd",
        "w_br_lru", "w_out", "peer_wq", "peer_k1", "peer_k2", "peer_u", "peer_v", "final_norm_w"]
_OUTS = [("y_prompt", (1, SEQ, D)), ("y_sample", (STREAMS, SLEN, D)),
         ("new_ssd_prompt", (DEPTH, 1, HEADS, HD, NS)), ("new_ssd_conv_prompt", (DEPTH, 1, HIST, CONVC)),
         ("new_lru_prompt", (DEPTH, 1, D)), ("new_lru_conv_prompt", (DEPTH, 1, HIST, D)),
         ("new_ssd_sample", (DEPTH, STREAMS, HEADS, HD, NS)), ("new_ssd_conv_sample", (DEPTH, STREAMS, HIST, CONVC)),
         ("new_lru_sample", (DEPTH, STREAMS, D)), ("new_lru_conv_sample", (DEPTH, STREAMS, HIST, D))]


def kernel(**inputs):
    import numpy as _np
    import concourse.bacc as _bacc
    from concourse.bass_utils import run_bass_kernel_spmd as _run

    nc = _bacc.Bacc("TRN2", target_bir_lowering=False, num_devices=1)
    arrays, args = {}, {}
    for name in _INS:
        x = _np.ascontiguousarray(inputs[name])
        arrays["in_" + name] = x
        args[name] = nc.dram_tensor("in_" + name, x.shape, F32, kind="ExternalInput").ap()
    for name, shape in _OUTS:
        args[name] = nc.dram_tensor("out_" + name, shape, F32, kind="ExternalOutput").ap()
    build(nc, args)
    r = _run(nc, [arrays], core_ids=[0])
    return tuple(r.results[0]["out_" + name] for name, _ in _OUTS)
```

```python
import concourse.bass as bass
from concourse import mybir
from contextlib import ExitStack

F32 = mybir.dt.float32
U32 = mybir.dt.uint32
ALU = mybir.AluOpType
ACT = mybir.ActivationFunctionType
AX = mybir.AxisListType
ds = bass.ds

DEPTH, D, P = 2, 1024, 128
KT = D // P
SEQ, STREAMS, SLEN = 512, 8, 16
TT = SEQ + STREAMS * SLEN
NT = TT // P
NB = TT // SLEN
HEADS, HD, NS = 16, 64, 64
CONVC = D + 4 * NS
W = 4
HIST = W - 1
EPS = 1e-6
PH, KEYS, TOPK = 8, 128, 16
PICKS = PH * TOPK
Z0, X0, DT0, LX0, LY0, GS0, GL0 = 0, D, D + CONVC, D + CONVC + HEADS, 2 * D + CONVC + HEADS, 3 * D + CONVC + HEADS, \
    4 * D + CONVC + HEADS
NEG = -3.0e38

SLOTS = 8
RING, HALF = 16, 8
BATCHES = PICKS // RING
SHARED = 2
SHARE = (BATCHES - SHARED) * RING // 4

W_CONV_SSD, W_CONV_LRU, W_SSD, W_LRU = 32, 64, 64 + 18 * 16, 96 + 18 * 16

LN1, LN2, NW, BA, BX, LAM, LCB, LCW, SCB = 0, 8, 16, 24, 32, 40, 48, 56, 88
ROWS_A = 98
SCW, BMOD, FIN, DD = ROWS_A, ROWS_A + 40, ROWS_A + 88, ROWS_A + 96
ROWS_B = 104
H0 = ROWS_A + ROWS_B
CV = H0 + 64
NCOLS = CV + 72


def build(nc, a):
    ctx = ExitStack()
    with ctx:
        def sb(name, shape, dt=F32):
            return ctx.enter_context(nc.sbuf_tensor(name, shape, dt))

        gathered = [ctx.enter_context(nc.semaphore(f"gathered_{n}")) for n in range(RING)]
        written = ctx.enter_context(nc.semaphore("states_written"))
        nums = []

        def sem(name):
            s = ctx.enter_context(nc.semaphore(name))
            nums.append(s.num)
            return s

        names = {}

        def phase_sem(name):
            if name not in names:
                names[name] = sem(name)
            return names[name]

        xT = sb("xT", [P, KT, TT])
        hT = sb("hT", [P, KT, TT])
        modE = sb("modE", [P, 6 * KT, NB])
        cols = sb("cols", [P, NCOLS])
        ident = sb("ident", [P, P])
        ones = sb("ones", [P, P])
        zeros = sb("zeros", [P, P])
        upto = [sb(f"upto{s}", [P, P]) for s in range(2)]
        after = [sb(f"after{s}", [P, P]) for s in range(2)]
        stream_of = sb("stream_of", [P, STREAMS])
        iota16 = sb("iota16", [P, TOPK])
        layer_row = sb("layer_row", [P, DEPTH])
        alog = sb("alog", [P, HEADS])
        dtb = sb("dtb", [P, HEADS])
        negA = sb("negA", [P, HEADS])
        dt = sb("dt", [P, NT, HEADS])
        dta = sb("dta", [P, NT, HEADS])
        spw = sb("spw", [P, 4, NT * HEADS])
        lamS = sb("lamS", [P, KT])
        stT = sb("stT", [P, 8 * HD])
        lruN = sb("lruN", [P, KT, 9])
        rowbuf = sb("rowbuf", [P, 2, P])
        small = sb("small", [P, 48])
        arenaR = sb("arenaR", [P, RING * D])
        arenaQ = sb("arenaQ", [P, 18 * TT])
        arenaW = sb("arenaW", [P, SLOTS * D])
        arenaX = sb("arenaX", [P, 2048])
        psum = ctx.enter_context(nc.psum_tensor("psum", [P, 8, 512], F32))

        def view(arena, at, *shape):
            n = 1
            for s in shape:
                n *= s
            v = arena[:, at:at + n]
            if len(shape) == 2:
                return v.rearrange("p (a b) -> p a b", a=shape[0])
            if len(shape) == 3:
                return v.rearrange("p (a b c) -> p a b c", a=shape[0], b=shape[1])
            return v

        wt = view(arenaW, 0, SLOTS, KT, P)
        rs = arenaQ[:, 9 * TT:10 * TT]
        ysT = view(arenaR, 0, KT, TT)
        ylT = view(arenaR, KT * TT, KT, TT)
        mT = view(arenaR, 2 * KT * TT, KT, TT)
        xbcT = view(arenaQ, 0, 10, TT)
        lxT = view(arenaQ, 10 * TT, KT, TT)

        def bank(b, n=1):
            return psum[:, b:b + n, :].rearrange("p b c -> p (b c)")

        def weight(name, l, col):
            w = a[name].rearrange("l (k p) c -> p (l k) c", p=P)
            return w[:, ds(l * KT, KT), ds(col, P)]

        def fetch_ahead(sp, l, name, col, slot, n=2):
            for u in range(n):
                sp.dma_start(wt[:, slot + u, :, :], weight(name, l, col + u * P)).then_inc(phase_sem("fetched_ahead"), 16)

        def finish_ahead(sp, n=2):
            sp.wait_ge(phase_sem("fetched_ahead"), 16 * n)

        def have_first(sp, wready):
            for s in wready:
                sp.sem_inc(s, 16)

        def project(slot, src, out, between=None):
            for o, n in ((0, SEQ), (SEQ, TT - SEQ)):
                for k in range(KT):
                    last = nc.tensor.matmul(out[:, o:o + n], wt[:, slot, k, :], src[:, k, o:o + n],
                                            start=k == 0, stop=k == KT - 1)
                    if between and o == 0:
                        between(k)
            return last

        class Steps:

            def __init__(self, eng, name, base=0):
                self.eng, self.sem, self.base, self.n = eng, phase_sem(name), base, 0

            def __call__(self, ins):
                ins.then_inc(self.sem, 1)
                self.n += 1

            def wait(self, eng=None):
                (eng or self.eng).wait_ge(self.sem, self.base + self.n)

            def hold(self):
                hold(self.eng, self.sem, self.base + self.n)

        def hold(eng, s, value):
            eng.wait_ge(s, value)
            eng.sem_inc(phase_sem("held"), 1)

        def end_phase():
            nc.all_engine_barrier(sems_to_clear=range(min(nums), max(nums) + 1))

        def b16(ap, n=SLEN):
            return ap.unsqueeze(len(ap.shape)).to_broadcast([*ap.shape, n])

        def softplus(dve, st, ready, x, n, out, work):
            ax, z, z2, q = (work[:, i, 0:n] for i in range(4))
            st(dve.scalar_tensor_tensor(ax, x, -1.0, x, ALU.mult, ALU.min))
            st.wait()
            dve.sem_inc(ready[0], 1)
            dve.wait_ge(ready[1], 1)
            st(dve.tensor_scalar(z, ax, 2.0, None, ALU.add))
            st.wait()
            st(dve.reciprocal(z2, z))
            st.wait()
            st(dve.tensor_tensor(z, ax, z2, ALU.mult))
            st.wait()
            st(dve.tensor_tensor(z2, z, z, ALU.mult))
            st(dve.memset(q, 1.0 / 17))
            st.wait()
            first = True
            for c in (15, 13, 11, 9, 7, 5, 3):
                if first:
                    st(dve.tensor_tensor(q, q, z2, ALU.mult))
                    first = False
                    st.wait()
                st(dve.scalar_tensor_tensor(q, q, 1.0 / c, z2, ALU.add, ALU.mult))
                st.wait()
            st(dve.scalar_tensor_tensor(q, q, 1.0, z, ALU.add, ALU.mult))
            st(dve.tensor_scalar(z2, x, 0.0, None, ALU.max))
            st.wait()
            st(dve.scalar_tensor_tensor(out, q, 2.0, z2, ALU.mult, ALU.add))
            st.wait()

        def modulation(dve, st, mod_done, sums, lo, hi):
            n = hi - lo
            src = sums[:, 0:n * 9].rearrange("p (c s) -> p c s", s=9)
            bias = cols[:, BMOD + lo:BMOD + hi].unsqueeze(2)
            for b0, b1, v in ((0, 32, src[:, :, 0:1].to_broadcast([P, n, 32])), (32, 40, src[:, :, 1:9])):
                dve.tensor_tensor(modE[:, lo:hi, b0:b1], v, bias.to_broadcast([P, n, b1 - b0]), ALU.add).then_inc(mod_done, 1)
            dve.wait_ge(mod_done, 2)

        def norm_scale(dve, st, at, ln):
            v = modE[:, at:at + KT, :]
            st(dve.scalar_tensor_tensor(v, v, 1.0, cols[:, ln:ln + KT].unsqueeze(2).to_broadcast([P, KT, NB]), ALU.add, ALU.mult))
            st.wait()

        xin = view(arenaR, 0, NT, D)
        x_loaded, s_const, tiles_turned, tiles_copied = (sem(n) for n in ("x_loaded", "s_const", "tiles_turned", "tiles_copied"))
        with nc.Block() as block:
            @block.sync
            def _(sp):
                sp.dma_start(xin[:, 0:4, :], a["x_prompt"].rearrange("o (t p) d -> p (o t) d", p=P)).then_inc(x_loaded, 16)
                sp.dma_start(xin[:, 4, :], a["x_sample"].rearrange("b t d -> (b t) d")).then_inc(x_loaded, 16)

            @block.gpsimd
            def _(pool):
                n = 0

                def put(ins):
                    nonlocal n
                    ins.then_inc(s_const, 1)
                    n += 1

                put(pool.memset(ident[:], 1.0))
                put(pool.memset(ones[:], 1.0))
                put(pool.memset(zeros[:], 0.0))
                put(pool.memset(stream_of[:], 1.0))
                put(pool.iota(iota16[:], [[1, TOPK]], base=0, channel_multiplier=0, allow_small_or_imprecise_dtypes=True))
                put(pool.iota(layer_row[:], [[KEYS * KEYS, DEPTH]], base=0, channel_multiplier=0, allow_small_or_imprecise_dtypes=True))
                pool.wait_ge(s_const, n)
                put(pool.affine_select(out=ident[:], in_=ident[:], compare_op=ALU.is_equal, fill=0.0, base=0,
                                       pattern=[[-1, P]], channel_multiplier=1))
                for s in range(2):
                    put(pool.affine_select(out=upto[s][:], in_=ones[:], compare_op=ALU.is_ge, fill=0.0, base=0,
                                           pattern=[[1, P]], channel_multiplier=-1))
                    put(pool.affine_select(out=after[s][:], in_=ones[:], compare_op=ALU.is_ge, fill=0.0, base=-1,
                                           pattern=[[-1, P]], channel_multiplier=1))
                put(pool.affine_select(out=stream_of[:], in_=stream_of[:], compare_op=ALU.is_ge, fill=0.0, base=0,
                                       pattern=[[-SLEN, STREAMS]], channel_multiplier=1))
                pool.wait_ge(s_const, n)
                put(pool.affine_select(out=stream_of[:], in_=stream_of[:], compare_op=ALU.is_ge, fill=0.0,
                                       base=SLEN - 1, pattern=[[SLEN, STREAMS]], channel_multiplier=-1))
                put(pool.affine_select(out=upto[1][:], in_=upto[1][:], compare_op=ALU.is_ge, fill=0.0, base=0,
                                       pattern=[[-SLEN, STREAMS], [0, SLEN]], channel_multiplier=1))
                put(pool.affine_select(out=after[1][:], in_=after[1][:], compare_op=ALU.is_ge, fill=0.0,
                                       base=SLEN - 1, pattern=[[SLEN, STREAMS], [0, SLEN]], channel_multiplier=-1))
                pool.wait_ge(s_const, n)

            @block.tensor
            def _(pe):
                pe.wait_ge(x_loaded, 32)
                pe.wait_ge(s_const, 15)
                for t in range(NT):
                    if t >= 4:
                        pe.wait_ge(tiles_copied, t - 3)
                    o = bank(2 * (t % 4), 2)
                    for k in range(KT):
                        last = pe.transpose(o[:, k * P:(k + 1) * P], xin[:, t, k * P:(k + 1) * P], ident[:])
                    last.then_inc(tiles_turned, 1)

            @block.vector
            def _(dve):
                for t in range(NT):
                    dve.wait_ge(tiles_turned, t + 1)
                    dve.tensor_copy(xT[:, :, t * P:(t + 1) * P],
                                    bank(2 * (t % 4), 2).rearrange("p (k c) -> p k c", k=KT)).then_inc(tiles_copied, 1)
                dve.wait_ge(tiles_copied, NT)
        end_phase()

        def norm_phase(out, scale, shift, ahead=None):
            sq = view(arenaR, 2 * KT * TT, KT, TT)
            rs = arenaX[:, 0:TT]
            with nc.Block() as block:
                squared, summed, rooted, ready, scaled, modulated = (phase_sem(n) for n in (
                    "squared", "summed", "rooted", "root_in", "scaled", "modulated"))

                @block.sync
                def _(sp):
                    if ahead:
                        fetch_ahead(sp, *ahead)
                        finish_ahead(sp)

                @block.scalar
                def _(act):
                    for k in range(KT):
                        act.activation(sq[:, k, :], xT[:, k, :], ACT.Square).then_inc(squared, 1)
                    act.wait_ge(ready, 1)
                    act.activation(rs, rs, ACT.Sqrt).then_inc(rooted, 1)
                    for k in range(KT):
                        act.wait_ge(scaled, k + 1)
                        if shift is None:
                            v = out[:, k, :]
                            ins = act.activation(v, v, ACT.Copy, scale=scale[:, k:k + 1])
                        else:
                            v = out[:, k, 0:SEQ]
                            ins = act.activation(v, v, ACT.Identity, scale=scale[:, k, 0:1], bias=shift[:, k, 0:1])
                        ins.then_inc(modulated, 1)

                @block.tensor
                def _(pe):
                    o = bank(0, 2)
                    for k in range(KT):
                        pe.wait_ge(squared, k + 1)
                        for at, n in ((0, SEQ), (SEQ, TT - SEQ)):
                            last = pe.matmul(o[:, at:at + n], ones[:], sq[:, k, at:at + n], start=k == 0,
                                             stop=k == KT - 1)
                    last.then_inc(summed, 1)

                @block.vector
                def _(dve):
                    st = Steps(dve, "dve_step")
                    dve.wait_ge(summed, 1)
                    dve.tensor_scalar(rs, bank(0, 2)[:, 0:TT], 1.0 / D, EPS, ALU.mult, ALU.add).then_inc(ready, 1)
                    dve.wait_ge(rooted, 1)
                    st(dve.reciprocal(rs, rs))
                    st.wait()
                    for k in range(KT):
                        dve.tensor_tensor(out[:, k, :], xT[:, k, :], rs, ALU.mult).then_inc(scaled, 1)
                    if shift is not None:
                        dve.wait_ge(scaled, KT)
                        v = out[:, :, SEQ:TT].rearrange("p k (b t) -> p k b t", t=SLEN)
                        st(dve.tensor_tensor(v, v, b16(scale[:, :, 32:40]), ALU.mult))
                        st.wait()
                        st(dve.tensor_tensor(v, v, b16(shift[:, :, 32:40]), ALU.add))
                        st.wait()
            end_phase()

        with nc.Fori(0, DEPTH) as l:
            with nc.Block() as block:
                d2 = small[96:104, 0:2]
                rowsD = arenaX[:, 0:P]
                rowsC = arenaX[:, P:2 * P]
                loaded, d_spread, silued, turned, colsd = (phase_sem(n) for n in (
                    "vectors_loaded", "d_spread", "c_silued", "vectors_turned", "vectors_ready"))
                slab = view(arenaR, 0, KT, 2 * D)
                mod_rows = view(arenaQ, 0, 2 * D)
                slab_in = [phase_sem(f"slab_in_{k}") for k in range(KT)]
                mod_sum, mod_copied, mod_turned, mod_done = (phase_sem(n) for n in (
                    "mod_sum", "mod_copied", "mod_turned", "mod_done"))
                ex_in, ex_out = phase_sem("exp_in"), phase_sem("exp_out")

                def rows(name, n, spec="l (k c) -> (l k) c"):
                    return a[name].rearrange(spec, c=P)[ds(l * n, n), :]

                @block.sync
                def _(sp):
                    for r, at, src in (
                        (0, LN1, rows("ln1_w", 8)), (0, LN2, rows("ln2_w", 8)), (0, NW, rows("ssd_norm_w", 8)),
                        (0, BA, rows("lru_ba", 8)), (0, BX, rows("lru_bx", 8)), (0, LAM, rows("lru_lambda", 8)),
                        (0, LCB, rows("lru_conv_b", 8)), (0, LCW, rows("lru_conv_w", 32, "l w (k c) -> (l w k) c")),
                        (0, SCB, rows("ssd_conv_b", 10)),
                    ):
                        sp.dma_start(rowbuf[at:at + src.shape[0], r, :], src).then_inc(loaded, 16)

                @block.scalar
                def _(act):
                    for at, src in ((0, rows("ssd_conv_w", 40, "l w (k c) -> (l w k) c")), (40, rows("b_mod", 48)),
                                    (88, a["final_norm_w"].rearrange("(k c) -> k c", c=P))):
                        act.dma_start(rowbuf[at:at + src.shape[0], 1, :], src).then_inc(loaded, 16)
                    act.dma_start(rowsC[0:64, :], rows("state_lru", 64, "l b (k c) -> (l b k) c")).then_inc(loaded, 16)
                    act.dma_start(rowsD[0:8, :], a["c_prompt"].rearrange("s (k c) -> (s k) c", c=P)).then_inc(loaded, 16)
                    act.dma_start(rowsD[8:72, :], a["c_sample"].rearrange("s (k c) -> (s k) c", c=P)).then_inc(loaded, 16)
                    act.dma_start(d2, a["ssd_d"].rearrange("l (j h) -> (l j) h", h=2)[ds(l * 8, 8), :]).then_inc(loaded, 16)
                    act.dma_start(alog[:], a["ssd_a_log"][ds(l, 1), :].to_broadcast([P, HEADS])).then_inc(loaded, 16)
                    act.dma_start(dtb[:], a["ssd_dt_bias"][ds(l, 1), :].to_broadcast([P, HEADS])).then_inc(loaded, 16)
                    for k in range(KT):
                        act.dma_start(slab[:, k, :], a["w_mod"].rearrange("l r c -> (l r) c")
                                      [ds(l * D + k * P, P), 0:2 * D]).then_inc(slab_in[k], 16)
                    act.wait_ge(loaded, 18 * 16)
                    act.activation(rowsD[0:72, :], rowsD[0:72, :], ACT.Silu).then_inc(silued, 1)
                    act.activation(negA[:], alog[:], ACT.Exp).then_inc(silued, 1)
                    act.wait_ge(ex_in, 1)
                    act.activation(spw[:, 0, 0:KT], spw[:, 0, 0:KT], ACT.Exp).then_inc(ex_out, 1)
                    act.wait_ge(mod_sum, 1)
                    act.activation(mod_rows[0:9, 0:D], bank(0, 2)[0:9, :], ACT.Copy).then_inc(mod_copied, 1)

                @block.tensor
                def _(pe):
                    pe.wait_ge(loaded, 18 * 16)
                    pe.wait_ge(silued, 1)
                    pe.wait_ge(d_spread, 1)
                    pe.transpose(bank(7)[:, 0:ROWS_A], rowbuf[0:ROWS_A, 0, :], ident[0:ROWS_A, 0:ROWS_A])
                    pe.transpose(bank(7)[:, ROWS_A:H0], rowbuf[0:ROWS_B, 1, :], ident[0:ROWS_B, 0:ROWS_B])
                    pe.transpose(bank(7)[:, H0:CV], rowsC[0:64, :], ident[0:64, 0:64])
                    pe.transpose(bank(7)[:, CV:NCOLS], rowsD[0:72, :], ident[0:72, 0:72]).then_inc(turned, 1)
                    pe.wait_ge(colsd, 1)
                    cT = cols[:, CV:NCOLS].rearrange("p (s k) -> p k s", k=KT)
                    for k in range(KT):
                        pe.wait_ge(slab_in[k], 16)
                        for i in range(4):
                            last = pe.matmul(bank(i)[0:9, :], cT[:, k, :], slab[:, k, i * 512:(i + 1) * 512],
                                             start=k == 0, stop=k == KT - 1)
                    last.then_inc(mod_sum, 1)
                    pe.wait_ge(mod_copied, 2)
                    for c in range(2 * KT):
                        last = pe.transpose(bank(4)[:, c * 9:c * 9 + 9], mod_rows[0:9, c * P:(c + 1) * P], ident[0:9, 0:9])
                    last.then_inc(mod_turned, 1)

                @block.vector
                def _(dve):
                    st = Steps(dve, "dve_step")
                    dve.wait_ge(loaded, 18 * 16)
                    dve.tensor_copy(rowbuf[96:104, 1, :].rearrange("p (h c) -> p h c", h=2), b16(d2, HD)).then_inc(d_spread, 1)
                    dve.wait_ge(turned, 1)
                    dve.tensor_copy(cols[:], bank(7)[:, 0:NCOLS]).then_inc(colsd, 1)
                    dve.wait_ge(silued, 2)
                    st(dve.tensor_scalar(negA[:], negA[:], -1.0, None, ALU.mult))
                    dve.wait_ge(colsd, 1)
                    lam = spw[:, 0, 16:16 + KT]
                    st(dve.tensor_scalar(lam, cols[:, LAM:LAM + KT], -1.0, None, ALU.mult))
                    st.wait()
                    softplus(dve, st, (ex_in, ex_out), lam, KT, lamS[:], spw)
                    st(dve.tensor_scalar(lamS[:], lamS[:], -4.0, None, ALU.mult))
                    dve.wait_ge(mod_sum, 1)
                    dve.tensor_copy(mod_rows[0:9, D:2 * D], bank(2, 2)[0:9, :]).then_inc(mod_copied, 1)
                    dve.wait_ge(mod_turned, 1)
                    modulation(dve, st, mod_done, bank(4), 0, 2 * KT)
                    norm_scale(dve, st, KT, LN1)
            end_phase()

            norm_phase(hT[:], modE[:, KT:2 * KT, :], modE[:, 0:KT, :], (l, "w_in", X0, 6))

            def conv_phase(col0, tiles, dst, wcol, bcol, state, C, new_p, new_s, silu, with_dt, slot0, ahead=None):
                PADC = HIST + SEQ + STREAMS * (HIST + SLEN)
                xpad = view(arenaR, 0, 2, PADC + 1)
                acc = view(arenaR, 2 * (PADC + 1), 2, PADC + 1)
                pre = view(arenaR, 4 * (PADC + 1), 2, TT)
                hist = view(arenaR, 4 * (PADC + 1) + 2 * TT, 2, P)
                last27 = view(arenaR, 4 * (PADC + 1) + 2 * TT + 2 * P, 2, 27)
                newrow = view(arenaW, 4096, C)
                wdt = view(arenaR, 12288, KT, HEADS)
                dt_rows = arenaX[0:HEADS, 0:TT]
                sample = lambda v: v[:, HIST + SEQ:PADC].rearrange("p (b t) -> p b t", b=STREAMS)
                loops = tiles // 2
                NY = PADC - HIST
                with nc.Block() as block:
                    wready = [phase_sem(f"weight_ready_{s}") for s in range(2)]
                    hready = [phase_sem(f"history_ready_{s}") for s in range(2)]
                    proj_done, hist_done, padded, tails, tails_done, stored = (phase_sem(n) for n in (
                        "projected", "history_turned", "padded", "tails", "tails_turned", "tails_stored"))
                    conved, silued, wdt_ready, dt_done, zeroed = (phase_sem(n) for n in (
                        "convolved", "silued", "wdt_ready", "dt_projected", "zeroed"))
                    ex_in, ex_out = phase_sem("exp_in"), phase_sem("exp_out")

                    @block.sync
                    def _(sp):
                        if with_dt:
                            sp.dma_start(wdt, a["w_in"].rearrange("l (k p) c -> p (l k) c", p=P)[:, ds(l * KT, KT), DT0:DT0 + HEADS])\
                              .then_inc(wdt_ready, 16)
                        have_first(sp, wready)
                        sp.sem_inc(proj_done, 2)
                        sp.sem_inc(hist_done, 2)

                        def history(j, u):
                            sp.dma_start(hist[0:24, u, :], state.rearrange("l b w c -> (l b w) c")
                                         [ds(l * 24, 24), ds(j * (2 * P) + u * P, P)]).then_inc(hready[u], 16)

                        for u in range(2):
                            history(0, u)
                        if ahead:
                            fetch_ahead(sp, *ahead)
                        with sp.Fori(1, loops) as j:
                            for u in range(2):
                                sp.wait_ge(proj_done, 2 * j + u + 1)
                                sp.dma_start(wt[:, slot0 + u, :, :], weight("w_in", l, col0 + j * (2 * P) + u * P)).then_inc(wready[u], 16)
                                sp.wait_ge(hist_done, 2 * j + u + 1)
                                history(j, u)
                        sp.wait_ge(stored, 2 + tiles)
                        sp.dma_start(new_p.rearrange("l b w c -> (l b w) c")[ds(l * 3, 3), :], newrow[0:3, :]).then_inc(written, 16)
                        sp.dma_start(new_s.rearrange("l b w c -> (l b w) c")[ds(l * 24, 24), :], newrow[3:27, :]).then_inc(written, 16)
                        if ahead:
                            finish_ahead(sp)

                    @block.tensor
                    def _(pe):
                        if with_dt:
                            pe.wait_ge(wdt_ready, 16)
                            for o, n in ((0, SEQ), (SEQ, TT - SEQ)):
                                for k in range(KT):
                                    last = pe.matmul(bank(4, 2)[0:HEADS, o:o + n], wdt[:, k, :], hT[:, k, o:o + n],
                                                     start=k == 0, stop=k == KT - 1)
                            last.then_inc(phase_sem("dt_heads"), 1)
                            pe.wait_ge(phase_sem("dt_rows"), 1)
                            for t in range(NT):
                                last = pe.transpose(bank(7)[:, t * HEADS:(t + 1) * HEADS], dt_rows[:, t * P:(t + 1) * P],
                                                    ident[0:HEADS, 0:HEADS])
                            last.then_inc(dt_done, 1)
                        pe.sem_inc(padded, 2)
                        pe.sem_inc(stored, 2)
                        with pe.Fori(0, loops) as j:
                            for u in range(2):
                                pe.wait_ge(wready[u], j * 16 + 16)
                                pe.wait_ge(padded, 2 * j + u + 1)
                                project(slot0 + u, hT, bank(2 * u, 2)).then_inc(proj_done, 1)
                                hold(pe, hready[u], j * 16 + 16)
                                pe.transpose(bank(2 * u, 2)[:, TT:TT + 24], hist[0:24, u, :], ident[0:24, 0:24])\
                                  .then_inc(hist_done, 1)
                            for u in range(2):
                                pe.wait_ge(tails, 2 * j + u + 1)
                                pe.wait_ge(stored, 2 * j + u + 1)
                                pe.transpose(bank(5 + u)[0:27, 0:P], last27[:, u, :], ident[:]).then_inc(tails_done, 1)

                    @block.scalar
                    def _(act):
                        if with_dt:
                            act.wait_ge(phase_sem("dt_heads"), 1)
                            act.activation(dt_rows, bank(4, 2)[0:HEADS, 0:TT], ACT.Copy).then_inc(phase_sem("dt_rows"), 1)
                            act.wait_ge(ex_in, 1)
                            act.activation(spw[:, 0, :], spw[:, 0, :], ACT.Exp).then_inc(ex_out, 1)
                        act.sem_inc(conved, 2)
                        act.wait_ge(zeroed, 1)
                        if not with_dt:
                            hold(act, written, l * W_LRU + W_CONV_SSD)
                        filled = phase_sem("filled")
                        with act.Fori(0, loops) as j:
                            for u in range(2):
                                act.wait_ge(hist_done, 2 + 2 * j + u + 1)
                                act.wait_ge(conved, 2 * j + u + 1)
                                o = bank(2 * u, 2)
                                act.activation(xpad[:, u, HIST:HIST + SEQ], o[:, 0:SEQ], ACT.Copy).then_inc(filled, 1)
                                act.activation(sample(xpad[:, u, :])[:, :, 0:HIST],
                                               o[:, TT:TT + 24].rearrange("p (b t) -> p b t", b=STREAMS),
                                               ACT.Copy).then_inc(filled, 1)
                                act.activation(sample(xpad[:, u, :])[:, :, HIST:], o[:, SEQ:TT].rearrange("p (b t) -> p b t", b=STREAMS),
                                               ACT.Copy).then_inc(padded, 1)
                            for u in range(2):
                                act.wait_ge(tails_done, 2 * j + u + 1)
                                act.activation(newrow[0:27, ds(j * (2 * P) + u * P, P)], bank(5 + u)[0:27, 0:P], ACT.Copy)\
                                   .then_inc(stored, 1)
                                if silu:
                                    act.wait_ge(conved, 2 + 2 * j + u + 1)
                                    act.activation(dst[:, ds(2 * j + u, 1), :], pre[:, u:u + 1, :], ACT.Silu).then_inc(silued, 1)
                        if silu:
                            act.wait_ge(silued, 2 + tiles)

                    @block.vector
                    def _(dve):
                        st = Steps(dve, "dve_step")
                        for u in range(2):
                            st(dve.memset(xpad[:, u, 0:HIST], 0.0))
                        st.wait()
                        dve.sem_inc(zeroed, 1)
                        if with_dt:
                            dve.wait_ge(dt_done, 1)
                            v = dt[:].rearrange("p t h -> p (t h)")
                            st(dve.tensor_tensor(dt[:], bank(7)[:, 0:NT * HEADS].rearrange("p (t h) -> p t h", t=NT),
                                                 dtb[:].unsqueeze(1).to_broadcast([P, NT, HEADS]), ALU.add))
                            st.wait()
                            softplus(dve, st, (ex_in, ex_out), v, NT * HEADS, v, spw)
                            st(dve.tensor_tensor(dta[:], dt[:], negA[:].unsqueeze(1).to_broadcast([P, NT, HEADS]), ALU.mult))
                        filled = phase_sem("filled")
                        if silu:
                            dve.sem_inc(silued, 2)
                        PER = 10
                        with dve.Fori(0, loops) as j:
                            st = Steps(dve, "conv_step", j * PER)
                            for u in range(2):
                                dve.wait_ge(filled, 4 * j + 2 * u + 2)
                                dve.wait_ge(padded, 2 + 2 * j + u + 1)
                                x, y = xpad[:, u, :], acc[:, u, 0:NY]
                                st(dve.tensor_copy(last27[:, u, 0:3], x[:, SEQ:SEQ + HIST]))
                                dve.tensor_copy(last27[:, u, 3:27].rearrange("p (b t) -> p b t", b=STREAMS),
                                                sample(x)[:, :, SLEN:]).then_inc(tails, 1)
                                dve.wait_ge(tails, 2 * j + u + 1)
                                w = lambda k: cols[:, ds(wcol + k * tiles + 2 * j + u, 1)]
                                st(dve.tensor_scalar(y, x[:, 0:NY], w(0), cols[:, ds(bcol + 2 * j + u, 1)], ALU.mult, ALU.add))
                                st.wait()
                                for k in (1, 2):
                                    st(dve.scalar_tensor_tensor(y, x[:, k:k + NY], w(k), y, ALU.mult, ALU.add))
                                    st.wait()
                                if silu:
                                    dve.wait_ge(silued, 2 * j + u + 1)
                                    to = pre[:, u, :]
                                else:
                                    to = dst[:, ds(2 * j + u, 1), :].rearrange("p o t -> p (o t)")
                                st(dve.scalar_tensor_tensor(to[:, 0:SEQ], x[:, HIST:HIST + SEQ], w(3), y[:, 0:SEQ], ALU.mult, ALU.add))
                                ysam = acc[:, u, HIST + SEQ:HIST + SEQ + STREAMS * (HIST + SLEN)].rearrange("p (b t) -> p b t", b=STREAMS)
                                dve.scalar_tensor_tensor(to[:, SEQ:TT].rearrange("p (b t) -> p b t", b=STREAMS),
                                                         sample(x)[:, :, HIST:], w(3), ysam[:, :, 0:SLEN],
                                                         ALU.mult, ALU.add).then_inc(conved, 1)
                            assert st.n == PER, st.n
                        dve.wait_ge(conved, 2 + tiles)
                        dve.wait_ge(phase_sem("conv_step"), loops * PER)
                end_phase()

            conv_phase(X0, 10, xbcT, SCW, SCB, a["state_ssd_conv"], CONVC, a["new_ssd_conv_prompt"],
                       a["new_ssd_conv_sample"], True, True, 6, (l, "w_in", LX0, 0))
            conv_phase(LX0, 8, lxT, LCW, LCB, a["state_lru_conv"], D, a["new_lru_conv_prompt"],
                       a["new_lru_conv_sample"], False, False, 0)

            at = KT * TT
            parts = {}
            for name, n in (("xc", 10 * P), ("mdta", 2048), ("E", 2048), ("Ea", 2048), ("Cw", 2048),
                            ("xw", 1024), ("cbm", 256), ("Btok", P)):
                parts[name] = (at, n)
                at += n
            assert at <= RING * D
            V = lambda n, *s: view(arenaR, parts[n][0], *s)
            xc, mdta, E, Ea = V("xc", 10, P), V("mdta", HEADS, P), V("E", HEADS, P), V("Ea", HEADS, P)
            Cw, xw, cbm, Btok = V("Cw", HEADS, P), V("xw", HEADS, HD), V("cbm", 2, P), V("Btok", P)
            xdt = view(arenaX, 0, HEADS, HD)
            Cz = view(arenaX, 1024, 2, P)
            stN = view(arenaW, 0, STREAMS * 4, P)
            stTb = view(arenaW, 4096, STREAMS, 4 * P)
            Bm = view(arenaR, parts["mdta"][0], 2, STREAMS * NS)
            dtax = view(arenaX, 1024, HEADS, HD)
            ex = small[:, 0:48]
            with nc.Block() as block:
                S = {n: phase_sem("ssd_" + n) for n in (
                    "staged", "turned", "cb", "mdta", "seg", "E", "acb", "Ea", "ex", "xdt", "xw", "cbm", "W",
                    "Cw", "y", "stadd", "ydone", "state", "Btok", "st_in", "st_turned", "st_copied", "dtax", "dec",
                    "decE", "Bm", "cz", "zeroed", "sadd", "sadded")}
                misc = bank(6)
                stN_parts = stN.rearrange("p (b j) (g n) -> p b j g n", j=4, g=2)
                PX = bank(4, 2)
                Y = bank(2, 2)

                def state_view(name):
                    return a[name].rearrange("l b (j hh) p n -> (hh p) (l b j) n", hh=2)

                @block.sync
                def _(sp):
                    v = stN.rearrange("p (b j) (g n) -> p b j g n", j=4, g=2)
                    src = state_view("state_ssd")
                    for b in range(STREAMS):
                        for g in range(2):
                            sp.dma_start(v[:, b, :, g, :], src[:, ds(l * 64 + b * 8 + g * 4, 4), :]).then_inc(S["st_in"], 16)
                    dst = state_view("new_ssd_sample")
                    sp.wait_ge(S["y"], 6)
                    fetch_ahead(sp, l, "w_in", Z0, 4)
                    sp.wait_ge(S["stadd"], 5)
                    pv = E[:, 0:4, :].rearrange("p j (g n) -> p j g n", g=2)
                    dp = a["new_ssd_prompt"].rearrange("l b (j hh) p n -> (hh p) (l b j) n", hh=2)
                    for g in range(2):
                        sp.dma_start(dp[:, ds(l * 8 + g * 4, 4), :], pv[:, :, g, :]).then_inc(written, 16)
                    sp.wait_ge(S["sadded"], 4)
                    for b in range(STREAMS):
                        sp.dma_start(dst[:, ds(l * 64 + b * 8, 4), :], v[:, b, :, 0, :]).then_inc(written, 16)
                    sp.wait_ge(S["sadded"], 8)
                    for b in range(STREAMS // 2, STREAMS):
                        sp.dma_start(dst[:, ds(l * 64 + b * 8 + 4, 4), :], v[:, b, :, 1, :]).then_inc(written, 16)
                    finish_ahead(sp)

                @block.gpsimd
                def _(pool):
                    def stage(t):
                        pool.tensor_copy(xc, xbcT[:, :, ds(t * P, P)]).then_inc(S["staged"], 1)
                        hold(pool, S["staged"], t + 1)
                        for g in range(2):
                            pool.tensor_copy(Cz[g * 64:g * 64 + 64, g, :], xc[g * 64:g * 64 + 64, 9, :]).then_inc(S["cz"], 1)

                    pool.memset(Cz, 0.0).then_inc(S["zeroed"], 1)
                    pool.memset(Cw, 0.0).then_inc(S["zeroed"], 1)
                    pool.wait_ge(S["zeroed"], 2)
                    stage(0)
                    with pool.Fori(1, 4) as t:
                        pool.wait_ge(S["cb"], t)
                        stage(t)
                    pool.wait_ge(S["cb"], 4)
                    stage(4)

                @block.tensor
                def _(pe):
                    def front(t, s):
                        pe.wait_ge(S["staged"], t + 1)
                        pe.wait_ge(S["cz"], 2 * t + 2)
                        for k in range(KT):
                            pe.transpose(PX[:, k * P:(k + 1) * P], xc[:, k, :], ident[:])
                        pe.transpose(misc[:, 384:512], xc[:, 8, :], ident[:])
                        d = dta[:, ds(t, 1), :].rearrange("p o h -> p (o h)")
                        pe.matmul(misc[:, 0:16], upto[s][:], d, start=True, stop=True)
                        pe.matmul(misc[:, 16:32], after[s][:], d, start=True, stop=True)
                        pe.matmul(misc[:, 32:48], ones[:], d, start=True, stop=True)
                        pe.matmul(misc[:, 64:320], xc[:, 8, :], Cz.rearrange("p g q -> p (g q)"), start=True, stop=True)\
                            .then_inc(S["cb"], 1)

                    def chunk(t, s, s_next):
                        pe.wait_ge(S["mdta"], t + 1)
                        for i in range(4):
                            if i == 2:
                                pe.wait_ge(S["ydone"], t + 1)
                            pe.matmul(bank(i), after[s][:], mdta[:, 4 * i:4 * i + 4, :].rearrange("p h q -> p (h q)"),
                                      start=True, stop=True).then_inc(S["seg"], 1)
                        for i in range(4):
                            pe.wait_ge(S["E"], 4 * t + i + 1)
                            pe.matmul(bank(i), ones[:], mdta[:, 4 * i:4 * i + 4, :].rearrange("p h q -> p (h q)"),
                                      start=True, stop=True).then_inc(S["acb"], 1)
                        if s_next is not None:
                            for n in ("xdt", "Btok", "cbm", "ex"):
                                pe.wait_ge(S[n], t + 1)
                            front(t + 1, s_next)
                        pe.wait_ge(S["Ea"], 4 * t + 4)
                        pe.wait_ge(S["xdt"], t + 1)
                        if s:
                            pe.wait_ge(S["dtax"], 1)
                            pe.wait_ge(S["state"], 5)
                            for i in range(8):
                                last = pe.matmul(bank(7)[:, i * 8:(i + 1) * 8],
                                                 dtax[:, 2 * i:2 * i + 2, :].rearrange("p h c -> p (h c)"),
                                                 stream_of[:], start=True, stop=True)
                            last.then_inc(S["dec"], 1)
                        for h in range(HEADS):
                            g, i = divmod(h, 8)
                            if i == 0:
                                pe.wait_ge(S["W"], 2 * t + g + 1)
                                pe.wait_ge(S["Cw"], 2 * t + g + 1)
                            po = 64 * (h % 2)
                            o = Y[po:po + 64, (h // 2) * P:(h // 2 + 1) * P]
                            pe.matmul(o, xdt[:, h, :], E[:, h, :], start=True, stop=False, skip_group_check=bool(s))
                            if not s:
                                last = pe.matmul(o, stT[:, i * HD:(i + 1) * HD], Cw[:, h, :], start=False, stop=True)
                            else:
                                for b in range(STREAMS):
                                    last = pe.matmul(o[:, b * SLEN:(b + 1) * SLEN], stTb[:, b, i * HD:(i + 1) * HD],
                                                     Cw[:, h, b * SLEN:(b + 1) * SLEN],
                                                     start=False, stop=b == STREAMS - 1, skip_group_check=True)
                        last.then_inc(S["y"], 1)
                        if not s:
                            pe.wait_ge(S["state"], t + 1)
                            pe.wait_ge(S["xw"], t + 1)
                            for g in range(2):
                                last = pe.matmul(bank(7)[g * 64:g * 64 + 64, :], Btok[:, g * NS:(g + 1) * NS],
                                                 xw[:, g * 8:g * 8 + 8, :].rearrange("p h c -> p (h c)"), start=True, stop=True)
                            last.then_inc(S["stadd"], 1)

                    pe.sem_inc(S["y"], 1)
                    front(0, 0)
                    with pe.Fori(0, 3) as t:
                        chunk(t, 0, 0)
                    chunk(3, 0, 1)
                    pe.wait_ge(S["st_in"], 16 * 16)
                    for b in range(STREAMS):
                        if b >= 2:
                            pe.wait_ge(S["st_copied"], b - 1)
                        else:
                            pe.wait_ge(S["Ea"], 16)
                        for j in range(4):
                            last = pe.transpose(bank(b % 2)[:, j * P:(j + 1) * P], stN[:, b * 4 + j, :], ident[:])
                        last.then_inc(S["st_turned"], 1)
                    pe.wait_ge(S["st_copied"], 8)
                    chunk(4, 1, None)
                    pe.wait_ge(S["ydone"], 6)
                    for j in range(4):
                        last = pe.transpose(misc[:, j * P:(j + 1) * P], stT[:, j * P:(j + 1) * P], ident[:])
                    last.then_inc(S["turned"], 1)
                    pe.wait_ge(S["Bm"], 2)
                    for i in range(8):
                        if i >= 4:
                            pe.wait_ge(S["sadded"], i - 3)
                        pe.matmul(bank(i % 4), xw[:, 2 * i:2 * i + 2, :].rearrange("p h c -> p (h c)"), Bm[:, i // 4, :],
                                  start=True, stop=True).then_inc(S["sadd"], 1)

                @block.scalar
                def _(act):
                    def chunk(t):
                        act.wait_ge(S["y"], t + 1)
                        for i in range(4):
                            act.wait_ge(S["seg"], 4 * t + i + 1)
                            act.activation(E[:, 4 * i:4 * i + 4, :].rearrange("p h q -> p (h q)"), bank(i), ACT.Exp).then_inc(S["E"], 1)
                        act.wait_ge(S["cbm"], t + 1)
                        act.wait_ge(S["state"], t + 1)
                        act.activation(ex, misc[:, 0:48], ACT.Exp).then_inc(S["ex"], 1)
                        for i in range(4):
                            act.wait_ge(S["acb"], 4 * t + i + 1)
                            act.activation(Ea[:, 4 * i:4 * i + 4, :].rearrange("p h q -> p (h q)"), bank(i), ACT.Exp).then_inc(S["Ea"], 1)

                    with act.Fori(0, 4) as t:
                        chunk(t)
                    hold(act, written, l * W_LRU + W_CONV_LRU)
                    for b in range(STREAMS):
                        act.wait_ge(S["st_turned"], b + 1)
                        act.activation(stTb[:, b, :], bank(b % 2), ACT.Copy).then_inc(S["st_copied"], 1)
                    chunk(4)
                    act.wait_ge(S["dec"], 1)
                    act.activation(spw[:, 0, 0:64], bank(7)[:, 0:64], ACT.Exp).then_inc(S["decE"], 1)
                    act.wait_ge(S["turned"], 1)
                    act.activation(E[:, 0:4, :].rearrange("p h q -> p (h q)"), misc, ACT.Copy).then_inc(S["stadd"], 1)
                    act.wait_ge(S["sadded"], 8)
                    v = stN.rearrange("p (b j) (g n) -> p b j g n", j=4, g=2)
                    dst = state_view("new_ssd_sample")
                    for b in range(STREAMS // 2):
                        act.dma_start(dst[:, ds(l * 64 + b * 8 + 4, 4), :], v[:, b, :, 1, :]).then_inc(written, 16)

                @block.vector
                def _(dve):
                    st = Steps(dve, "ssd_step")

                    def masked(t, s):
                        d = dta[:, ds(t, 1), :].rearrange("p o h -> p (o h)")
                        dve.tensor_tensor(mdta, upto[s][:].unsqueeze(1).to_broadcast([P, HEADS, P]), b16(d, P), ALU.mult)\
                           .then_inc(S["mdta"], 1)

                    def chunk(t, s, s_next, st):
                        n0 = st.n
                        dtt = dt[:, ds(t, 1), :].rearrange("p o h -> p (o h)")
                        dve.wait_ge(S["cb"], t + 1)
                        dve.tensor_copy(Btok, misc[:, 384:512]).then_inc(S["Btok"], 1)
                        dve.tensor_tensor(xdt, PX.rearrange("p (h c) -> p h c", h=HEADS), b16(dtt, HD), ALU.mult).then_inc(S["xdt"], 1)
                        dve.tensor_tensor(cbm, misc[:, 64:320].rearrange("p (g q) -> p g q", g=2),
                                          upto[s][:].unsqueeze(1).to_broadcast([P, 2, P]), ALU.mult).then_inc(S["cbm"], 1)
                        ys = ysT[:, :, ds(t * P, P)]
                        st(dve.tensor_tensor(ys, xbcT[:, 0:KT, ds(t * P, P)], b16(cols[:, DD:DD + KT], P), ALU.mult))
                        if s:
                            dve.tensor_copy(dtax, b16(dta[:, t, :], HD)).then_inc(S["dtax"], 1)
                        dve.wait_ge(S["cbm"], t + 1)
                        for g in range(2):
                            dve.wait_ge(S["E"], 4 * t + 2 * g + 2)
                            v = E[:, 8 * g:8 * g + 8, :]
                            dve.tensor_tensor(v, v, cbm[:, g, :].unsqueeze(1).to_broadcast([P, 8, P]), ALU.mult).then_inc(S["W"], 1)
                        dve.wait_ge(S["ex"], t + 1)
                        dve.wait_ge(S["xdt"], t + 1)
                        dve.tensor_tensor(xw, xdt, b16(ex[:, 16:32], HD), ALU.mult).then_inc(S["xw"], 1)
                        for g in range(2):
                            r = slice(g * 64, g * 64 + 64)
                            dve.wait_ge(S["Ea"], 4 * t + 2 * g + 2)
                            dve.tensor_tensor(Cw[r, g * 8:g * 8 + 8, :], Ea[r, g * 8:g * 8 + 8, :],
                                              xbcT[r, 9:10, ds(t * P, P)].to_broadcast([64, 8, P]), ALU.mult).then_inc(S["Cw"], 1)
                        if s_next is not None:
                            masked(t + 1, s_next)
                        if s:
                            dve.wait_ge(S["acb"], 4 * t + 4)
                            dve.wait_ge(S["Btok"], t + 1)
                            for g in range(2):
                                dve.tensor_tensor(Bm[:, g, :].rearrange("p (b n) -> p b n", b=STREAMS),
                                                  Btok[:, g * NS:(g + 1) * NS].unsqueeze(1).to_broadcast([P, STREAMS, NS]),
                                                  b16(stream_of[:], NS), ALU.mult).then_inc(S["Bm"], 1)
                            dve.wait_ge(S["decE"], 1)
                            dve.wait_ge(S["st_turned"], STREAMS)
                            for i in range(8):
                                g, j = divmod(i, 4)
                                v = stN_parts[:, :, j, g, :]
                                st(dve.tensor_tensor(v, v, b16(spw[:, 0, i * 8:i * 8 + 8], NS), ALU.mult))
                        st.wait()
                        dve.wait_ge(S["y"], t + 2)
                        dve.tensor_tensor(ys, Y.rearrange("p (k q) -> p k q", k=KT), ys, ALU.add).then_inc(S["ydone"], 1)
                        if not s:
                            for g in range(2):
                                r = slice(g * 64, g * 64 + 64)
                                v = stT[r, :].rearrange("p (h c) -> p h c", h=8)
                                st(dve.tensor_tensor(v, v, b16(ex[r, 32 + g * 8:40 + g * 8], HD), ALU.mult))
                            st.wait()
                            dve.wait_ge(S["stadd"], t + 1)
                            dve.tensor_tensor(stT[:], stT[:], bank(7), ALU.add).then_inc(S["state"], 1)
                            dve.wait_ge(S["state"], t + 2)
                        return st.n - n0

                    dve.sem_inc(S["ydone"], 1)
                    dve.memset(stT[:], 0.0).then_inc(S["state"], 1)
                    masked(0, 0)
                    dve.wait_ge(S["state"], 1)
                    PER = 3
                    with dve.Fori(0, 3) as t:
                        used = chunk(t, 0, 0, Steps(dve, "ssd_step", t * PER))
                        assert used == PER, used
                    st = Steps(dve, "ssd_step", 3 * PER)
                    chunk(3, 0, 1, st)
                    chunk(4, 1, None, st)
                    for i in range(8):
                        g, j = divmod(i, 4)
                        dve.wait_ge(S["sadd"], i + 1)
                        v = stN_parts[:, :, j, g, :]
                        dve.tensor_tensor(v, v, bank(i % 4).rearrange("p (b n) -> p b n", b=STREAMS),
                                          ALU.add).then_inc(S["sadded"], 1)
                    dve.wait_ge(S["sadded"], 8)
            end_phase()

            with nc.Block() as block:
                wready = [phase_sem(f"weight_ready_{s}") for s in range(2)]
                done, gated, silued, squared, summed, rooted, ready = (phase_sem(n) for n in (
                    "projected", "gated", "silued", "squared", "summed", "rooted", "root_in"))
                sz = view(arenaX, 0, 2, TT)
                sq = view(arenaR, 2 * KT * TT, 2, TT)
                slot0 = 4

                @block.sync
                def _(sp):
                    have_first(sp, wready)
                    sp.sem_inc(done, 2)
                    fetch_ahead(sp, l, "w_in", LY0, 6)
                    with sp.Fori(1, KT // 2) as j:
                        for u in range(2):
                            sp.wait_ge(done, 2 * j + u + 1)
                            sp.dma_start(wt[:, slot0 + u, :, :], weight("w_in", l, Z0 + j * (2 * P) + u * P)).then_inc(wready[u], 16)
                    finish_ahead(sp)

                @block.tensor
                def _(pe):
                    def add_square(u, first, final):
                        for o, n in ((0, SEQ), (SEQ, TT - SEQ)):
                            last = pe.matmul(bank(4, 2)[:, o:o + n], ones[:], sq[:, u, o:o + n], start=first, stop=final)
                        return last

                    for o, n in ((0, SEQ), (SEQ, TT - SEQ)):
                        pe.matmul(bank(4, 2)[:, o:o + n], zeros[:], hT[:, 0, o:o + n], start=True, stop=False)
                    pe.sem_inc(silued, 2)
                    with pe.Fori(0, 4) as j:
                        for u in range(2):
                            pe.wait_ge(wready[u], j * 16 + 16)
                            pe.wait_ge(silued, 2 * j + u + 1)
                            project(slot0 + u, hT, bank(2 * u, 2)).then_inc(done, 1)
                        for u in range(2):
                            pe.wait_ge(squared, 2 * j + u + 1)
                            add_square(u, False, False).then_inc(summed, 1)
                    for o, n in ((0, SEQ), (SEQ, TT - SEQ)):
                        last = pe.matmul(bank(4, 2)[:, o:o + n], zeros[:], hT[:, 0, o:o + n], start=False, stop=True)
                    last.then_inc(summed, 1)

                @block.scalar
                def _(act):
                    act.sem_inc(gated, 2)
                    act.sem_inc(summed, 2)
                    with act.Fori(0, 4) as j:
                        for u in range(2):
                            act.wait_ge(done, 2 + 2 * j + u + 1)
                            act.wait_ge(gated, 2 * j + u + 1)
                            act.activation(sz[:, u, :], bank(2 * u, 2)[:, 0:TT], ACT.Silu).then_inc(silued, 1)
                        for u in range(2):
                            act.wait_ge(gated, 2 + 2 * j + u + 1)
                            act.wait_ge(summed, 2 * j + u + 1)
                            act.activation(sq[:, u:u + 1, :], ysT[:, ds(2 * j + u, 1), :], ACT.Square).then_inc(squared, 1)
                    act.wait_ge(ready, 1)
                    act.activation(rs, rs, ACT.Sqrt).then_inc(rooted, 1)

                @block.vector
                def _(dve):
                    with dve.Fori(0, 4) as j:
                        for u in range(2):
                            dve.wait_ge(silued, 2 + 2 * j + u + 1)
                            y = ysT[:, ds(2 * j + u, 1), :]
                            dve.tensor_tensor(y, y, sz[:, u:u + 1, :], ALU.mult).then_inc(gated, 1)
                        for u in range(2):
                            dve.wait_ge(squared, 2 * j + u + 1)
                            y = ysT[:, ds(2 * j + u, 1), :]
                            dve.tensor_scalar(y, y, cols[:, ds(NW + 2 * j + u, 1)], None, ALU.mult).then_inc(phase_sem("weighted"), 1)
                    dve.wait_ge(summed, 2 + 9)
                    dve.wait_ge(gated, 2 + 8)
                    dve.tensor_scalar(rs, bank(4, 2)[:, 0:TT], 1.0 / D, EPS, ALU.mult, ALU.add).then_inc(ready, 1)
                    dve.wait_ge(rooted, 1)
                    st = Steps(dve, "dve_step")
                    st(dve.reciprocal(rs, rs))
                    st.wait()
                    dve.wait_ge(phase_sem("weighted"), 8)
            end_phase()

            srcs = ((("w_in", GS0), hT), (("w_br_ssd", 0), ysT), (("w_in", GL0), hT), (("w_br_lru", 0), ylT))

            with nc.Block() as block:
                wready = [phase_sem(f"weight_ready_{s}") for s in range(2)]
                gready = [phase_sem(f"gate_weights_ready_{s}") for s in range(2)]
                done, gates_done, evac, zeroed = (phase_sem(n) for n in ("projected", "gates_done", "ly_taken", "zeroed"))
                sg, th, gs, sgs, rt, q, fin = (phase_sem(n) for n in (
                    "sigmoids", "tanh", "gelu_in", "gelu_sig", "rooted", "root_in", "lru_done"))
                aa, uu = phase_sem("a_made"), phase_sem("u_made")
                wbd = view(arenaW, 5 * D, 4, P)
                rows = [arenaR[:, 2 * KT * TT + i * TT:2 * KT * TT + (i + 1) * TT] for i in range(9)]
                rows += [arenaQ[:, i * TT:(i + 1) * TT] for i in range(9)]
                buf = [dict(zip(("R", "I", "LY", "G", "Q4", "AA", "UU", "REC", "HS"), rows[u * 9:])) for u in range(2)]

                @block.sync
                def _(sp):
                    def gate_weights(j, u):
                        for i, nm in enumerate(("lru_wa", "lru_wx")):
                            for h in range(2):
                                src = a[nm].rearrange("l n d e -> (l n d) e")[ds(l * D + j * (2 * P) + u * P + h * 64, 64), :]
                                sp.dma_start(wbd[h * 64:h * 64 + 64, 2 * u + i, h * 64:h * 64 + 64], src).then_inc(gready[u], 16)

                    sp.wait_ge(zeroed, 1)
                    have_first(sp, wready)
                    sp.sem_inc(done, 2)
                    sp.sem_inc(gates_done, 2)
                    for u in range(2):
                        gate_weights(0, u)
                    hold(sp, written, l * W_LRU + W_SSD)
                    fetch_ahead(sp, l, *srcs[0][0], 0, 1)
                    fetch_ahead(sp, l, *srcs[1][0], 1, 1)
                    fetch_ahead(sp, l, *srcs[2][0], 2, 1)
                    fetch_ahead(sp, l, *srcs[3][0], 3, 1)
                    with sp.Fori(1, KT // 2) as j:
                        for u in range(2):
                            sp.wait_ge(gates_done, 2 * j + u + 1)
                            gate_weights(j, u)
                            sp.wait_ge(done, 2 * j + u + 1)
                            sp.dma_start(wt[:, 6 + u, :, :], weight("w_in", l, LY0 + j * (2 * P) + u * P)).then_inc(wready[u], 16)
                    finish_ahead(sp, 4)

                @block.tensor
                def _(pe):
                    pe.sem_inc(sg, 2)
                    pe.sem_inc(evac, 2)
                    with pe.Fori(0, KT // 2) as j:
                        for u in range(2):
                            pe.wait_ge(gready[u], j * 64 + 64)
                            pe.wait_ge(sg, 4 * j + 2 * u + 2)
                            for i in range(2):
                                for o, n in ((0, SEQ), (SEQ, TT - SEQ)):
                                    last = pe.matmul(bank(2 * i, 2)[:, o:o + n], wbd[:, 2 * u + i, :],
                                                     lxT[:, ds(2 * j + u, 1), o:o + n].rearrange("p o t -> p (o t)"),
                                                     start=True, stop=True)
                            last.then_inc(gates_done, 1)
                            pe.wait_ge(wready[u], j * 16 + 16)
                            pe.wait_ge(evac, 2 * j + u + 1)
                            project(6 + u, hT, bank(4 + 2 * u, 2)).then_inc(done, 1)

                @block.scalar
                def _(act):
                    for s in (fin, aa, uu):
                        act.sem_inc(s, 2)
                    with act.Fori(0, KT // 2) as j:
                        for u in range(2):
                            B = buf[u]
                            act.wait_ge(gates_done, 2 + 2 * j + u + 1)
                            act.wait_ge(aa, 2 * j + u + 1)
                            act.activation(B["R"], bank(0, 2)[:, 0:TT], ACT.Sigmoid, bias=cols[:, ds(BA + 2 * j + u, 1)]).then_inc(sg, 1)
                            act.wait_ge(uu, 2 * j + u + 1)
                            act.activation(B["I"], bank(2, 2)[:, 0:TT], ACT.Sigmoid, bias=cols[:, ds(BX + 2 * j + u, 1)]).then_inc(sg, 1)
                            act.wait_ge(sg, 2 + 4 * j + 2 * u + 1)
                            act.activation(B["R"], B["R"], ACT.Tanh, scale=lamS[:, ds(2 * j + u, 1)]).then_inc(th, 1)
                        for u in range(2):
                            act.wait_ge(q, 2 * j + u + 1)
                            act.activation(buf[u]["Q4"], buf[u]["Q4"], ACT.Sqrt).then_inc(rt, 1)
                        for u in range(2):
                            B = buf[u]
                            act.wait_ge(done, 2 + 2 * j + u + 1)
                            act.wait_ge(fin, 2 * j + u + 1)
                            act.activation(B["G"], bank(4 + 2 * u, 2)[:, 0:TT], ACT.Square, scale=0.044715 ** 0.5).then_inc(phase_sem("squared"), 1)
                            act.activation(B["LY"], bank(4 + 2 * u, 2)[:, 0:TT], ACT.Copy).then_inc(evac, 1)
                        for u in range(2):
                            act.wait_ge(gs, 2 * j + u + 1)
                            act.activation(buf[u]["G"], buf[u]["G"], ACT.Sigmoid, scale=1.5957691216057308).then_inc(sgs, 1)

                @block.vector
                def _(dve):
                    st = Steps(dve, "dve_step")
                    st(dve.memset(wbd, 0.0))
                    st.wait()
                    dve.sem_inc(zeroed, 1)
                    hold(dve, written, l * W_LRU + W_SSD)
                    PER = 16
                    blk = lambda v: v.rearrange("p (b t) -> p b t", t=SLEN)
                    with dve.Fori(0, KT // 2) as j:
                        st = Steps(dve, "lru_step", j * PER)
                        for u in range(2):
                            R, I, LY, G, Q4, AA, UU, REC, HS = (buf[u][n] for n in ("R", "I", "LY", "G", "Q4", "AA", "UU", "REC", "HS"))
                            dve.wait_ge(th, 2 * j + u + 1)
                            st(dve.tensor_scalar(REC, R, -1.0, 1.0, ALU.mult, ALU.add))
                            dve.tensor_scalar(Q4, R, -4.0, 1e-30, ALU.mult, ALU.max).then_inc(q, 1)
                            st.wait()
                            st(dve.reciprocal(REC, REC))
                            st(dve.tensor_tensor(I, I, lxT[:, ds(2 * j + u, 1), :].rearrange("p o t -> p (o t)"), ALU.mult))
                            st.wait()
                            dve.scalar_tensor_tensor(AA, R, 1.0, REC, ALU.add, ALU.mult).then_inc(aa, 1)
                            st(dve.tensor_tensor(I, I, REC, ALU.mult))
                        for u in range(2):
                            R, I, LY, G, Q4, AA, UU, REC, HS = (buf[u][n] for n in ("R", "I", "LY", "G", "Q4", "AA", "UU", "REC", "HS"))
                            st.wait()
                            dve.wait_ge(rt, 2 * j + u + 1)
                            dve.tensor_tensor(UU, I, Q4, ALU.mult).then_inc(uu, 1)
                            dve.wait_ge(aa, 2 + 2 * j + u + 1)
                            h0 = cols[:, H0:CV].rearrange("p (b k) -> p b k", k=KT)[:, :, ds(2 * j + u, 1)]
                            first = blk(AA)[:, 32:40, 0:1]
                            tmp = small[:, 8 * u:8 * u + 8].unsqueeze(2)
                            st(dve.tensor_tensor(tmp, first, h0, ALU.mult))
                            st.wait()
                            dve.wait_ge(uu, 2 + 2 * j + u + 1)
                            st(dve.tensor_tensor(blk(UU)[:, 32:40, 0:1], blk(UU)[:, 32:40, 0:1], tmp, ALU.add))
                            st(dve.memset(first, 0.0))
                            st.wait()
                            st(dve.tensor_tensor_scan(HS, AA, UU, 0.0, ALU.mult, ALU.add))
                            st.wait()
                            dve.tensor_copy(lruN[:, ds(2 * j + u, 1), 1:9], blk(HS)[:, 32:40, SLEN - 1:SLEN].rearrange("p b o -> p o b"))\
                               .then_inc(phase_sem("last_taken"), 1)
                            dve.tensor_copy(lruN[:, ds(2 * j + u, 1), 0:1], HS[:, SEQ - 1:SEQ].unsqueeze(1)).then_inc(phase_sem("last_taken"), 1)
                        for u in range(2):
                            G, LY = buf[u]["G"], buf[u]["LY"]
                            dve.wait_ge(evac, 2 + 2 * j + u + 1)
                            dve.wait_ge(phase_sem("squared"), 2 * j + u + 1)
                            dve.scalar_tensor_tensor(G, G, 1.0, LY, ALU.add, ALU.mult).then_inc(gs, 1)
                        for u in range(2):
                            G, LY, HS = buf[u]["G"], buf[u]["LY"], buf[u]["HS"]
                            dve.wait_ge(sgs, 2 * j + u + 1)
                            dve.tensor_tensor(G, G, LY, ALU.mult).then_inc(phase_sem("gelu"), 1)
                            dve.wait_ge(phase_sem("gelu"), 2 * j + u + 1)
                            dve.tensor_tensor(ylT[:, ds(2 * j + u, 1), :], G.unsqueeze(1), HS.unsqueeze(1), ALU.mult).then_inc(fin, 1)
                        assert st.n == PER, st.n
                    dve.wait_ge(fin, 2 + KT)
                    dve.wait_ge(phase_sem("last_taken"), 2 * KT)
            end_phase()

            with nc.Block() as block:
                wready = [phase_sem(f"weight_ready_{s}") for s in range(4)]
                done, sg, taken = phase_sem("projected"), phase_sem("sigmoids"), phase_sem("taken")
                G2 = view(arenaX, 0, 2, TT)
                M1 = arenaX[:, 2 * TT:3 * TT]
                banks = (0, 2, 4, 2)
                mod_w = view(arenaQ, 0, 4, D)
                mod_ps = bank(7)[:, 0:4 * KT * 9]
                outrow = view(arenaW, 4096, D)

                @block.sync
                def _(sp):
                    def mod_weights(j, u):
                        sp.dma_start(mod_w[:, u, :], a["w_mod"].rearrange("l r c -> (l r) c")
                                     [ds(l * D + j * P, P), (2 + u) * D:(3 + u) * D]).then_inc(wready[u], 16)

                    sp.sem_inc(done, 4)
                    for u in range(4):
                        mod_weights(0, u)
                    have_first(sp, wready)
                    fetch_ahead(sp, l, "w_out", 0, 6)
                    with sp.Fori(1, KT) as j:
                        for u, ((nm, c0), _) in enumerate(srcs):
                            sp.wait_ge(done, 4 * j + u + 1)
                            sp.dma_start(wt[:, u, :, :], weight(nm, l, c0 + j * P)).then_inc(wready[u], 16)
                            mod_weights(j, u)
                    finish_ahead(sp)
                    sp.wait_ge(phase_sem("lru_rows"), 2)
                    sp.dma_start(a["new_lru_prompt"].rearrange("l b c -> (l b) c")[ds(l, 1), :], outrow[0:1, :]).then_inc(written, 16)
                    sp.dma_start(a["new_lru_sample"].rearrange("l b c -> (l b) c")[ds(l * 8, 8), :], outrow[1:9, :]).then_inc(written, 16)

                @block.tensor
                def _(pe):
                    pe.sem_inc(sg, 2)
                    pe.sem_inc(taken, 2)
                    cT = cols[:, CV:NCOLS].rearrange("p (s k) -> p k s", k=KT)
                    for k in range(KT):
                        last = pe.transpose(bank(5 + k // 4)[0:9, k % 4 * P:(k % 4 + 1) * P], lruN[:, k, :], ident[:])
                    last.then_inc(phase_sem("lru_turned"), 1)
                    pe.matmul(mod_ps, zeros[:], xT[:, 0, 0:4 * KT * 9], start=True, stop=False)
                    with pe.Fori(0, KT) as j:
                        for u, (_, src) in enumerate(srcs):
                            def between(c):
                                at = (u * KT + c) * 9
                                pe.matmul(mod_ps[:, at:at + 9], mod_w[:, u, c * P:(c + 1) * P],
                                          cT[:, ds(j, 1), :].rearrange("p o s -> p (o s)"), start=False, stop=False)

                            pe.wait_ge(wready[u], j * 32 + 32)
                            if u % 2 == 0:
                                pe.wait_ge(sg, 2 * j + u // 2 + 1)
                                if u == 2:
                                    pe.wait_ge(phase_sem("lru_rows"), 2)
                            else:
                                pe.wait_ge(taken, 2 * j + u // 2 + 2)
                            project(u, src, bank(banks[u], 2), between).then_inc(done, 1)
                    pe.matmul(mod_ps, zeros[:], xT[:, 0, 0:4 * KT * 9], start=False, stop=True).then_inc(phase_sem("mod_sum"), 1)
                    pe.wait_ge(phase_sem("mod_sum"), 1)

                @block.scalar
                def _(act):
                    act.wait_ge(phase_sem("lru_turned"), 1)
                    for i in range(2):
                        act.activation(outrow[0:9, i * 512:(i + 1) * 512], bank(5 + i)[0:9, :], ACT.Copy).then_inc(phase_sem("lru_rows"), 1)
                    with act.Fori(0, KT) as j:
                        for i in range(2):
                            act.wait_ge(done, 4 + 4 * j + 2 * i + 1)
                            act.wait_ge(taken, 2 * j + i + 1)
                            act.activation(G2[:, i, :], bank(banks[2 * i], 2)[:, 0:TT], ACT.Sigmoid).then_inc(sg, 1)

                @block.vector
                def _(dve):
                    with dve.Fori(0, KT) as j:
                        m = mT[:, ds(j, 1), :].rearrange("p o t -> p (o t)")
                        dve.wait_ge(sg, 2 + 2 * j + 1)
                        dve.tensor_tensor(G2[:, 0, :], G2[:, 0, :], rs, ALU.mult).then_inc(phase_sem("rooted"), 1)
                        dve.wait_ge(phase_sem("rooted"), j + 1)
                        dve.wait_ge(done, 4 + 4 * j + 2)
                        dve.tensor_tensor(M1, bank(2, 2)[:, 0:TT], G2[:, 0, :], ALU.mult).then_inc(taken, 1)
                        dve.wait_ge(sg, 2 + 2 * j + 2)
                        dve.wait_ge(done, 4 + 4 * j + 4)
                        dve.tensor_tensor(m, bank(2, 2)[:, 0:TT], G2[:, 1, :], ALU.mult).then_inc(taken, 1)
                        dve.wait_ge(taken, 2 + 2 * j + 2)
                        dve.tensor_tensor(m, m, M1, ALU.add).then_inc(phase_sem("merged"), 1)
                        dve.wait_ge(phase_sem("merged"), j + 1)
            end_phase()

            with nc.Block() as block:
                wready = [phase_sem(f"weight_ready_{s}") for s in range(2)]
                done, taken = phase_sem("projected"), phase_sem("taken")
                TMP = view(arenaX, 0, 2, TT)

                @block.sync
                def _(sp):
                    sp.sem_inc(done, 2)
                    have_first(sp, wready)
                    with sp.Fori(1, KT // 2) as j:
                        for u in range(2):
                            sp.wait_ge(done, 2 * j + u + 1)
                            sp.dma_start(wt[:, 6 + u, :, :], weight("w_out", l, j * (2 * P) + u * P)).then_inc(wready[u], 16)
                    hold(sp, written, l * W_LRU + W_LRU)

                @block.tensor
                def _(pe):
                    pe.sem_inc(taken, 2)
                    with pe.Fori(0, 4) as j:
                        for u in range(2):
                            pe.wait_ge(wready[u], j * 16 + 16)
                            pe.wait_ge(taken, 2 * j + u + 1)
                            project(6 + u, mT, bank(2 * u, 2)).then_inc(done, 1)

                @block.vector
                def _(dve):
                    blk = lambda v: v.rearrange("p (b t) -> p b t", t=SLEN)
                    st = Steps(dve, "dve_step")
                    modulation(dve, st, phase_sem("mod_done"), bank(7), 2 * KT, 6 * KT)
                    norm_scale(dve, st, 4 * KT, LN2)
                    with dve.Fori(0, 4) as j:
                        for u in range(2):
                            dve.wait_ge(done, 2 + 2 * j + u + 1)
                            g = modE[:, ds(2 * KT + 2 * j + u, 1), :].rearrange("p o b -> p (o b)")
                            x = xT[:, ds(2 * j + u, 1), :].rearrange("p o t -> p (o t)")
                            dve.tensor_tensor(blk(TMP[:, u, :]), blk(bank(2 * u, 2)[:, 0:TT]), b16(g), ALU.mult).then_inc(taken, 1)
                            dve.wait_ge(taken, 2 + 2 * j + u + 1)
                            dve.tensor_tensor(x, x, TMP[:, u, :], ALU.add).then_inc(phase_sem("added"), 1)
                    dve.wait_ge(phase_sem("added"), KT)
            end_phase()

            norm_phase(hT[:], modE[:, 4 * KT:5 * KT, :], modE[:, 3 * KT:4 * KT, :],
                       (l, "peer_wq", 0, 0))

            qT = view(arenaQ, 0, 2 * PH, TT)
            ring = view(arenaR, 0, RING, D)
            diag = view(arenaW, 0, RING, P)
            qs = view(arenaW, 2048, 2 * PH, P)
            cand = view(arenaW, 2048, PH, TOPK * TOPK)
            cand1 = view(arenaW, 3072, 1, TOPK * TOPK)
            hs = view(arenaW, 4096, KT, P)
            osb = arenaW[:, 4096:4096 + D]
            hrow = arenaW[:, 5120:6144]
            cut = view(arenaX, 0, 2 * PH, KEYS)
            ccut = view(arenaX, 0, PH, TOPK * TOPK)
            kT = view(arenaQ, 16 * TT + 1024, 2, P)
            ps_out, ps_sc, ps_t = bank(0, 2), bank(2, 4), bank(6, 2)
            free = [(arenaW, 6144, 8192), (arenaQ, 16 * TT, 16 * TT + 1024)]
            acc = hrow

            def tile_of(*shape):
                n = 1
                for x in shape:
                    n *= x
                for i, (ar, lo, hi) in enumerate(free):
                    if hi - lo >= n:
                        free[i] = (ar, lo + n, hi)
                        return view(ar, lo, *shape)
                raise ValueError("no room")

            val = tile_of(2 * PH, TOPK)
            key = tile_of(2 * PH, TOPK).bitcast(U32)
            keyf = tile_of(2 * PH, TOPK)
            eidx = tile_of(NT, PICKS).bitcast(U32)
            sval = tile_of(PH, TOPK)
            place = tile_of(PH, TOPK).bitcast(U32)
            parts = tile_of(2, PICKS).bitcast(U32)
            partf = tile_of(2, PICKS)
            gate = tile_of(PH, TOPK)
            hid = tile_of(PICKS)
            gel = tile_of(PICKS)
            wgt = tile_of(PICKS)
            slot_idx = small[:, 16:32].rearrange("p (h n) -> p h n", h=2).bitcast(U32)
            den = small[:, 32:40]
            sv1 = spw[:, 0:1, 0:TOPK]
            pl1 = spw[:, 1:2, 0:TOPK].bitcast(U32)
            row0 = small[:, 40:41]
            with nc.Block() as block:
                G = {n: phase_sem("peer_" + n) for n in (
                    "keys_in", "keys_turned", "keys", "q_staged", "h_staged", "h_turned", "h_rows", "scores", "idx",
                    "exp_in", "exp_out", "u_used", "v_used", "v_added", "hid", "gelu", "wgt", "diag", "sum", "osb",
                    "o_turned", "resid", "slots", "row0", "projected", "q_taken", "head_idx", "acc")}
                wready = [phase_sem(f"weight_ready_{s}") for s in range(2)]

                @block.sync
                def _(sp):
                    for i, nm in enumerate(("peer_k1", "peer_k2")):
                        sp.dma_start(rowbuf[:, i, :], a[nm].rearrange("l k d -> (l k) d")[ds(l * KEYS, KEYS), :]).then_inc(G["keys_in"], 16)
                    have_first(sp, wready)
                    sp.sem_inc(G["projected"], 2)
                    with sp.Fori(1, PH) as j:
                        for u in range(2):
                            sp.wait_ge(G["projected"], 2 * j + u + 1)
                            sp.dma_start(wt[:, u, :, :], weight("peer_wq", l, j * (2 * P) + u * P)).then_inc(wready[u], 16)

                @block.gpsimd
                def _(pool):
                    for n in ("u_used", "v_used", "v_added"):
                        pool.sem_inc(G[n], 2)
                    u_table = a["peer_u"].rearrange("l e d -> (l e) d")
                    v_table = a["peer_v"].rearrange("l e d -> (l e) d")

                    def gather(t, i, hf, table, at):
                        pool.tensor_copy(slot_idx[:, hf:hf + 1, :], eidx[:, ds(t, 1), ds(at, HALF)]).then_inc(G["slots"], 1)
                        hold(pool, G["slots"], t * 32 + i + 1)
                        for n in range(HALF):
                            pool.indirect_dma_start(ring[:, hf * HALF + n, :], None, table,
                                                    bass.IndirectOffsetOnAxis(ap=slot_idx[:, hf, n:n + 1], axis=0))\
                                .then_inc(gathered[hf * HALF + n], 16)

                    def gather_u(t, first):
                        with pool.Fori(0, BATCHES) as m:
                            if first:
                                hold(pool, G["head_idx"], m + 2)
                            for hf in range(2):
                                hold(pool, G["u_used"], t * 16 + m * 2 + hf + 1)
                                if not first:
                                    hold(pool, G["v_used"], t * 16 + hf + 1)
                                    hold(pool, G["v_added"], t * (SHARE // 2) + hf + 1)
                                gather(t, m * 2 + hf, hf, u_table, m * RING + hf * HALF)

                    def gather_v(t):
                        for lo, hi in ((0, SHARED), (SHARED, BATCHES)):
                            with pool.Fori(lo, hi) as m:
                                for hf in range(2):
                                    hold(pool, G["u_used"], t * 16 + 16 + hf + 1)
                                    hold(pool, G["v_used"], t * 16 + m * 2 + hf + 1)
                                    if lo:
                                        hold(pool, G["v_added"], t * (SHARE // 2) + (m - SHARED) * 2 + hf + 1)
                                    gather(t, m * 2 + (16 + hf), hf, v_table, m * RING + hf * HALF)

                    gather_u(0, True)
                    gather_v(0)
                    with pool.Fori(1, NT) as t:
                        hold(pool, G["idx"], t)
                        gather_u(t, False)
                        gather_v(t)

                @block.tensor
                def _(pe):
                    pe.wait_ge(G["keys_in"], 32)
                    for i in range(2):
                        last = pe.transpose(ps_t[:, i * P:(i + 1) * P], rowbuf[:, i, :], ident[:])
                    last.then_inc(G["keys_turned"], 1)
                    pe.wait_ge(G["keys"], 1)
                    pe.sem_inc(G["q_taken"], 2)
                    pe.sem_inc(G["head_idx"], 1)

                    def head_scores():
                        for u in range(2):
                            last = pe.matmul(bank(4 + u)[:, 0:KEYS], qs[:, u, :], kT[:, u, :], start=True, stop=True)
                        last.then_inc(G["scores"], 1)

                    def first_head():
                        for u in range(2):
                            pe.wait_ge(wready[u], 16)
                            for k in range(KT):
                                last = pe.matmul(bank(4 + u)[:, KEYS:KEYS + P], wt[:, u, k, :], hT[:, k, 0:P],
                                                 start=k == 0, stop=k == KT - 1)
                            last.then_inc(phase_sem("first_query"), 1)
                        pe.wait_ge(G["q_staged"], 2)
                        head_scores()

                    def queries():
                        def both(j):
                            for u in range(2):
                                pe.wait_ge(wready[u], j * 16 + 16)
                                pe.wait_ge(G["q_taken"], 2 * j + u + 1)
                                project(u, hT, bank(2 * u, 2)).then_inc(G["projected"], 1)

                        both(0)
                        with pe.Fori(1, PH) as j:
                            both(j)
                            pe.wait_ge(G["q_staged"], 2 * j + 2)
                            pe.wait_ge(G["head_idx"], j + 1)
                            head_scores()

                    def score(t):
                        pe.wait_ge(G["q_staged"], 2 * PH + t)
                        for i in range(2 * PH):
                            last = pe.matmul(ps_sc[:, i * KEYS:(i + 1) * KEYS], qs[:, i, :], kT[:, i % 2, :], start=True, stop=True)
                        last.then_inc(G["scores"], 1)

                    def turn_h(t):
                        pe.wait_ge(G["h_staged"], t + 1)
                        for k in range(KT):
                            last = pe.transpose(ps_t[:, k * P:(k + 1) * P], hs[:, k, :], ident[:])
                        last.then_inc(G["h_turned"], 1)

                    def retrieve(t):
                        for c in range(2):
                            pe.matmul(ps_out[:, c * 512:(c + 1) * 512], zeros[:], hT[:, 0, 0:512], start=True, stop=False)
                        for lo, hi in ((0, SHARED), (SHARED, BATCHES)):
                            with pe.Fori(lo, hi) as m:
                                for hf in range(2):
                                    pe.wait_ge(G["diag"], t * 16 + m * 2 + hf + 1)
                                    for n in range(hf * HALF, (hf + 1) * HALF):
                                        if lo and n % 4 == 3:
                                            continue
                                        pe.wait_ge(gathered[n], l * (NT * 256) + t * 256 + 128 + m * 16 + 16)
                                        for c in range(2):
                                            last = pe.matmul(ps_out[:, c * 512:(c + 1) * 512], diag[:, n, :],
                                                             ring[:, n, c * 512:(c + 1) * 512], start=False, stop=False)
                                    last.then_inc(G["v_used"], 1)
                        pe.wait_ge(G["acc"], t + 1)
                        for c in range(2):
                            last = pe.matmul(ps_out[:, c * 512:(c + 1) * 512], ident[:], acc[:, c * 512:(c + 1) * 512],
                                             start=False, stop=True)
                        last.then_inc(G["sum"], 1)
                        pe.wait_ge(G["osb"], t + 1)
                        for k in range(KT):
                            last = pe.transpose(ps_t[:, k * P:(k + 1) * P], osb[:, k * P:(k + 1) * P], ident[:])
                        last.then_inc(G["o_turned"], 1)

                    first_head()
                    turn_h(0)
                    queries()
                    with pe.Fori(0, NT - 1) as t:
                        score(t + 1)
                        retrieve(t)
                        pe.wait_ge(G["resid"], t + 1)
                        turn_h(t + 1)
                    retrieve(NT - 1)

                @block.scalar
                def _(act):
                    act.wait_ge(G["keys_turned"], 1)
                    act.activation(kT.rearrange("p i k -> p (i k)"), ps_t[:, 0:2 * P], ACT.Copy).then_inc(G["keys"], 1)

                    def stage_q(t):
                        act.activation(qs, qT[:, :, ds(t * P, P)], ACT.Copy).then_inc(G["q_staged"], 1)

                    def stage_h(t, more=True):
                        act.activation(hs, hT[:, :, ds(t * P, P)], ACT.Copy).then_inc(G["h_staged"], 1)
                        act.wait_ge(G["h_turned"], t + 1)
                        if more:
                            act.wait_ge(G["sum"], t)
                        act.activation(hrow, ps_t, ACT.Copy).then_inc(G["h_rows"], 1)

                    def exponent(t):
                        act.wait_ge(G["exp_in"], t + 1)
                        act.activation(gate, gate, ACT.Exp).then_inc(G["exp_out"], 1)

                    def tile(t, more):
                        act.wait_ge(G["hid"], t + 1)
                        act.activation(gel, hid, ACT.Gelu_apprx_tanh).then_inc(G["gelu"], 1)
                        if more:
                            stage_q(t + 1)
                        act.wait_ge(G["wgt"], t + 1)
                        for lo, hi in ((0, SHARED), (SHARED, BATCHES)):
                            with act.Fori(lo, hi) as m:
                                for hf in range(2):
                                    act.wait_ge(G["v_used"], t * 16 + m * 2 + hf + 1)
                                    for n in range(hf * HALF, (hf + 1) * HALF):
                                        if lo and n % 4 == 3:
                                            continue
                                        last = act.activation(diag[:, n, :], ident[:], ACT.Copy, scale=wgt[:, ds(m * RING + n, 1)])
                                        if n < (hf + 1) * HALF - (2 if lo else 1):
                                            last.then_inc(phase_sem("diag_part"), 1)
                                    last.then_inc(G["diag"], 1)
                        if more:
                            exponent(t + 1)
                        act.wait_ge(G["sum"], t + 1)
                        act.activation(osb, ps_out, ACT.Copy).then_inc(G["osb"], 1)
                        if more:
                            act.wait_ge(G["o_turned"], t + 1)
                            stage_h(t + 1)

                    def take_query(j, u):
                        act.wait_ge(G["projected"], 2 + 2 * j + u + 1)
                        act.activation(qT[:, ds(2 * j + u, 1), :], bank(2 * u, 2)[:, 0:TT].unsqueeze(1), ACT.Copy)\
                           .then_inc(G["q_taken"], 1)

                    for u in range(2):
                        act.wait_ge(phase_sem("first_query"), u + 1)
                        act.activation(qs[:, u, :], bank(4 + u)[:, KEYS:KEYS + P], ACT.Copy).then_inc(G["q_staged"], 1)
                    stage_h(0, False)
                    for u in range(2):
                        take_query(0, u)
                    with act.Fori(1, PH) as j:
                        for u in range(2):
                            take_query(j, u)
                            hold(act, G["q_taken"], 2 + 2 * j + u + 1)
                            act.activation(qs[:, u:u + 1, :], qT[:, ds(2 * j + u, 1), 0:P], ACT.Copy).then_inc(G["q_staged"], 1)
                    exponent(0)
                    with act.Fori(0, NT - 1) as t:
                        tile(t, True)
                    tile(NT - 1, False)

                @block.vector
                def _(dve):
                    def top16(st, src, work, vals, places, n):
                        for i in range(n):
                            st(dve.max(vals[:, i, 0:8], src[:, i, :]))
                        st.hold()
                        for i in range(n):
                            st(dve.max_index(places[:, i, 0:8], vals[:, i, 0:8], src[:, i, :]))
                            st(dve.match_replace(work[:, i, :], vals[:, i, 0:8], src[:, i, :], NEG))
                        st.hold()
                        for i in range(n):
                            st(dve.max(vals[:, i, 8:16], work[:, i, :]))
                        st.hold()
                        for i in range(n):
                            st(dve.max_index(places[:, i, 8:16], vals[:, i, 8:16], work[:, i, :]))
                        st.hold()

                    def choose(st, sc, cnd, nh, v, k, kf, sv, pl, e_out, signal):
                        shape = [P, nh, TOPK, TOPK]
                        picks = nh * TOPK
                        top16(st, sc, cut, v, k, 2 * nh)
                        st(dve.tensor_copy(kf, k))
                        v4 = v.rearrange("p (h s) k -> p h s k", s=2)
                        k4 = kf.rearrange("p (h s) k -> p h s k", s=2)
                        st(dve.tensor_tensor(cnd.rearrange("p h (a b) -> p h a b", a=TOPK),
                                             v4[:, :, 0, :].unsqueeze(3).to_broadcast(shape),
                                             v4[:, :, 1, :].unsqueeze(2).to_broadcast(shape), ALU.add))
                        st.hold()
                        top16(st, cnd, ccut, sv, pl, nh)
                        flat = pl.rearrange("p h k -> p (h k)")
                        pt, pf = parts[:, :, 0:picks], partf[:, :, 0:picks]
                        st(dve.tensor_scalar(pt[:, 0, :], flat, 4, None, ALU.logical_shift_right))
                        st(dve.tensor_scalar(pt[:, 1, :], flat, TOPK - 1, None, ALU.bitwise_and))
                        st.wait()
                        st(dve.tensor_copy(pf, pt))
                        st.wait()
                        eqs = (cnd, ccut[:, 0:nh, :])
                        for s in range(2):
                            st(dve.tensor_tensor(eqs[s].rearrange("p h (k a) -> p (h k) a", a=TOPK),
                                                 pf[:, s, :].unsqueeze(2).to_broadcast([P, picks, TOPK]),
                                                 iota16[:].unsqueeze(1).to_broadcast([P, picks, TOPK]), ALU.is_equal))
                        st.wait()
                        for s in range(2):
                            e4 = eqs[s].rearrange("p h (k a) -> p h k a", a=TOPK)
                            st(dve.tensor_tensor(e4, e4, k4[:, :, s, :].unsqueeze(2).to_broadcast(shape), ALU.mult))
                        st.wait()
                        for s in range(2):
                            st(dve.tensor_reduce(pf[:, s, :], eqs[s].rearrange("p h (k a) -> p (h k) a", a=TOPK),
                                                 op=ALU.add, axis=AX.X))
                        st.wait()
                        st(dve.scalar_tensor_tensor(pf[:, 0, :], pf[:, 0, :], float(KEYS), pf[:, 1, :], ALU.mult, ALU.add))
                        st.wait()
                        dve.tensor_scalar(e_out, pf[:, 0:1, :], row0, None, ALU.add).then_inc(signal, 1)

                    def gates(t, st):
                        dve.tensor_tensor(gate, sval, sval[:, :, 0:1].to_broadcast([P, PH, TOPK]), ALU.subtract)\
                           .then_inc(G["exp_in"], 1)
                        dve.wait_ge(G["exp_out"], t + 1)
                        st(dve.tensor_reduce(den, gate, op=ALU.add, axis=AX.X))
                        st.wait()
                        st(dve.reciprocal(den, den))
                        st.wait()
                        st(dve.tensor_tensor(gate, gate, b16(den, TOPK), ALU.mult))
                        st.wait()

                    def dot_ring(t, m):
                        for n in range(RING):
                            dve.wait_ge(gathered[n], l * (NT * 256) + t * 256 + m * 16 + 16)
                            ins = dve.scalar_tensor_tensor(out=ring[:, n, :], in0=ring[:, n, :], scalar=1.0, in1=hrow,
                                                           op0=ALU.mult, op1=ALU.mult,
                                                           accum_out=hid[:, ds(m * RING + n, 1)])
                            ins.then_inc(G["u_used"] if n % HALF == HALF - 1 else phase_sem("dot_part"), 1)

                    def tile(t, more, dotted=False):
                        base = FIRST + t * TILE
                        st = Steps(dve, "peer_step", base)
                        if not dotted:
                            hold(dve, G["h_rows"], t + 1)
                            with dve.Fori(0, BATCHES) as m:
                                dot_ring(t, m)
                        dve.wait_ge(G["u_used"], t * 16 + 16 + 2)
                        dve.sem_inc(G["hid"], 1)
                        dve.wait_ge(G["gelu"], t + 1)
                        dve.tensor_tensor(wgt, gel, gate.rearrange("p h k -> p (h k)"), ALU.mult).then_inc(G["wgt"], 1)
                        st(dve.memset(acc, 0.0))
                        dve.wait_ge(G["wgt"], t + 1)
                        if more:
                            hold(dve, G["scores"], PH + t + 1)
                            choose(st, ps_sc.rearrange("p (i k) -> p i k", k=KEYS), cand, PH, val, key, keyf, sval, place,
                                   eidx[:, ds(t + 1, 1), :], G["idx"])
                        st.hold()
                        with dve.Fori(SHARED, BATCHES) as m:
                            for i, n in enumerate(range(3, RING, 4)):
                                dve.wait_ge(gathered[n], l * (NT * 256) + t * 256 + 128 + m * 16 + 16)
                                if i:
                                    dve.wait_ge(phase_sem("share"), t * SHARE + (m - SHARED) * 4 + i)
                                else:
                                    dve.wait_ge(phase_sem("share"), t * SHARE + (m - SHARED) * 4)
                                dve.scalar_tensor_tensor(acc, ring[:, n, :], wgt[:, ds(m * RING + n, 1)], acc, ALU.mult, ALU.add)\
                                   .then_inc(phase_sem("share"), 1)
                                if i % 2:
                                    dve.wait_ge(phase_sem("share"), t * SHARE + (m - SHARED) * 4 + i + 1)
                                    dve.sem_inc(G["v_added"], 1)
                        dve.wait_ge(phase_sem("share"), t * SHARE + SHARE)
                        dve.sem_inc(G["acc"], 1)
                        if more:
                            gates(t + 1, st)
                        dve.wait_ge(G["o_turned"], t + 1)
                        tmp = arenaX[:, 0:D]
                        for k in range(KT):
                            blk = lambda v: v[:, k * P:(k + 1) * P].rearrange("p (b t) -> p b t", t=SLEN)
                            g = modE[:, 5 * KT + k:5 * KT + k + 1, ds(t * 8, 8)].rearrange("p o b -> p (o b)")
                            st(dve.tensor_tensor(blk(tmp), blk(ps_t), b16(g), ALU.mult))
                        if more:
                            assert st.n == TILE, st.n
                        st.wait()
                        x = xT[:, :, ds(t * P, P)]
                        dve.tensor_tensor(x, x, tmp.rearrange("p (k c) -> p k c", k=KT), ALU.add).then_inc(G["resid"], 1)
                        dve.wait_ge(G["resid"], t + 1)

                    TOP = 5
                    LOOKUP = 2 + 3 + 6 + 1
                    PICK = 3 * PH * TOP + LOOKUP + 3
                    HEAD = 3 * TOP + LOOKUP
                    FIRST = PH * HEAD + 3
                    TILE = 1 + PICK + KT
                    dve.tensor_copy(row0, layer_row[:, ds(l, 1)]).then_inc(G["row0"], 1)
                    dve.wait_ge(G["row0"], 1)
                    def head(j):
                        st = Steps(dve, "peer_step", j * HEAD)
                        hold(dve, G["scores"], j + 1)
                        choose(st, psum[:, 4:6, 0:KEYS], cand1, 1, val[:, 0:2, :], key[:, 0:2, :], keyf[:, 0:2, :], sv1,
                               pl1, eidx[:, 0:1, ds(j * TOPK, TOPK)], G["head_idx"])
                        dve.tensor_copy(sval[:, ds(j, 1), :], sv1).then_inc(phase_sem("sums_kept"), 1)
                        dve.wait_ge(phase_sem("sums_kept"), j + 1)
                        assert st.n == HEAD, st.n

                    head(0)
                    hold(dve, G["h_rows"], 1)
                    dot_ring(0, 0)
                    head(1)
                    with dve.Fori(2, PH) as j:
                        head(j)
                        dot_ring(0, j - 1)
                    dot_ring(0, PH - 1)
                    gates(0, Steps(dve, "peer_step", PH * HEAD))
                    tile(0, True, True)
                    with dve.Fori(1, NT - 1) as t:
                        tile(t, True)
                    tile(NT - 1, False)
            end_phase()

        norm_phase(hT[:], cols[:, FIN:FIN + KT], None)
        yout = view(arenaR, 0, NT, D)
        with nc.Block() as block:
            turned, y_ready = tiles_turned, tiles_copied

            @block.tensor
            def _(pe):
                for t in range(NT):
                    if t >= 4:
                        pe.wait_ge(y_ready, t - 3)
                    for k in range(KT):
                        last = pe.transpose(bank(2 * (t % 4), 2)[:, k * P:(k + 1) * P], hT[:, k, t * P:(t + 1) * P], ident[:])
                    last.then_inc(turned, 1)

            @block.scalar
            def _(act):
                for t in range(NT):
                    act.wait_ge(turned, t + 1)
                    act.activation(yout[:, t, :], bank(2 * (t % 4), 2), ACT.Copy).then_inc(y_ready, 1)

            @block.sync
            def _(sp):
                sp.wait_ge(y_ready, 4)
                sp.dma_start(a["y_prompt"].rearrange("o (t p) d -> p (o t) d", p=P), yout[:, 0:4, :]).then_inc(written, 16)
                sp.wait_ge(y_ready, 5)
                sp.dma_start(a["y_sample"].rearrange("b t d -> (b t) d"), yout[:, 4, :]).then_inc(written, 16)
                sp.wait_ge(written, DEPTH * W_LRU + 32)


_INS = ["x_prompt", "x_sample", "c_prompt", "c_sample", "state_ssd", "state_ssd_conv", "state_lru", "state_lru_conv",
        "ln1_w", "ln2_w", "w_mod", "b_mod", "w_in", "ssd_conv_w", "ssd_conv_b", "ssd_dt_bias", "ssd_a_log", "ssd_d",
        "ssd_norm_w", "lru_conv_w", "lru_conv_b", "lru_wa", "lru_ba", "lru_wx", "lru_bx", "lru_lambda", "w_br_ssd",
        "w_br_lru", "w_out", "peer_wq", "peer_k1", "peer_k2", "peer_u", "peer_v", "final_norm_w"]
_OUTS = [("y_prompt", (1, SEQ, D)), ("y_sample", (STREAMS, SLEN, D)),
         ("new_ssd_prompt", (DEPTH, 1, HEADS, HD, NS)), ("new_ssd_conv_prompt", (DEPTH, 1, HIST, CONVC)),
         ("new_lru_prompt", (DEPTH, 1, D)), ("new_lru_conv_prompt", (DEPTH, 1, HIST, D)),
         ("new_ssd_sample", (DEPTH, STREAMS, HEADS, HD, NS)), ("new_ssd_conv_sample", (DEPTH, STREAMS, HIST, CONVC)),
         ("new_lru_sample", (DEPTH, STREAMS, D)), ("new_lru_conv_sample", (DEPTH, STREAMS, HIST, D))]


def kernel(**inputs):
    import numpy as _np
    import concourse.bacc as _bacc
    from concourse.bass_utils import run_bass_kernel_spmd as _run

    nc = _bacc.Bacc("TRN2", target_bir_lowering=False, num_devices=1)
    arrays, args = {}, {}
    for name in _INS:
        x = _np.ascontiguousarray(inputs[name])
        arrays["in_" + name] = x
        args[name] = nc.dram_tensor("in_" + name, x.shape, F32, kind="ExternalInput").ap()
    for name, shape in _OUTS:
        args[name] = nc.dram_tensor("out_" + name, shape, F32, kind="ExternalOutput").ap()
    build(nc, args)
    r = _run(nc, [arrays], core_ids=[0])
    return tuple(r.results[0]["out_" + name] for name, _ in _OUTS)
```
